# Optimizing a Trainium2 kernel written in Bass

```python
import math
import jax, jax.numpy as jnp
from jax import lax
import numpy as np

'''
One inference step of a 4-layer interleaved hybrid decoder trunk serving two request groups with the same weights.
Layer i uses token mixer (i mod 3): 0 = chunked spatial-gating MLP (gMLP SGU, 128-position chunks),
1 = gated linear attention (GLA, chunked, per-token causal), 2 = MoBA block-sparse softmax attention with
T5 relative-position bias. Every layer: x += mixer(rmsnorm(x)); x += swiglu(rmsnorm(x)). Final rmsnorm.

Inputs:
  x_prompt   (BATCH, SEQ, D_MODEL)          new prompts, positions 0..SEQ-1
  x_sample   (DEC_BATCH, DEC_SEQ, D_MODEL)  new tokens at positions PAST_LEN..PAST_LEN+DEC_SEQ-1
  cache_k, cache_v (N_LAYERS_C, N_POOL, PAGE_SIZE, MOBA_HEADS, MOBA_DH)  paged K/V pool of MoBA layers,
             N_POOL = (DEC_BATCH * N_PAGES * 5) // 4, N_PAGES = PAST_LEN // PAGE_SIZE
  page_table (DEC_BATCH, N_PAGES) int32     logical page -> physical page
  state_gla  (N_LAYERS_B, DEC_BATCH, GLA_HEADS, GLA_DK, GLA_DV)  GLA recurrent states
  followed by the weights.
Returns the tuple:
  y_prompt          (BATCH, SEQ, D_MODEL)
  y_sample          (DEC_BATCH, DEC_SEQ, D_MODEL)
  k_new_prompt      (N_LAYERS_C, BATCH, SEQ, MOBA_HEADS, MOBA_DH)
  v_new_prompt      (N_LAYERS_C, BATCH, SEQ, MOBA_HEADS, MOBA_DH)
  k_new_sample      (N_LAYERS_C, DEC_BATCH, DEC_SEQ, MOBA_HEADS, MOBA_DH)
  v_new_sample      (N_LAYERS_C, DEC_BATCH, DEC_SEQ, MOBA_HEADS, MOBA_DH)
  gla_state_prompt  (N_LAYERS_B, BATCH, GLA_HEADS, GLA_DK, GLA_DV)
  gla_state_sample  (N_LAYERS_B, DEC_BATCH, GLA_HEADS, GLA_DK, GLA_DV)
  sgu_v_sample      (N_LAYERS_A, DEC_BATCH, DEC_SEQ, A_HALF)   normalised v rows of the newly opened chunk
'''

D_MODEL = 1024
BATCH = 1
SEQ = 256
DEPTH = 4
DEC_BATCH = 8
DEC_SEQ = 1
PAST_LEN = 256
PAGE_SIZE = 128

N_MIXERS = 3
N_LAYERS_A = (DEPTH + 2) // 3
N_LAYERS_B = (DEPTH + 1) // 3
N_LAYERS_C = DEPTH // 3
EPS = 1e-6

A_CHUNK = 128
A_HALF = 3 * D_MODEL
A_GROUPS = 8
A_GROUP_DIM = A_HALF // A_GROUPS

GLA_HEADS = 4
GLA_DK = D_MODEL // 2 // GLA_HEADS
GLA_DV = D_MODEL // GLA_HEADS
GLA_GATE_RANK = 16
GLA_GATE_NORM = 16.0
GLA_CHUNK = 64
GLA_PROJ = 2 * GLA_HEADS * GLA_DK + 2 * GLA_HEADS * GLA_DV + GLA_GATE_RANK

MOBA_HEADS = 16
MOBA_DH = D_MODEL // MOBA_HEADS
MOBA_BLOCK = 256
MOBA_TOPK = 3
MOBA_QBLK = 8
REL_BUCKETS = 32
REL_MAX_DIST = 128

D_FF = -(-8 * D_MODEL // (3 * 256)) * 256

kernel_name = "interleaved_sgu_gla_moba_decoder_step"

def rms_norm(x, g):
    x32 = x.astype(jnp.float32)
    y = x32 * lax.rsqrt(jnp.mean(x32 * x32, axis=-1, keepdims=True) + EPS)
    return (y * g.astype(jnp.float32)).astype(x.dtype)

def layer_norm(x, g, b):
    x32 = x.astype(jnp.float32)
    mu = jnp.mean(x32, axis=-1, keepdims=True)
    xc = x32 - mu
    y = xc * lax.rsqrt(jnp.mean(xc * xc, axis=-1, keepdims=True) + EPS)
    return (y * g.astype(jnp.float32) + b.astype(jnp.float32)).astype(x.dtype)

def swiglu(h, w_up, w_down):
    g, u = jnp.split(h @ w_up, 2, axis=-1)
    return (jax.nn.silu(g) * u) @ w_down

def chunk_spatial_mix(v, w_s, b_s):
    bsz, L, G, Dg = v.shape
    n = -(-L // A_CHUNK)
    vp = jnp.pad(v, ((0, 0), (0, n * A_CHUNK - L), (0, 0), (0, 0))).reshape(bsz, n, A_CHUNK, G, Dg)
    causal = jnp.tril(jnp.ones((A_CHUNK, A_CHUNK), dtype=bool))
    w = jnp.where(causal[None], w_s, 0.0).astype(v.dtype)
    s = jnp.einsum('gij,bnjgd->bnigd', w, vp) + b_s.T[None, None, :, :, None].astype(v.dtype)
    return s.reshape(bsz, n * A_CHUNK, G, Dg)[:, :L]

def sgu_mixer(h, w_in, ln_g, ln_b, w_s, b_s, w_out):
    bsz, L, _ = h.shape
    u, v = jnp.split(jax.nn.gelu(h @ w_in, approximate=False), 2, axis=-1)
    v = layer_norm(v, ln_g, ln_b)
    s = chunk_spatial_mix(v.reshape(bsz, L, A_GROUPS, A_GROUP_DIM), w_s, b_s).reshape(bsz, L, A_HALF)
    return (u * s) @ w_out, v

def gla_recurrence(q, k, v, log_a, s0):
    bsz, L, H, _ = q.shape
    c = min(GLA_CHUNK, L)
    n = -(-L // c)
    pad = n * c - L

    def to_chunks(t):
        t = jnp.pad(t.astype(jnp.float32), ((0, 0), (0, pad), (0, 0), (0, 0)))
        return t.reshape(bsz, n, c, H, t.shape[-1]).transpose(1, 0, 2, 3, 4)

    causal = jnp.tril(jnp.ones((c, c), dtype=bool))[None, :, :, None, None]

    def step(S, inp):
        qc, kc, vc, ac = inp
        cum = jnp.cumsum(ac, axis=1)
        o_inter = jnp.einsum('bthk,bhkv->bthv', qc * jnp.exp(cum), S)
        decay = jnp.exp(jnp.where(causal, cum[:, :, None] - cum[:, None, :], -jnp.inf))
        att = jnp.einsum('bthk,bshk,btshk->bhts', qc, kc, decay)
        o_intra = jnp.einsum('bhts,bshv->bthv', att, vc)
        last = cum[:, -1]
        k_dec = kc * jnp.exp(last[:, None] - cum)
        S_new = jnp.exp(last)[..., None] * S + jnp.einsum('bshk,bshv->bhkv', k_dec, vc)
        return S_new, o_inter + o_intra

    s_fin, o = lax.scan(step, s0.astype(jnp.float32),
                        (to_chunks(q), to_chunks(k), to_chunks(v), to_chunks(log_a)))
    o = o.transpose(1, 0, 2, 3, 4).reshape(bsz, n * c, H, v.shape[-1])[:, :L]
    return o, s_fin

def gla_mixer(h, s0, w_in, w_gate, b_gate, gn, w_out):
    bsz, L, _ = h.shape
    dq, dv = GLA_HEADS * GLA_DK, GLA_HEADS * GLA_DV
    q, k, v, g, gl = jnp.split(h @ w_in, [dq, 2 * dq, 2 * dq + dv, 2 * dq + 2 * dv], axis=-1)
    log_a = jax.nn.log_sigmoid((gl @ w_gate + b_gate).astype(jnp.float32)) / GLA_GATE_NORM
    q = q.reshape(bsz, L, GLA_HEADS, GLA_DK) * (GLA_DK ** -0.5)
    k = k.reshape(bsz, L, GLA_HEADS, GLA_DK)
    v = v.reshape(bsz, L, GLA_HEADS, GLA_DV)
    log_a = log_a.reshape(bsz, L, GLA_HEADS, GLA_DK)
    o, s_fin = gla_recurrence(q, k, v, log_a, s0)
    o = o * lax.rsqrt(jnp.mean(o * o, axis=-1, keepdims=True) + EPS) * gn.astype(jnp.float32)
    o = o.reshape(bsz, L, dv).astype(h.dtype) * jax.nn.silu(g)
    return o @ w_out, s_fin.astype(s0.dtype)

def t5_bucket(dist):
    max_exact = REL_BUCKETS // 2
    n = jnp.maximum(dist, 0)
    nf = jnp.maximum(n, max_exact).astype(jnp.float32)
    large = max_exact + (jnp.log(nf / max_exact) / math.log(REL_MAX_DIST / max_exact)
                         * (REL_BUCKETS - max_exact)).astype(jnp.int32)
    return jnp.where(n < max_exact, n, jnp.minimum(large, REL_BUCKETS - 1))

def moba_qkv(h, w_in):
    bsz, L, _ = h.shape
    q, k, v = jnp.split(h @ w_in, 3, axis=-1)
    return (q.reshape(bsz, L, MOBA_HEADS, MOBA_DH), k.reshape(bsz, L, MOBA_HEADS, MOBA_DH),
            v.reshape(bsz, L, MOBA_HEADS, MOBA_DH))

def moba_attention(q, k, v, q_pos, rel_bias):
    bsz, Lq, H, Dh = q.shape
    T = k.shape[1]
    nb = -(-T // MOBA_BLOCK)
    padt = nb * MOBA_BLOCK - T
    if padt:
        k = jnp.pad(k, ((0, 0), (0, padt), (0, 0), (0, 0)))
        v = jnp.pad(v, ((0, 0), (0, padt), (0, 0), (0, 0)))
    kb = k.reshape(bsz, nb, MOBA_BLOCK, H, Dh)
    vb = v.reshape(bsz, nb, MOBA_BLOCK, H, Dh)
    k_mean = jnp.mean(kb, axis=2, dtype=jnp.float32)
    kk = min(MOBA_TOPK, nb)
    qb = min(MOBA_QBLK, Lq)
    nq = -(-Lq // qb)
    padq = nq * qb - Lq
    qs = jnp.pad(q, ((0, 0), (0, padq), (0, 0), (0, 0))).reshape(bsz, nq, qb, H, Dh).transpose(1, 0, 2, 3, 4)
    ps = jnp.pad(q_pos, (0, padq), mode='edge').reshape(nq, qb)
    b_ix = jnp.arange(bsz)[:, None, None, None]
    h_ix = jnp.arange(H)[None, :, None, None]
    offs = jnp.arange(MOBA_BLOCK, dtype=jnp.int32)
    bias_tab = rel_bias.astype(jnp.float32)
    scale = Dh ** -0.5

    def step(inp):
        qc, pc = inp
        own = pc // MOBA_BLOCK
        gate = jnp.einsum('bqhd,bnhd->bhqn', qc, k_mean, preferred_element_type=jnp.float32)
        past = jnp.arange(nb)[None, :] < own[:, None]
        gate = jnp.where(past[None, None], gate, -jnp.inf)
        _, top = lax.top_k(gate, kk)
        idx = jnp.concatenate([top.astype(jnp.int32),
                               jnp.broadcast_to(own[None, None, :, None], (bsz, H, qb, 1)).astype(jnp.int32)], axis=-1)
        slot_ok = jnp.concatenate([jnp.arange(kk)[None, :] < own[:, None],
                                   jnp.ones((qb, 1), dtype=bool)], axis=-1)
        ksel = kb[b_ix, idx, :, h_ix]
        vsel = vb[b_ix, idx, :, h_ix]
        dist = pc[None, None, :, None, None] - (idx[..., None] * MOBA_BLOCK + offs)
        bias = bias_tab[t5_bucket(dist), h_ix[..., None]]
        logits = jnp.einsum('bqhd,bhqtsd->bhqts', qc, ksel, preferred_element_type=jnp.float32) * scale + bias
        mask = slot_ok[None, None, :, :, None] & (dist >= 0)
        logits = jnp.where(mask, logits, -jnp.inf)
        p = jax.nn.softmax(logits.reshape(bsz, H, qb, -1), axis=-1).reshape(logits.shape)
        return jnp.einsum('bhqts,bhqtsd->bqhd', p.astype(vsel.dtype), vsel)

    o = lax.map(step, (qs, ps))
    return o.transpose(1, 0, 2, 3, 4).reshape(bsz, nq * qb, H, Dh)[:, :Lq]

def gather_paged(cache_layer, page_table, new, pad):
    n_dec = page_table.shape[0]
    past = cache_layer[page_table].reshape(n_dec, -1, MOBA_HEADS, MOBA_DH).astype(new.dtype)
    zeros = jnp.zeros((n_dec, pad, MOBA_HEADS, MOBA_DH), new.dtype)
    return jnp.concatenate([past, new, zeros], axis=1)

def setup_inputs(seed: int = 0) -> dict:
    key = jax.random.key(seed)
    ks = jax.random.split(key, 32)
    f32 = jnp.float32

    def nrm(k, shape, scale):
        return jax.random.normal(k, shape, f32) * scale

    n_pages = PAST_LEN // PAGE_SIZE
    n_pool = (DEC_BATCH * n_pages * 5) // 4
    page_table = jax.random.permutation(ks[4], n_pool)[:DEC_BATCH * n_pages].reshape(DEC_BATCH, n_pages).astype(jnp.int32)
    return {
        'x_prompt': nrm(ks[0], (BATCH, SEQ, D_MODEL), 1.0),
        'x_sample': nrm(ks[1], (DEC_BATCH, DEC_SEQ, D_MODEL), 1.0),
        'cache_k': nrm(ks[2], (N_LAYERS_C, n_pool, PAGE_SIZE, MOBA_HEADS, MOBA_DH), 1.0),
        'cache_v': nrm(ks[3], (N_LAYERS_C, n_pool, PAGE_SIZE, MOBA_HEADS, MOBA_DH), 1.0),
        'page_table': page_table,
        'state_gla': nrm(ks[5], (N_LAYERS_B, DEC_BATCH, GLA_HEADS, GLA_DK, GLA_DV), 0.5),
        'norm_mix': 1.0 + nrm(ks[6], (DEPTH, D_MODEL), 0.02),
        'norm_ffn': 1.0 + nrm(ks[7], (DEPTH, D_MODEL), 0.02),
        'norm_final': 1.0 + nrm(ks[8], (D_MODEL,), 0.02),
        'w_in_a': nrm(ks[9], (N_LAYERS_A, D_MODEL, 2 * A_HALF), D_MODEL ** -0.5),
        'ln_a_g': 1.0 + nrm(ks[10], (N_LAYERS_A, A_HALF), 0.02),
        'ln_a_b': nrm(ks[11], (N_LAYERS_A, A_HALF), 0.02),
        'w_s_a': nrm(ks[12], (N_LAYERS_A, A_GROUPS, A_CHUNK, A_CHUNK), A_CHUNK ** -0.5),
        'b_s_a': 1.0 + nrm(ks[13], (N_LAYERS_A, A_GROUPS, A_CHUNK), 0.1),
        'w_out_a': nrm(ks[14], (N_LAYERS_A, A_HALF, D_MODEL), A_HALF ** -0.5),
        'w_in_b': nrm(ks[15], (N_LAYERS_B, D_MODEL, GLA_PROJ), D_MODEL ** -0.5),
        'w_gate_b': nrm(ks[16], (N_LAYERS_B, GLA_GATE_RANK, GLA_HEADS * GLA_DK), GLA_GATE_RANK ** -0.5),
        'b_gate_b': nrm(ks[17], (N_LAYERS_B, GLA_HEADS * GLA_DK), 0.1),
        'gn_b': 1.0 + nrm(ks[18], (N_LAYERS_B, GLA_DV), 0.02),
        'w_out_b': nrm(ks[19], (N_LAYERS_B, GLA_HEADS * GLA_DV, D_MODEL), (GLA_HEADS * GLA_DV) ** -0.5),
        'w_in_c': nrm(ks[20], (N_LAYERS_C, D_MODEL, 3 * MOBA_HEADS * MOBA_DH), D_MODEL ** -0.5),
        'w_out_c': nrm(ks[21], (N_LAYERS_C, MOBA_HEADS * MOBA_DH, D_MODEL), (MOBA_HEADS * MOBA_DH) ** -0.5),
        'rel_bias': nrm(ks[22], (REL_BUCKETS, MOBA_HEADS), 0.5),
        'w_up': nrm(ks[23], (DEPTH, D_MODEL, 2 * D_FF), D_MODEL ** -0.5),
        'w_down': nrm(ks[24], (DEPTH, D_FF, D_MODEL), D_FF ** -0.5),
    }

def reference(x_prompt, x_sample, cache_k, cache_v, page_table, state_gla,
              norm_mix, norm_ffn, norm_final,
              w_in_a, ln_a_g, ln_a_b, w_s_a, b_s_a, w_out_a,
              w_in_b, w_gate_b, b_gate_b, gn_b, w_out_b,
              w_in_c, w_out_c, rel_bias,
              w_up, w_down):
    past_len = page_table.shape[1] * PAGE_SIZE
    n_pr, l_pr = x_prompt.shape[0], x_prompt.shape[1]
    n_dec, l_dec = x_sample.shape[0], x_sample.shape[1]
    pos_p = jnp.arange(l_pr, dtype=jnp.int32)
    pos_s = past_len + jnp.arange(l_dec, dtype=jnp.int32)
    xp, xs = x_prompt, x_sample
    k_p, v_p, k_s, v_s, gla_p, gla_s, sgu_s = [], [], [], [], [], [], []
    for i in range(DEPTH):
        kind, j = i % N_MIXERS, i // N_MIXERS
        hp = rms_norm(xp, norm_mix[i])
        hs = rms_norm(xs, norm_mix[i])
        if kind == 0:
            mp, _ = sgu_mixer(hp, w_in_a[j], ln_a_g[j], ln_a_b[j], w_s_a[j], b_s_a[j], w_out_a[j])
            ms, v_rows = sgu_mixer(hs, w_in_a[j], ln_a_g[j], ln_a_b[j], w_s_a[j], b_s_a[j], w_out_a[j])
            sgu_s.append(v_rows)
        elif kind == 1:
            s_zero = jnp.zeros((n_pr, GLA_HEADS, GLA_DK, GLA_DV), xp.dtype)
            mp, sp = gla_mixer(hp, s_zero, w_in_b[j], w_gate_b[j], b_gate_b[j], gn_b[j], w_out_b[j])
            ms, ss = gla_mixer(hs, state_gla[j], w_in_b[j], w_gate_b[j], b_gate_b[j], gn_b[j], w_out_b[j])
            gla_p.append(sp)
            gla_s.append(ss)
        else:
            qp, kp, vp = moba_qkv(hp, w_in_c[j])
            op = moba_attention(qp, kp, vp, pos_p, rel_bias)
            qs, kn, vn = moba_qkv(hs, w_in_c[j])
            pad = (-(past_len + l_dec)) % MOBA_BLOCK
            os_ = moba_attention(qs, gather_paged(cache_k[j], page_table, kn, pad),
                                 gather_paged(cache_v[j], page_table, vn, pad), pos_s, rel_bias)
            mp = op.reshape(n_pr, l_pr, -1) @ w_out_c[j]
            ms = os_.reshape(n_dec, l_dec, -1) @ w_out_c[j]
            k_p.append(kp)
            v_p.append(vp)
            k_s.append(kn)
            v_s.append(vn)
        xp = xp + mp
        xs = xs + ms
        xp = xp + swiglu(rms_norm(xp, norm_ffn[i]), w_up[i], w_down[i])
        xs = xs + swiglu(rms_norm(xs, norm_ffn[i]), w_up[i], w_down[i])
    y_prompt = rms_norm(xp, norm_final)
    y_sample = rms_norm(xs, norm_final)
    return (y_prompt, y_sample, jnp.stack(k_p), jnp.stack(v_p), jnp.stack(k_s), jnp.stack(v_s),
            jnp.stack(gla_p), jnp.stack(gla_s), jnp.stack(sgu_s))


_drawn_inputs = setup_inputs


def setup_inputs(seed=0):
    import zlib

    import numpy as np

    out = dict(_drawn_inputs(seed))
    spreads = {}
    factors = {'norm_final': 2.989, 'ln_a_g': 2.833, 'ln_a_b': 2.838, 'gn_b': 5.917}
    for name, (base, spread) in spreads.items():
        noise = np.random.default_rng([zlib.crc32(name.encode()), seed]).standard_normal(out[name].shape)
        drawn = base * np.exp(spread * noise) if base else spread * noise
        out[name] = __import__('jax').numpy.asarray(drawn.astype(out[name].dtype))
    for name, factor in factors.items():
        out[name] = (out[name] * factor).astype(out[name].dtype)
    return out
```

```python
from contextlib import ExitStack

import concourse.bass as bass
from concourse import mybir
import numpy as np

F32 = mybir.dt.float32
F32R = mybir.dt.float32r
I32 = mybir.dt.int32
ALU = mybir.AluOpType
ACT = mybir.ActivationFunctionType
AX = mybir.AxisListType

P = 128
D = 1024
DC = D // P
SEQ = 256
NSAMP = 8
TOK = SEQ + NSAMP
NBLK = SEQ // P
DEPTH = 4
EPS = 1e-6

HALF = 3 * D
HC = HALF // P
GROUPS = 8
GC = HC // GROUPS

GH, DK, DV = 4, 128, 256
RANK = 16
GLA_PROJ = 2 * GH * DK + 2 * GH * DV + RANK
GATE_NORM = 16.0
LEVELS = [128, 64, 32, 16, 8, 4, 2, 1]

MH, DH = 16, 64
NPAGES = 2
NPOOL = NSAMP * NPAGES * 5 // 4
BUCKETS = 32
MAXDIST = 128
STRIP = 3 * P - 1
NEG = -1e30

DFF = 2816
FC = DFF // P

KC = 8
PW = 256
SLOTS = 2
BANKS = 4
PAGE_SLOTS = 4
SQ_STEPS = 2 * DC + 1


def need(eng, sem, value):
    if not isinstance(value, int) or value > 0:
        eng.wait_ge(sem, value)


def run_loop(eng, start, end, body, peel=False):
    if peel:
        body(start, True)
        start += 1
    if end - start == 1:
        body(start, False)
    elif start < end:
        with eng.Fori(start, end) as i:
            body(i, False)


def cut(i, size):
    return slice(i * size, (i + 1) * size) if isinstance(i, int) else bass.ds(i * size, size)


def one(i):
    return slice(i, i + 1) if isinstance(i, int) else bass.ds(i, 1)


def chunk(tensor, m):
    return tensor[:, one(m), :].rearrange("p a t -> p (a t)")


class Steps:

    def __init__(self, sem, names):
        self.sem, self.names, self.at = sem, names, 0
        self.number = {n: k + 1 for k, n in enumerate(names)}
        assert len(self.number) == len(names)

    def did(self, instruction, name):
        assert self.names[self.at] == name, (self.names[self.at], name)
        self.at += 1
        instruction.then_inc(self.sem, 1)

    def wait(self, eng, name):
        eng.wait_ge(self.sem, self.number[name])


def make_plan():
    now = dict(piece=0, tile=0, norm=0, func=0, turn=0, act=0)
    phases = {}

    def add(name, **count):
        phases[name] = dict(now)
        for k, v in count.items():
            now[k] += v

    add("load", tile=DC, norm=1)
    for layer in range(DEPTH):
        if layer % 3 == 0:
            add(("in", layer), piece=2 * HC // 2, tile=2 * HC, func=2 * HC, turn=HC)
            add(("mix", layer), tile=HC, act=HC)
            add(("out", layer), piece=4 * HC // KC, tile=DC, norm=1)
        else:
            turns = 2 * DC // 2 if layer % 3 == 1 else 3 * DC
            add(("in", layer), piece=3 * DC // 2, tile=3 * DC, func=turns, turn=turns)
            add(("mix", layer), act=DC)
            add(("out", layer), piece=DC // 2, tile=DC, norm=1)
        add(("up", layer), piece=FC, tile=2 * FC, func=FC, act=FC)
        add(("down", layer), piece=12, tile=DC, norm=int(layer < DEPTH - 1))
    add("final", tile=DC)
    return phases


def build(nc, A):
    ph = make_plan()
    with ExitStack() as ctx:
        def sem(name):
            return ctx.enter_context(nc.semaphore(name))

        ps = [ctx.enter_context(nc.psum_tensor(f"bank{b}", [P, 512], F32)) for b in range(8)]
        SS = ps[4]
        TURN = [ps[5], ps[6]]

        start_of, top = {}, [16640]

        def sb(name, shape, dt=F32):
            size = int(np.prod(shape[1:])) * 4
            start_of[name] = top[0]
            top[0] += -(-size // 32) * 32
            return nc.alloc_sbuf_tensor_at(name, shape, dt, offset=start_of[name])

        def over(name, host, offset, shape, dt=F32):
            start_of[name] = start_of[host] + offset
            return nc.alloc_sbuf_tensor_at(name, shape, dt, offset=start_of[host] + offset)

        raw = sb("raw", [P, SLOTS, KC, PW])
        whi = sb("whi", [P, SLOTS, KC, PW], F32R)
        wlo = sb("wlo", [P, SLOTS, KC, PW], F32R)
        x = sb("x", [P, DC, TOK])
        xh = sb("xh", [P, DC, TOK], F32R)
        xl = sb("xl", [P, DC, TOK], F32R)
        xg = sb("xg", [P, 2, TOK])
        tbuf = sb("tbuf", [P, BANKS, TOK])
        gbuf = sb("gbuf", [P, BANKS, TOK])
        gs = sb("gs", [P, 2, TOK])
        abuf = sb("abuf", [P, 2, TOK])
        rms = sb("rms", [P, TOK])
        rinv = sb("rinv", [P, TOK])
        sqsum = sb("sqsum", [P, TOK])
        sq = sb("sq", [P, TOK])
        ones = sb("ones", [P, SEQ])
        ident = sb("ident", [P, P])
        halves = sb("halves", [P, 2])
        own = sb("own", [P, NSAMP])
        cols = sb("cols", [P, 70])
        w_rank = sb("w_rank", [P, DC, RANK])
        w_gate = sb("w_gate", [RANK, GH * DK])
        table = sb("table", [1, NSAMP * NPAGES], I32)
        w00 = sb("w00", [NSAMP, GROUPS])
        ws_diag = sb("ws_diag", [NSAMP, GROUPS, NSAMP])
        stats = sb("stats", [P, NBLK + 1, 6, 6])
        moments = sb("moments", [P, NBLK + 1, 2])
        lnstd = sb("lnstd", [P, NBLK + 1])
        lninv = sb("lninv", [P, NBLK + 1])
        small = sb("small", [P, 16])
        eps = sb("eps", [P, 1])
        softs = sb("softs", [P, 2, 8])
        acth = sb("acth", [P, HC, TOK], F32R)
        actl = sb("actl", [P, HC, TOK], F32R)
        feat = sb("feat", [P, HC, TOK])
        vt = sb("vt", [P, NBLK, HALF])
        vts = sb("vts", [NSAMP, HALF])
        assert top[0] <= 229344, top[0]

        TAIL = DC * TOK * 4
        xin = over("xin", "vt", 0, [P, NBLK + 1, D])
        col_rows = over("col_rows", "vt", 4 * 3 * D, [70, P])
        ytok = over("ytok", "vt", 0, [P, NBLK + 1, D])
        yout = over("yout", "acth", 0, [P, NBLK + 1, D])
        gain_fin = over("gain_fin", "feat", 0, [P, D])
        ln_gain = over("ln_gain", "acth", 0, [P, HALF])
        ln_bias = over("ln_bias", "acth", 4 * HALF, [P, HALF])
        ws_nat = over("ws_nat", "acth", 8 * HALF, [P, GROUPS, P])
        ws_t = over("ws_t", "xh", 0, [P, GROUPS, P])
        ws_bias = over("ws_bias", "xl", 0, [1, GROUPS, TOK])
        v_tok = over("v_tok", "vt", 0, [P, NBLK, GH * DV])
        vs_tok = over("vs_tok", "vt", 8192, [NSAMP, GH * DV])
        kd_tok = over("kd_tok", "vt", 12288, [P, NBLK, GH * DK])
        att = over("att", "vt", 16384, [P, GH, NBLK, P])
        att01 = over("att01", "vt", 20480, [P, GH, P])
        cum = over("cum", "vt", 22528, [P, GH, SEQ])
        qf = over("qf", "vt", 26624, [P, GH, SEQ])
        kf = over("kf", "vt", 30720, [P, GH, SEQ])
        loga = over("loga", "acth", TAIL, [P, GH, TOK])
        zt = over("zt", "acth", TAIL + 4224, [P, GH, TOK])
        decay = [over("decay0", "acth", TAIL + 4224, [P, GH, SEQ]),
                 over("decay1", "acth", TAIL + 8448, [P, GH, SEQ])]
        level_mask = over("level_mask", "gs", 0, [P, len(LEVELS), P], I32)
        gl = over("gl", "acth", TAIL + 13568, [RANK, TOK])
        ea = over("ea", "acth", TAIL + 14624, [P, GH, NSAMP])
        states = over("states", "actl", TAIL, [P, NSAMP // 2, GH, DV])
        onehot = over("onehot", "xh", 0, [NSAMP, NSAMP, P])
        kc = over("kc", "xh", 4096, [P, GH, SEQ])
        kd = over("kd", "xl", 0, [P, GH, SEQ])
        qc = over("qc", "xl", 4096, [P, GH, SEQ])
        o_sq = over("o_sq", "xl", 0, [P, DC, TOK])
        head_std = over("head_std", "acth", TAIL, [P, GH, TOK])
        s_fin = over("s_fin", "acth", TAIL + 4224, [P, GH, DV])
        strip = over("strip", "acth", TAIL, [P, MH, 2 * P])
        pages = over("pages", "actl", TAIL, [P, PAGE_SLOTS, D])
        prod = [over("prod0", "tbuf", 0, [P, D]), over("prod1", "gs", 0, [P, D])]
        q_row = over("q_row", "gbuf", 0, [P, D])
        logit = over("logit", "tbuf", 0, [P, 2, 3 * P])
        prob_t = over("prob_t", "gbuf", 0, [P, 2, 3 * P])
        sc = over("sc", "xh", 4096, [P, NPAGES, P])
        sp_tok = over("sp_tok", "xh", 5120, [P, NPAGES, P])
        o_samp = over("o_samp", "xh", 6144, [P, DC, NSAMP])
        new_qk = over("new_qk", "xh", 6400, [P, DC, NSAMP])
        new_z = over("new_z", "xh", 6656, [P, NSAMP, DC, 2])
        new_own = over("new_own", "xh", 7168, [P, NSAMP])
        new_p = over("new_p", "xh", 7232, [NSAMP, P])
        relb = over("relb", "xl", 0, [BUCKETS, NSAMP, MH])
        of_strip = over("of_strip", "xl", 512, [BUCKETS, STRIP + 1])
        of_past = over("of_past", "xl", 2048, [BUCKETS, SEQ + 1])
        rows = over("rows", "xl", 3104, [MH, STRIP + 1])
        slog = over("slog", "xl", 4640, [P, SEQ + 1])
        sbias = over("sbias", "xl", 5696, [P, SEQ + 1])
        scratch = nc.dram_tensor("bias_by_distance", [MH, STRIP + 1], F32)

        raw_landed = [sem(f"raw_landed{s}") for s in range(SLOTS)]
        w_hi = sem("w_hi")
        w_lo = sem("w_lo")
        mm_done = sem("mm_done")
        tile_made = sem("tile_made")
        bank_read = sem("bank_read")
        gained = sem("gained")
        xh_done = sem("xh_done")
        xl_done = sem("xl_done")
        sq_done = sem("sq_done")
        ss_done = sem("ss_done")
        rms_done = sem("rms_done")
        rinv_done = sem("rinv_done")
        func_done = sem("func_done")
        turned = sem("turned")
        unturned = sem("unturned")
        gs_done = sem("gs_done")
        a_done = sem("a_done")
        ah_done = sem("ah_done")
        al_done = sem("al_done")
        in_landed = sem("in_landed")
        cols_landed = sem("cols_landed")
        const_landed = sem("const_landed")
        gate_landed = sem("gate_landed")
        table_landed = sem("table_landed")
        ones_done = sem("ones_done")
        cols_turned = sem("cols_turned")
        cols_done = sem("cols_done")
        ln_landed = sem("ln_landed")
        ws_landed = sem("ws_landed")
        w00_landed = sem("w00_landed")
        ws_masked = sem("ws_masked")
        ws_turned = sem("ws_turned")
        ws_ready = sem("ws_ready")
        ws_bias_landed = sem("ws_bias_landed")
        ws_bias_done = sem("ws_bias_done")
        diag_done = sem("diag_done")
        stats_done = sem("stats_done")
        moments_done = sem("moments_done")
        lnstd_done = sem("lnstd_done")
        lninv_done = sem("lninv_done")
        lnormed = sem("lnormed")
        stored = sem("stored")
        state_landed = sem("state_landed")
        state_stored = sem("state_stored")
        mask_landed = sem("mask_landed")
        page_landed = [sem(f"page_landed{s}") for s in range(PAGE_SLOTS)]
        bias_landed = sem("bias_landed")
        scratch_landed = sem("scratch_landed")
        strip_landed = sem("strip_landed")
        fsq_done = sem("fsq_done")
        fstd_done = sem("fstd_done")
        finv_done = sem("finv_done")
        y_done = sem("y_done")
        fin_landed = sem("fin_landed")

        STORES = []

        def store(eng, out, src):
            eng.dma_start(out, src).then_inc(stored, 16)
            STORES.append(1)

        def pieces_of(name):
            kind, layer = name
            j = layer // 3

            def by_chunk(w):
                return w.rearrange("(c p) n -> p c n", p=P)

            if kind == "up":
                w = by_chunk(A["w_up"][layer])
                return [(w, 0, KC, t * DFF) for t in range(2)], PW, FC // 2
            if kind == "in":
                w = by_chunk(A[("w_in_a", "w_in_b", "w_in_c")[layer % 3]][j])
                return [(w, 0, KC, t * PW) for t in range(2)], 2 * PW, 12 if layer % 3 == 0 else 6
            if kind == "out" and layer % 3:
                w = by_chunk(A[("", "w_out_b", "w_out_c")[layer % 3]][j])
                return [(w, 0, KC, t * PW) for t in range(2)], 2 * PW, 2
            w = by_chunk(A["w_out_a"][j] if kind == "out" else A["w_down"][layer])
            depth = HC if kind == "out" else FC
            return [(w, c, min(KC, depth - c), t * PW) for t in range(2)
                    for c in range(0, depth, KC)], 2 * PW, 2

        def stream(sp, name):
            pieces, step, n = pieces_of(name)
            base, per = ph[name]["piece"], len(pieces)

            def body(i, shift):
                for t, (w, c, k, col) in enumerate(pieces):
                    need(sp, w_lo, base + per * i + t - SLOTS + 1)
                    at = i * step + (col + shift)
                    columns = slice(at, at + PW) if isinstance(at, int) else bass.ds(at, PW)
                    sp.dma_start(raw[:, t % SLOTS, 0:k, :], w[:, c:c + k, columns])\
                        .then_inc(raw_landed[t % SLOTS], 16)

            if name == ("out", 2):
                body(0, 0)
                sp_pages(sp)
                body(1, 0)
            elif name[0] == "in" and name[1] % 3 == 0:
                run_loop(sp, 0, n // 2, lambda i, f: body(i, HALF), peel=base == 0)
                run_loop(sp, n // 2, n, lambda i, f: body(i, -HALF))
            else:
                run_loop(sp, 0, n, lambda i, f: body(i, 0))

        def chunks_after(name, t):
            k = [k for _, _, k, _ in pieces_of(name)[0]]
            return k[t + 1] if t + 1 < len(k) else KC

        def split_hi(act, number, landed, slot, k):
            act.wait_ge(raw_landed[slot], landed)
            need(act, mm_done, 2 * (number - SLOTS + 1))
            act.activation(whi[:, slot, 0:k, :], raw[:, slot, 0:k, :], ACT.Copy).then_inc(w_hi, 1)

        def split_lo(dve, number, slot, k):
            dve.wait_ge(w_hi, number + 1)
            need(dve, mm_done, 2 * (number - SLOTS + 1))
            dve.tensor_tensor(wlo[:, slot, 0:k, :], raw[:, slot, 0:k, :],
                              whi[:, slot, 0:k, :].bitcast(F32), ALU.subtract).then_inc(w_lo, 1)

        def next_piece(eng, name, i, t, last=False):
            if last:
                return
            base, per = ph[name]["piece"], len(pieces_of(name)[0])
            number, slot, k = base + per * i + t + 1, (t + 1) % SLOTS, chunks_after(name, t)
            if eng is nc.vector:
                split_lo(eng, number, slot, k)
            else:
                nth = (base + t + 1) // SLOTS + 1
                split_hi(eng, number, i * (16 * per // SLOTS) + 16 * nth, slot, k)

        def tile_mms(pe, bank, slot, half, chunks, rh, rl, c0, depth):
            side = slice(half * P, half * P + P)
            for c in chunks:
                pe.matmul(bank[:, 0:TOK], whi[:, slot, c, side], rh[:, c0 + c, :],
                          start=(c0 + c == 0), stop=False)
                pe.matmul(bank[:, 0:TOK], whi[:, slot, c, side], rl[:, c0 + c, :],
                          start=False, stop=False)
                mm = pe.matmul(bank[:, 0:TOK], wlo[:, slot, c, side], rh[:, c0 + c, :],
                               start=False, stop=(c0 + c == depth - 1))
            return mm

        def sum_squares(pe, norm):
            pe.wait_ge(sq_done, SQ_STEPS * (norm + 1))
            need(pe, rms_done, norm)
            pe.matmul(SS[:, 0:TOK], ones[:, 0:P], sqsum[:, :], start=True, stop=True)\
                .then_inc(ss_done, 1)

        def turn_tile(pe, turn, func, j):
            pe.wait_ge(func_done, func + 1)
            need(pe, unturned, 2 * (turn - 1))
            out = TURN[j % 2]
            for b in range(NBLK):
                pe.transpose(out[:, b * P:(b + 1) * P], gbuf[:, j, b * P:(b + 1) * P], ident[:, :])
            pe.transpose(out[0:NSAMP, SEQ:SEQ + P], gbuf[:, j, SEQ:TOK], ident[:, :])\
                .then_inc(turned, 1)

        def pe_project(pe, name, start, end, turns_from=None, new_norm=None):
            at = ph[name]
            p0, t0 = at["piece"], at["tile"]

            def turn(i, j):
                step = i - start if isinstance(i, int) else i + (-start)
                q = 4 * step + (at["turn"] + j)
                f = 4 * i + (at["func"] + j) if name[1] % 3 != 1 else 4 * step + (at["func"] + j)
                turn_tile(pe, q, f, j % BANKS)

            def body(i, first):
                for t in range(2):
                    pe.wait_ge(w_lo, p0 + 2 * i + t + 1)
                    for half in range(2):
                        j = 2 * t + half
                        need(pe, bank_read, t0 + 4 * i + j - BANKS + 1)
                        if first and new_norm is not None and j == 0:
                            for c in range(DC):
                                pe.wait_ge(xl_done, DC * new_norm + c + 1)
                                mm = tile_mms(pe, ps[j], t, half, [c], xh, xl, 0, DC)
                        else:
                            mm = tile_mms(pe, ps[j], t, half, range(KC), xh, xl, 0, DC)
                        mm.then_inc(mm_done, 1)
                        if first and new_norm is not None and j == 0:
                            sum_squares(pe, new_norm)
                        if turns_from is not None and not (first and j == 0):
                            turn(i, j - 1)

            run_loop(pe, start, end, body, peel=turns_from is not None or new_norm is not None)
            if turns_from is not None:
                turn(end - 1, BANKS - 1)

        def pe_out(pe, name):
            at = ph[name]
            pieces, _, steps = pieces_of(name)
            per = len(pieces)
            depth = sum(k for _, _, k, _ in pieces) // 2
            acts = ph[("mix", name[1])] if name[0] == "out" else ph[("up", name[1])]

            def body(i, first):
                for t, (_, c0, k, _) in enumerate(pieces):
                    panel = t // (per // 2)
                    pe.wait_ge(w_lo, at["piece"] + per * i + t + 1)
                    for half in range(2):
                        j = 2 * panel + half
                        if c0 == 0:
                            need(pe, bank_read, at["tile"] + 4 * i + j - BANKS + 1)
                        if first and panel == 0 and half == 0:
                            for c in range(k):
                                pe.wait_ge(al_done, acts["act"] + c0 + c + 1)
                                mm = tile_mms(pe, ps[j], t % SLOTS, half, [c], acth, actl, c0, depth)
                        else:
                            mm = tile_mms(pe, ps[j], t % SLOTS, half, range(k), acth, actl, c0, depth)
                        mm.then_inc(mm_done, 1)

            run_loop(pe, 0, steps, body, peel=True)

        def mm_value(name, i, j):
            pieces = pieces_of(name)[0]
            per, p0 = len(pieces), ph[name]["piece"]
            each = per // 2
            return 2 * per * i + (2 * p0 + 2 * each * (j // 2) + 2 * (each - 1) + j % 2 + 1)

        def new_chunk_vector(dve, norm, gain, m, j, tile, tile_wait, add):
            dve.wait_ge(*tile_wait)
            if add:
                dve.tensor_tensor(chunk(x, m), chunk(x, m), ps[j % BANKS][:, 0:TOK],
                                  ALU.add).then_inc(bank_read, 1)
            else:
                dve.tensor_copy(chunk(x, m), ps[j % BANKS][:, 0:TOK]).then_inc(bank_read, 1)
            if norm is None:
                return
            need(dve, xl_done, DC * norm + m - 1)
            dve.wait_ge(bank_read, tile + 1)
            dve.tensor_scalar(xg[:, j % 2, :], chunk(x, m),
                              cols[:, one(m + gain)], None, ALU.mult).then_inc(gained, 1)

        def new_chunk_lo(dve, norm, m, j):
            dve.wait_ge(xh_done, DC * norm + m + 1)
            dve.tensor_tensor(chunk(xl, m), xg[:, j % 2, :],
                              chunk(xh, m).bitcast(F32), ALU.subtract).then_inc(xl_done, 1)

        def new_chunk_scalar(act, norm, m, j):
            act.wait_ge(gained, DC * norm + m + 1)
            act.activation(chunk(xh, m), xg[:, j % 2, :], ACT.Copy)\
                .then_inc(xh_done, 1)

        def gain_of(name):
            if name == "load":
                return 0
            kind, layer = name
            return DC * (DEPTH + layer) if kind == "out" else DC * (layer + 1)

        def has_norm(name):
            return name != ("down", DEPTH - 1)

        def vector_out(dve, name):
            at = ph[name]
            per = len(pieces_of(name)[0])
            norm = at["norm"] if has_norm(name) else None

            def body(i, last):
                for t in range(per):
                    next_piece(dve, name, i, t, last and t == per - 1)
                    if t % (per // 2) == per // 2 - 1:
                        pair = (2 * (t // (per // 2)), 2 * (t // (per // 2)) + 1)
                        for j in pair:
                            new_chunk_vector(dve, norm, gain_of(name), 4 * i + j, j,
                                             at["tile"] + 4 * i + j,
                                             (mm_done, mm_value(name, i, j)), True)
                        for j in pair:
                            if norm is not None:
                                new_chunk_lo(dve, norm, 4 * i + j, j)

            if norm is None:
                body(0, False)
                body(1, True)
            else:
                run_loop(dve, 0, 2, lambda i, f: body(i, False))

        def scalar_out(act, name):
            at = ph[name]
            per = len(pieces_of(name)[0])

            def body(i, last):
                for t in range(per):
                    next_piece(act, name, i, t, last and t == per - 1)
                    if has_norm(name) and t % (per // 2) == per // 2 - 1:
                        for j in (2 * (t // (per // 2)), 2 * (t // (per // 2)) + 1):
                            new_chunk_scalar(act, at["norm"], 4 * i + j, j)

            if not has_norm(name):
                body(0, False)
                body(1, True)
            else:
                run_loop(act, 0, 2, lambda i, f: body(i, False))

        def pool_squares(pool, name):
            at = ph[name]
            norm = at["norm"]
            base = SQ_STEPS * norm
            need(pool, ss_done, norm)
            pool.memset(sqsum[:, :], 0.0).then_inc(sq_done, 1)
            for_tiles = at["tile"]

            def body(m, first):
                pool.wait_ge(bank_read, m + (for_tiles + 1))
                pool.tensor_tensor(sq[:, :], chunk(x, m), chunk(x, m), ALU.mult)\
                    .then_inc(sq_done, 1)
                pool.wait_ge(sq_done, 2 * m + (base + 2))
                pool.tensor_tensor(sqsum[:, :], sqsum[:, :], sq[:, :], ALU.add).then_inc(sq_done, 1)
                pool.wait_ge(sq_done, 2 * m + (base + 3))

            run_loop(pool, 0, DC, body)

        def scalar_rms(act, norm):
            act.wait_ge(ss_done, norm + 1)
            need(act, rinv_done, norm)
            act.activation(rms[:, :], SS[:, 0:TOK], ACT.Sqrt, scale=1.0 / D, bias=eps[:, :])\
                .then_inc(rms_done, 1)

        def vector_rinv(dve, norm):
            dve.wait_ge(rms_done, norm + 1)
            dve.reciprocal(rinv[:, :], rms[:, :]).then_inc(rinv_done, 1)
            dve.wait_ge(rinv_done, norm + 1)

        def vector_up(dve, layer):
            name = ("up", layer)
            at = ph[name]
            f0, a0, g0 = at["func"], at["act"], FC * layer

            def body(i, first):
                next_piece(dve, name, i, 0)
                if first:
                    vector_rinv(dve, at["norm"] - 1)
                for j in range(2):
                    need(dve, func_done, f0 + 2 * i + j - 1)
                    dve.wait_ge(mm_done, mm_value(name, i, j))
                    dve.tensor_tensor(tbuf[:, j, :], ps[j][:, 0:TOK], rinv[:, :], ALU.mult)\
                        .then_inc(bank_read, 1)
                next_piece(dve, name, i, 1)
                for j in range(2):
                    dve.wait_ge(func_done, f0 + 2 * i + j + 1)
                    dve.tensor_tensor(gs[:, j, :], gbuf[:, j, :], rinv[:, :], ALU.mult)\
                        .then_inc(gs_done, 1)
                for j in range(2):
                    dve.wait_ge(gs_done, g0 + 2 * i + j + 1)
                    dve.wait_ge(mm_done, mm_value(name, i, 2 + j))
                    need(dve, al_done, a0 + 2 * i + j - 1)
                    dve.tensor_tensor(abuf[:, j, :], ps[2 + j][:, 0:TOK], gs[:, j, :], ALU.mult)\
                        .then_inc(bank_read, 1)
                for j in range(2):
                    dve.wait_ge(ah_done, a0 + 2 * i + j + 1)
                    dve.tensor_tensor(chunk(actl, 2 * i + j), abuf[:, j, :],
                                      chunk(acth, 2 * i + j).bitcast(F32), ALU.subtract)\
                        .then_inc(al_done, 1)

            run_loop(dve, 0, FC // 2, body, peel=True)

        def scalar_up(act, layer):
            name = ("up", layer)
            at = ph[name]
            t0, a0, g0 = at["tile"], at["act"], FC * layer

            def body(i, first):
                next_piece(act, name, i, 0)
                if first:
                    scalar_rms(act, at["norm"] - 1)
                for j in range(2):
                    act.wait_ge(bank_read, t0 + 4 * i + j + 1)
                    if not first:
                        act.wait_ge(gs_done, g0 + 2 * i + j - 1)
                    act.activation(gbuf[:, j, :], tbuf[:, j, :], ACT.Silu).then_inc(func_done, 1)
                next_piece(act, name, i, 1)
                for j in range(2):
                    act.wait_ge(bank_read, t0 + 4 * i + 2 + j + 1)
                    act.activation(chunk(acth, 2 * i + j), abuf[:, j, :], ACT.Copy)\
                        .then_inc(ah_done, 1)

            run_loop(act, 0, FC // 2, body, peel=True)

        def pool_setup(pool):
            pool.dma_start(xin[:, 0:NBLK, :], A["x_prompt"][0].rearrange("(b p) d -> p b d", p=P))\
                .then_inc(in_landed, 16)
            pool.dma_start(xin[0:NSAMP, NBLK, :], A["x_sample"].rearrange("b s d -> (b s) d"))\
                .then_inc(in_landed, 16)
            for src, row in (("norm_mix", 0), ("norm_ffn", 32), ("b_gate_b", 64), ("gn_b", 68)):
                flat = A[src].rearrange("a (c p) -> (a c) p", p=P)
                pool.dma_start(col_rows[row:row + flat.shape[0], :], flat).then_inc(cols_landed, 16)
            pool.dma_start(w_rank[:, :, :], A["w_in_b"][0].rearrange("(c p) n -> p c n", p=P)
                           [:, :, GLA_PROJ - RANK:GLA_PROJ]).then_inc(gate_landed, 16)
            pool.dma_start(w_gate[:, :], A["w_gate_b"][0]).then_inc(gate_landed, 16)

        def scalar_setup(act):
            act.dma_start(ident[:, :], A["c_ident"]).then_inc(const_landed, 16)
            act.dma_start(halves[:, :], A["c_halves"]).then_inc(const_landed, 16)
            act.dma_start(own[:, :], A["c_own"]).then_inc(const_landed, 16)
            act.dma_start(table[:, :], A["page_table"].rearrange("(o b) n -> o (b n)", o=1))\
                .then_inc(table_landed, 16)

        def pe_load(pe):
            pe.wait_ge(const_landed, 48)
            pe.wait_ge(cols_landed, 64)
            pe.transpose(TURN[0][:, 0:70], col_rows[:, :], ident[0:70, 0:70]).then_inc(cols_turned, 1)
            pe.wait_ge(in_landed, 32)
            for m in range(DC):
                need(pe, bank_read, m - BANKS + 1)
                bank = ps[m % BANKS]
                for b in range(NBLK):
                    pe.transpose(bank[:, b * P:(b + 1) * P], xin[:, b, m * P:(m + 1) * P], ident[:, :])
                pe.transpose(bank[:, SEQ:TOK], xin[0:NSAMP, NBLK, m * P:(m + 1) * P],
                             ident[0:NSAMP, 0:NSAMP]).then_inc(tile_made, 1)

        def vector_load(dve):
            dve.memset(eps[:, :], EPS).then_inc(ones_done, 1)
            dve.memset(ones[:, :], 1.0).then_inc(ones_done, 1)
            dve.wait_ge(cols_turned, 1)
            dve.tensor_copy(cols[:, :], TURN[0][:, 0:70]).then_inc(cols_done, 1)
            dve.wait_ge(cols_done, 1)
            split_lo(dve, 0, 0, KC)
            for m in range(DC):
                new_chunk_vector(dve, 0, 0, m, m, m, (tile_made, m + 1), False)
                if m:
                    new_chunk_lo(dve, 0, m - 1, m - 1)
            new_chunk_lo(dve, 0, DC - 1, DC - 1)

        def scalar_load(act):
            split_hi(act, 0, 16, 0, KC)
            for m in range(DC):
                new_chunk_scalar(act, 0, m, m)

        def vector_in(dve, name, start, end, whole=False, stats_of=None, first_of_phase=False):
            at = ph[name]

            def body(i, first):
                for t in range(2):
                    next_piece(dve, name, i, t)
                    if first and first_of_phase and t == 0:
                        vector_rinv(dve, at["norm"] - 1)
                    for j in (2 * t, 2 * t + 1):
                        dve.wait_ge(mm_done, mm_value(name, i, j))
                        out = chunk(feat, 4 * i + j) if whole else tbuf[:, j, :]
                        if not whole:
                            need(dve, func_done, at["func"] + 4 * i + j - BANKS + 1)
                        dve.tensor_tensor(out, ps[j][:, 0:TOK], rinv[:, :], ALU.mult)\
                            .then_inc(bank_read, 1)
                    if stats_of is not None and t == 0 and not first:
                        vector_stats(dve, name, i + (-1))

            run_loop(dve, start, end, body, peel=first_of_phase or stats_of is not None)
            if stats_of is not None:
                vector_stats(dve, name, end - 1)

        def vector_stats(dve, name, i):
            dve.wait_ge(unturned, 8 * i + (2 * ph[name]["turn"] + 8))
            for b in range(NBLK + 1):
                src = vt[:, b, cut(i, 4 * P)] if b < NBLK else vts[:, cut(i, 4 * P)]
                n = P if b < NBLK else NSAMP
                dve.bn_stats(stats[0:n, b, one(i), :].rearrange("p a s -> p (a s)"), src)\
                    .then_inc(stats_done, 1)

        def scalar_in(act, name, start, end, func, turns=False, into_feat=None, reads_feat=False,
                      first_of_phase=False):
            at = ph[name]
            partial = name[1] % 3 == 1

            def finish_turn(i, j):
                step = i + (-start)
                q = 4 * step + (at["turn"] + j)
                act.wait_ge(turned, q + 1)
                m = 4 * step + j
                if partial:
                    prompts, samples = v_tok, vs_tok
                else:
                    prompts, samples = vt, vts
                bank = TURN[j % 2]
                act.activation(prompts[:, :, cut(m, P)],
                               bank[:, 0:SEQ].rearrange("p (b t) -> p b t", b=NBLK), ACT.Copy)\
                    .then_inc(unturned, 1)
                act.activation(samples[:, cut(m, P)], bank[0:NSAMP, SEQ:SEQ + P], ACT.Copy)\
                    .then_inc(unturned, 1)

            def body(i, first):
                for t in range(2):
                    next_piece(act, name, i, t)
                    if first and first_of_phase and t == 0:
                        scalar_rms(act, at["norm"] - 1)
                    if func is None:
                        continue
                    for j in (2 * t, 2 * t + 1):
                        act.wait_ge(bank_read, at["tile"] + 4 * i + j + 1)
                        src = chunk(feat, 4 * i + j) if reads_feat else tbuf[:, j, :]
                        if turns:
                            need(act, turned, 4 * (i + (-start)) + (at["turn"] + j - BANKS + 1))
                            out = gbuf[:, j, :]
                        else:
                            out = chunk(feat, 4 * i + (j + into_feat))
                        act.activation(out, src, func).then_inc(func_done, 1)
                        if turns and not (first and j == 0):
                            finish_turn(i, j - 1)

            if turns and name[1]:
                act.wait_ge(stored, 16 * (0, 1, 2, 6)[name[1]])
            run_loop(act, start, end, body, peel=turns or first_of_phase)
            if turns:
                finish_turn(end - 1, BANKS - 1)

        def sgu_number(layer):
            return layer // 3

        def pool_sgu(pool, layer):
            s = sgu_number(layer)
            at = ph[("in", layer)]
            need(pool, tile_made, 1) if layer == 0 else pool.wait_ge(mm_done, 2 * at["piece"])
            pool.dma_start(ln_gain[:, :], A["ln_a_g"][s:s + 1, :].broadcast_to([P, HALF]))\
                .then_inc(ln_landed, 16)
            pool.dma_start(ln_bias[:, :], A["ln_a_b"][s:s + 1, :].broadcast_to([P, HALF]))\
                .then_inc(ln_landed, 16)
            pool.dma_start(ws_nat[:, :, :], A["w_s_a"][s].rearrange("g i j -> i g j"))\
                .then_inc(ws_landed, 16)
            if s:
                pool.wait_ge(diag_done, s)
            pool.dma_start(w00[:, :], A["w_s_a"][s].rearrange("g i j -> (i j) g")[0:1, :]
                           .broadcast_to([NSAMP, GROUPS]), allow_slow_non_contiguous=True)\
                .then_inc(w00_landed, 16)
            pool.wait_ge(ws_landed, 16 * (s + 1))
            pool.affine_select(out=ws_nat[:, :, :], in_=ws_nat[:, :, :], compare_op=ALU.is_ge,
                               fill=0.0, base=0, pattern=[[0, GROUPS], [-1, P]],
                               channel_multiplier=1).then_inc(ws_masked, 1)
            pool.wait_ge(ln_landed, 32 * (s + 1))
            n = 9 * s
            for b in range(NBLK + 1):
                pool.wait_ge(lninv_done, (NBLK + 1) * s + b + 1)
                v = vt[:, b, :] if b < NBLK else vts[:, :]
                rows = P if b < NBLK else NSAMP
                pool.tensor_scalar(v, v, moments[0:rows, b, 0:1], lninv[0:rows, b:b + 1],
                                   ALU.subtract, ALU.mult).then_inc(lnormed, 1)
                pool.wait_ge(lnormed, n + 1)
                pool.tensor_tensor(v, v, ln_gain[0:rows, :], ALU.mult).then_inc(lnormed, 1)
                pool.wait_ge(lnormed, n + 2)
                pool.tensor_tensor(v, v, ln_bias[0:rows, :], ALU.add).then_inc(lnormed, 1)
                n += 3
            pool.wait_ge(lnormed, n)
            store(pool, A["sgu_v_sample"][s].rearrange("b o d -> (b o) d"), vts[:, :])
            pool.wait_ge(mm_done, 2 * (at["piece"] + HC))
            b_s = A["b_s_a"][s:s + 1]
            for b in range(NBLK):
                pool.dma_start(ws_bias[:, :, b * P:(b + 1) * P], b_s).then_inc(ws_bias_landed, 16)
            pool.wait_ge(ws_bias_landed, 32 * (s + 1))
            pool.tensor_copy(ws_bias[:, :, SEQ:TOK], ws_bias[:, :, 0:1]
                             .broadcast_to([1, GROUPS, NSAMP])).then_inc(ws_bias_done, 1)

        def vector_moments(dve, layer):
            s = sgu_number(layer)
            dve.wait_ge(stats_done, 6 * (NBLK + 1) * (s + 1))
            for b in range(NBLK + 1):
                n = P if b < NBLK else NSAMP
                dve.bn_aggr(moments[0:n, b, :], stats[0:n, b, :, :].rearrange("p a s -> p (a s)"))\
                    .then_inc(moments_done, 1)
            for b in range(NBLK + 1):
                n = P if b < NBLK else NSAMP
                dve.wait_ge(lnstd_done, (NBLK + 1) * s + b + 1)
                dve.reciprocal(lninv[0:n, b:b + 1], lnstd[0:n, b:b + 1]).then_inc(lninv_done, 1)

        def scalar_lnstd(act, layer):
            s = sgu_number(layer)
            for b in range(NBLK + 1):
                n = P if b < NBLK else NSAMP
                act.wait_ge(moments_done, (NBLK + 1) * s + b + 1)
                act.activation(lnstd[0:n, b:b + 1], moments[0:n, b, 1:2], ACT.Sqrt, scale=1.0,
                               bias=eps[0:n, :]).then_inc(lnstd_done, 1)

        def pe_sgu(pe, layer):
            s = sgu_number(layer)
            at = ph[("mix", layer)]
            pe.wait_ge(ws_masked, s + 1)
            for g in range(GROUPS):
                pe.transpose(TURN[g // 4][:, (g % 4) * P:(g % 4 + 1) * P], ws_nat[:, g, :],
                             ident[:, :]).then_inc(ws_turned, 1)
            pe.wait_ge(ws_ready, 2 * (s + 1))
            pe.wait_ge(ws_bias_done, s + 1)
            pe.wait_ge(diag_done, s + 1)
            pe.wait_ge(lnormed, 9 * (s + 1))
            for c in range(HC):
                g = c // GC
                bank = ps[c % BANKS]
                side = slice(c * P, (c + 1) * P)
                need(pe, bank_read, at["tile"] + c - BANKS + 1)
                pe.matmul(bank[:, 0:TOK], ones[0:1, 0:P], ws_bias[0:1, g, :], start=True, stop=False,
                          skip_group_check=True)
                for b in range(NBLK):
                    pe.matmul(bank[:, b * P:(b + 1) * P], vt[:, b, side], ws_t[:, g, :],
                              start=False, stop=False, skip_group_check=True)
                pe.matmul(bank[:, SEQ:TOK], vts[:, side], ws_diag[:, g, :], start=False, stop=True,
                          skip_group_check=True).then_inc(tile_made, 1)

        def made_before(layer):
            return DC + HC * (layer // 3)

        def vector_sgu(dve, layer):
            s = sgu_number(layer)
            at = ph[("mix", layer)]
            dve.wait_ge(w00_landed, 16 * (s + 1))
            dve.tensor_tensor(ws_diag[:, :, :],
                              ident[0:NSAMP, 0:NSAMP].unsqueeze(1).broadcast_to([NSAMP, GROUPS, NSAMP]),
                              w00[:, :].unsqueeze(2).broadcast_to([NSAMP, GROUPS, NSAMP]), ALU.mult)\
                .then_inc(diag_done, 1)
            dve.wait_ge(func_done, ph[("in", layer)]["func"] + 2 * HC)

            def body(i, first):
                for j in range(BANKS):
                    dve.wait_ge(tile_made, made_before(layer) + 4 * i + j + 1)
                    need(dve, al_done, at["act"] + 4 * i + j - 1)
                    dve.tensor_tensor(abuf[:, j % 2, :], ps[j][:, 0:TOK], chunk(feat, 4 * i + j),
                                      ALU.mult).then_inc(bank_read, 1)
                    if j % 2:
                        for e in (j - 1, j):
                            dve.wait_ge(ah_done, at["act"] + 4 * i + e + 1)
                            dve.tensor_tensor(chunk(actl, 4 * i + e), abuf[:, e % 2, :],
                                              chunk(acth, 4 * i + e).bitcast(F32), ALU.subtract)\
                                .then_inc(al_done, 1)

            run_loop(dve, 0, HC // BANKS, body, peel=at["act"] == 0)

        def scalar_sgu(act, layer):
            s = sgu_number(layer)
            at = ph[("mix", layer)]
            for h in range(2):
                act.wait_ge(ws_turned, GROUPS * s + 4 * (h + 1))
                act.activation(ws_t[:, 4 * h:4 * h + 4, :],
                               TURN[h][:, :].rearrange("p (g t) -> p g t", g=4), ACT.Copy)\
                    .then_inc(ws_ready, 1)
            act.wait_ge(lnormed, 9 * (s + 1))

            def body(i, first):
                for j in range(BANKS):
                    act.wait_ge(bank_read, at["tile"] + 4 * i + j + 1)
                    act.activation(chunk(acth, 4 * i + j), abuf[:, j % 2, :], ACT.Copy)\
                        .then_inc(ah_done, 1)

            run_loop(act, 0, HC // BANKS, body)

        def pe_final(pe):
            at = ph["final"]["tile"]
            for m in range(DC):
                pe.wait_ge(bank_read, at + m - BANKS + 1)
                pe.wait_ge(bank_read, ph[("down", DEPTH - 1)]["tile"] + m + 1)
                bank = ps[m % BANKS]
                for b in range(NBLK):
                    pe.transpose(bank[:, b * P:(b + 1) * P], x[:, m, b * P:(b + 1) * P], ident[:, :])
                pe.transpose(bank[0:NSAMP, SEQ:SEQ + P], x[:, m, SEQ:TOK], ident[:, :])\
                    .then_inc(tile_made, 1)

        def vector_final(dve):
            base = made_before(DEPTH - 1) + HC
            for m in range(DC):
                dve.wait_ge(tile_made, base + m + 1)
                bank = ps[m % BANKS]
                side = slice(m * P, (m + 1) * P)
                dve.tensor_copy(ytok[0:NSAMP, NBLK, side], bank[0:NSAMP, SEQ:SEQ + P])\
                    .then_inc(y_done, 1)
                dve.tensor_copy(ytok[:, 0:NBLK, side],
                                bank[:, 0:SEQ].rearrange("p (b t) -> p b t", b=NBLK))\
                    .then_inc(bank_read, 1)
            dve.wait_ge(y_done, DC)
            dve.wait_ge(bank_read, ph["final"]["tile"] + DC)
            for b in range(NBLK + 1):
                n = P if b < NBLK else NSAMP
                dve.wait_ge(fstd_done, b + 1)
                dve.reciprocal(small[0:n, 8 + b:9 + b], small[0:n, 4 + b:5 + b]).then_inc(finv_done, 1)
            dve.wait_ge(fin_landed, 16)
            for b in range(NBLK + 1):
                n = P if b < NBLK else NSAMP
                dve.wait_ge(finv_done, b + 1)
                dve.wait_ge(fsq_done, b + 1)
                dve.scalar_tensor_tensor(out=yout[0:n, b, :], in0=ytok[0:n, b, :],
                                         scalar=small[0:n, 8 + b:9 + b], in1=gain_fin[0:n, :],
                                         op0=ALU.mult, op1=ALU.mult).then_inc(y_done, 1)

        def scalar_final(act):
            act.wait_ge(bank_read, ph["final"]["tile"] + DC)
            act.wait_ge(y_done, DC)
            for b in range(NBLK + 1):
                n = P if b < NBLK else NSAMP
                act.activation(yout[0:n, b, :], ytok[0:n, b, :], ACT.Square,
                               accum_out=small[0:n, b:b + 1]).then_inc(fsq_done, 1)
            for b in range(NBLK + 1):
                n = P if b < NBLK else NSAMP
                act.wait_ge(fsq_done, b + 1)
                act.activation(small[0:n, 4 + b:5 + b], small[0:n, b:b + 1], ACT.Sqrt,
                               scale=1.0 / D, bias=eps[0:n, :]).then_inc(fstd_done, 1)

        def pool_final(pool):
            pool.wait_ge(y_done, DC + NBLK)
            store(pool, A["y_prompt"][0].rearrange("(b p) d -> p b d", p=P), yout[:, 0:NBLK, :])
            pool.wait_ge(y_done, DC + NBLK + 1)
            store(pool, A["y_sample"].rearrange("b s d -> (b s) d"), yout[0:NSAMP, NBLK, :])

        G0 = ph[("mix", 1)]
        inner = range(1, len(LEVELS))
        V_NAMES = (["onehot", "gl"] + [f"z{h}" for h in range(GH)] + ["minz", "loga"]
                   + [f"cum{h}" for h in range(GH)] + ["att0", "cpd0", "cpd1", "qf0"]
                   + [n for lv in inner for n in ([f"qf{lv}"] + (["cp0_0"] if lv == 1 else
                                                                  [f"cp{lv - 1}_0", f"cp{lv - 1}_1"]))]
                   + [f"cp{inner[-1]}_{e}" for e in range(2)]
                   + [f"sn{b}_{h}" for b in range(NSAMP) for h in range(GH)]
                   + [f"o{i}" for i in range(DC)] + ["os", "hinv"]
                   + [f"og{i}" for i in range(DC)])
        S_NAMES = (["qs", "kc", "qss", "absz", "e", "ln", "ea", "edk", "kt0", "kt1"]
                   + [f"ed{lv}" for lv in range(len(LEVELS))] + ["sf0", "sf1"]
                   + [f"sm{b}_{h}" for b in range(NSAMP) for h in range(GH)] + ["silu"]
                   + [f"hstd{h}" for h in range(GH)])
        G_NAMES = (["qf0s", "kf0s", "dk", "kd"]
                   + [f"{n}{lv}" for lv in range(len(LEVELS)) for n in ("dl", "dr", "kf")] + ["osq"])
        T_NAMES = (["gl"] + [f"z{h}" for h in range(GH)] + ["dg", "kt0", "kt1"]
                   + [f"lv{lv}" for lv in range(len(LEVELS))] + ["st0", "st1"]
                   + [n for b in range(NSAMP) for n in (f"vb{b}", f"so{b}")]
                   + [f"o{i}" for i in range(DC)] + [f"hs{h}" for h in range(GH)])
        gla_v = Steps(sem("gla_vector"), V_NAMES)
        gla_s = Steps(sem("gla_scalar"), S_NAMES)
        gla_g = Steps(sem("gla_gpsimd"), G_NAMES)
        gla_t = Steps(sem("gla_tensor"), T_NAMES)

        def level_banks(lv):
            return [ps[1], ps[2]] if lv % 2 == 0 else [ps[3], ps[7]]

        def halves_of(t, m):
            return t[:, :, :].rearrange("p h (n e m) -> p (h n) e m", e=2, m=m)

        def pe_gla(pe):
            w = gla_v.wait
            pe.wait_ge(gate_landed, 32)
            pe.wait_ge(bank_read, G0["tile"])
            for c in range(DC):
                pe.matmul(ps[0][0:RANK, 0:TOK], w_rank[:, c, :], xh[:, c, :].bitcast(F32),
                          start=(c == 0), stop=False)
                mm = pe.matmul(ps[0][0:RANK, 0:TOK], w_rank[:, c, :], xl[:, c, :].bitcast(F32),
                               start=False, stop=(c == DC - 1))
            gla_t.did(mm, "gl")
            w(pe, "gl")
            for h in range(GH):
                gla_t.did(pe.matmul(ps[h][:, 0:TOK], w_gate[:, h * DK:(h + 1) * DK], gl[:, :],
                                    start=True, stop=True), f"z{h}")
            gla_s.wait(pe, "kc")
            w(pe, "z3")
            scores(pe, level_banks(0), kc, qc, "dg")
            gla_g.wait(pe, "kd")
            pe.wait_ge(unturned, 2 * (ph[("in", 1)]["turn"] + DC))
            for b in range(NBLK):
                for h in range(GH):
                    mm = pe.transpose(TURN[b][:, h * P:(h + 1) * P], kd[:, h, b * P:(b + 1) * P],
                                      ident[:, :])
                gla_t.did(mm, f"kt{b}")
            for lv in range(len(LEVELS)):
                w(pe, f"qf{lv}")
                gla_g.wait(pe, f"kf{lv}")
                if lv == 0:
                    for h in range(GH):
                        mm = pe.matmul(ps[0][:, h * P:(h + 1) * P], kf[:, h, 0:P], qf[:, h, P:SEQ],
                                       start=True, stop=True, skip_group_check=True)
                    gla_t.did(mm, "lv0")
                    continue
                if lv == 2:
                    w(pe, "cpd1")
                if lv > 2:
                    w(pe, f"cp{lv - 2}_1")
                scores(pe, level_banks(lv), kf, qf, f"lv{lv}")
            gla_s.wait(pe, "kt1")
            for h in range(GH):
                for b in range(NBLK):
                    mm = pe.matmul(TURN[h // 2][:, (h % 2) * DV:(h % 2 + 1) * DV],
                                   kd_tok[:, b, h * DK:(h + 1) * DK],
                                   v_tok[:, b, h * DV:(h + 1) * DV], start=(b == 0),
                                   stop=(b == NBLK - 1), skip_group_check=True)
                if h % 2:
                    gla_t.did(mm, f"st{h // 2}")
            w(pe, "onehot")
            w(pe, "cp0_0")
            for b in range(NSAMP):
                if b < 2:
                    w(pe, f"cp{inner[-1] - (inner[-1] + b) % 2}_1")
                else:
                    w(pe, f"sn{b - 2}_{GH - 1}")
                for e in range(2):
                    mm = pe.matmul(level_banks(b)[e][:, :], onehot[:, b, :],
                                   vs_tok[:, e * 512:(e + 1) * 512], start=True, stop=True)
                gla_t.did(mm, f"vb{b}")
                w(pe, f"sn{b}_{GH - 1}")
                gla_s.wait(pe, "qss")
                for i in range(DC):
                    h, e = i // 2, i % 2
                    mm = pe.matmul(ps[0][:, i * NSAMP + b:i * NSAMP + b + 1],
                                   states[:, b % 4, h, e * P:(e + 1) * P],
                                   feat[:, h, SEQ + b:SEQ + b + 1], start=True, stop=True,
                                   skip_group_check=True)
                gla_t.did(mm, f"so{b}")
            for i in range(DC):
                h, side = i // 2, slice(i * P, (i + 1) * P)
                bank = [ps[1], ps[2], ps[3], ps[7]][i % 4]
                if i >= 4:
                    w(pe, f"o{i - 4}")
                pe.matmul(bank[:, 0:P], v_tok[:, 0, side], att[:, h, 0, :], start=True, stop=True,
                          skip_group_check=True)
                pe.matmul(bank[:, P:SEQ], v_tok[:, 0, side], att01[:, h, :], start=True, stop=False,
                          skip_group_check=True)
                gla_t.did(pe.matmul(bank[:, P:SEQ], v_tok[:, 1, side], att[:, h, 1, :], start=False,
                                    stop=True, skip_group_check=True), f"o{i}")
            gla_g.wait(pe, "osq")
            for h in range(GH):
                bank = [ps[4], ps[5], ps[6], ps[0]][h]
                if h == 1:
                    gla_s.wait(pe, "sf1")
                for e in range(2):
                    mm = pe.matmul(bank[:, 0:TOK], ones[:, 0:P], o_sq[:, 2 * h + e, :],
                                   start=(e == 0), stop=(e == 1))
                gla_t.did(mm, f"hs{h}")

        def scores(pe, banks, k, q, name):
            for h in range(GH):
                for b in range(NBLK):
                    at = (h % 2) * SEQ + b * P
                    side = slice(b * P, (b + 1) * P)
                    mm = pe.matmul(banks[h // 2][:, at:at + P], k[:, h, side], q[:, h, side],
                                   start=True, stop=True, skip_group_check=True)
            gla_t.did(mm, name)

        def vector_gla(dve):
            did, wt = gla_v.did, gla_t.wait
            dve.wait_ge(mm_done, 2 * ph[("out", 1)]["piece"])
            wt(dve, "gl")
            did(dve.tensor_copy(onehot[:, :, :], ident[0:NSAMP, 0:NSAMP].unsqueeze(2)
                                .broadcast_to([NSAMP, NSAMP, P])), "onehot")
            did(dve.tensor_tensor(gl[:, :], ps[0][0:RANK, 0:TOK], rinv[0:RANK, :], ALU.mult), "gl")
            for h in range(GH):
                wt(dve, f"z{h}")
                did(dve.tensor_scalar(zt[:, h, :], ps[h][:, 0:TOK], cols[:, 64 + h:65 + h], None,
                                      ALU.add), f"z{h}")
            gla_v.wait(dve, "z3")
            gla_s.wait(dve, "absz")
            did(dve.tensor_scalar(zt[:, :, :], zt[:, :, :], 0.0, 1.0 / GATE_NORM, ALU.min, ALU.mult),
                "minz")
            gla_s.wait(dve, "ln")
            gla_v.wait(dve, "minz")
            did(dve.scalar_tensor_tensor(out=loga[:, :, :], in0=loga[:, :, :],
                                         scalar=-1.0 / GATE_NORM, in1=zt[:, :, :], op0=ALU.mult,
                                         op1=ALU.add), "loga")
            gla_v.wait(dve, "loga")
            for h in range(GH):
                did(dve.tensor_tensor_scan(cum[:, h, :], ones[:, 0:SEQ], loga[:, h, 0:SEQ], 0.0,
                                           ALU.mult, ALU.add), f"cum{h}")
            did(dve.memset(att[:, :, :, :], 0.0), "att0")
            wt(dve, "dg")
            gla_v.wait(dve, "att0")
            dve.wait_ge(mask_landed, 16)
            copy_level(dve, len(LEVELS) - 1, level_banks(0), "cpd")
            for lv, m in enumerate(LEVELS):
                gla_s.wait(dve, f"ed{lv}")
                if lv:
                    wt(dve, f"lv{lv - 1}")
                else:
                    gla_g.wait(dve, "qf0s")
                    gla_s.wait(dve, "qs")
                did(dve.tensor_tensor(halves_of(qf, m)[:, :, 1, :], halves_of(qc, m)[:, :, 1, :],
                                      halves_of(decay[lv % 2], m)[:, :, 1, :], ALU.mult), f"qf{lv}")
                if lv == 1:
                    wt(dve, "lv0")
                    did(dve.tensor_copy(att01[:, :, :], ps[0][:, :].rearrange("p (h t) -> p h t", h=GH)),
                        "cp0_0")
                elif lv > 1:
                    copy_level(dve, lv - 2, level_banks(lv - 1), f"cp{lv - 1}_")
            wt(dve, f"lv{inner[-1]}")
            copy_level(dve, inner[-1] - 1, level_banks(inner[-1]), f"cp{inner[-1]}_")
            for b in range(NSAMP):
                wt(dve, f"vb{b}")
                for h in range(GH):
                    gla_s.wait(dve, f"sm{b}_{h}")
                    bank = level_banks(b)[h // 2]
                    did(dve.scalar_tensor_tensor(
                        out=states[:, b % 4, h, :], in0=bank[:, (h % 2) * DV:(h % 2 + 1) * DV],
                        scalar=feat[:, GH + h, SEQ + b:SEQ + b + 1], in1=states[:, b % 4, h, :],
                        op0=ALU.mult, op1=ALU.add), f"sn{b}_{h}")
            for i in range(DC):
                wt(dve, f"o{i}")
                bank = [ps[1], ps[2], ps[3], ps[7]][i % 4]
                did(dve.tensor_copy(feat[:, DC + i, 0:SEQ], bank[:, 0:SEQ]), f"o{i}")
            did(dve.tensor_copy(feat[:, DC:2 * DC, SEQ:TOK],
                                ps[0][:, 0:DC * NSAMP].rearrange("p (i b) -> p i b", i=DC)), "os")
            gla_s.wait(dve, "hstd3")
            did(dve.reciprocal(head_std[:, :, :], head_std[:, :, :]), "hinv")
            gla_v.wait(dve, "hinv")
            for i in range(DC):
                need(dve, al_done, G0["act"] + i - 1)
                did(dve.scalar_tensor_tensor(out=feat[:, DC + i, :], in0=feat[:, DC + i, :],
                                             scalar=cols[:, 68 + i % 2:69 + i % 2],
                                             in1=head_std[:, i // 2, :], op0=ALU.mult, op1=ALU.mult),
                    f"og{i}")
                gla_v.wait(dve, f"og{i}")
                dve.tensor_tensor(abuf[:, i % 2, :], feat[:, DC + i, :], feat[:, 2 * DC + i, :],
                                  ALU.mult).then_inc(a_done, 1)
                if i:
                    mixer_lo(dve, G0["act"], i - 1)
            mixer_lo(dve, G0["act"], DC - 1)

        def copy_level(dve, mask, banks, name):
            for e in range(2):
                if e == 0 and name != "cpd":
                    gla_t.wait(dve, f"lv{name[2:-1]}")
                if name != "cpd":
                    former = "cpd" if name == "cp1_" else f"cp{mask}_"
                    gla_v.wait(dve, f"{former}{e}")
                gla_v.did(dve.copy_predicated(
                    att[:, 2 * e:2 * e + 2, :, :].rearrange("p h b t -> p (h b) t"),
                    level_mask[:, mask:mask + 1, :].broadcast_to([P, 2 * NBLK, P]),
                    banks[e][:, :].rearrange("p (n t) -> p n t", t=P)), f"{name}{e}")

        def mixer_lo(dve, act0, c):
            dve.wait_ge(ah_done, act0 + c + 1)
            dve.tensor_tensor(actl[:, c, :], abuf[:, c % 2, :], acth[:, c, :].bitcast(F32),
                              ALU.subtract).then_inc(al_done, 1)

        def mixer_hi(act, act0, c, number):
            act.wait_ge(a_done, number + 1)
            act.activation(acth[:, c, :], abuf[:, c % 2, :], ACT.Copy).then_inc(ah_done, 1)

        def scalar_gla(act):
            did, wv, wg, wt = gla_s.did, gla_v.wait, gla_g.wait, gla_t.wait
            act.wait_ge(bank_read, G0["tile"])
            wt(act, "gl")
            did(act.activation(qc[:, :, :], feat[:, 0:GH, 0:SEQ], ACT.Copy, scale=DK ** -0.5), "qs")
            did(act.activation(kc[:, :, :], feat[:, GH:2 * GH, 0:SEQ], ACT.Copy), "kc")
            did(act.activation(feat[:, 0:GH, SEQ:TOK], feat[:, 0:GH, SEQ:TOK], ACT.Copy,
                               scale=DK ** -0.5), "qss")
            wv(act, "z3")
            did(act.activation(loga[:, :, :], zt[:, :, :], ACT.Abs), "absz")
            gla_s.wait(act, "absz")
            did(act.activation(loga[:, :, :], loga[:, :, :], ACT.Exp, scale=-1.0), "e")
            gla_s.wait(act, "e")
            did(act.activation(loga[:, :, :], loga[:, :, :], ACT.Ln, bias=1.0), "ln")
            wv(act, "loga")
            did(act.activation(ea[:, :, :], loga[:, :, SEQ:TOK], ACT.Exp), "ea")
            wg(act, "dk")
            did(act.activation(decay[1][:, :, :], decay[1][:, :, :], ACT.Exp), "edk")
            for b in range(NBLK):
                wt(act, f"kt{b}")
                did(act.activation(kd_tok[:, b, :], TURN[b][:, :], ACT.Copy), f"kt{b}")
            for lv in range(len(LEVELS)):
                wg(act, f"dr{lv}")
                did(act.activation(decay[lv % 2][:, :, :], decay[lv % 2][:, :, :], ACT.Exp), f"ed{lv}")
            wv(act, f"qf{len(LEVELS) - 1}")
            wg(act, f"kf{len(LEVELS) - 1}")
            for e in range(2):
                wt(act, f"st{e}")
                did(act.activation(s_fin[:, 2 * e:2 * e + 2, :],
                                   TURN[e][:, :].rearrange("p (h v) -> p h v", h=2), ACT.Copy),
                    f"sf{e}")
            gla_s.wait(act, "ea")
            for b in range(NSAMP):
                if b % 4 == 0:
                    act.wait_ge(state_landed, 16 * (b // 4 + 1))
                for h in range(GH):
                    did(act.activation(states[:, b % 4, h, :], states[:, b % 4, h, :], ACT.Copy,
                                       scale=ea[:, h, b:b + 1]), f"sm{b}_{h}")
            did(act.activation(feat[:, 2 * DC:3 * DC, :], feat[:, 2 * DC:3 * DC, :], ACT.Silu), "silu")
            for h in range(GH):
                bank = [ps[4], ps[5], ps[6], ps[0]][h]
                wt(act, f"hs{h}")
                did(act.activation(head_std[:, h, :], bank[:, 0:TOK], ACT.Sqrt, scale=1.0 / DV,
                                   bias=eps[:, :]), f"hstd{h}")
            for c in range(DC):
                mixer_hi(act, G0["act"], c, c)

        def pool_gla(pool):
            did, wv, ws, wt = gla_g.did, gla_v.wait, gla_s.wait, gla_t.wait
            pool.wait_ge(mm_done, 2 * ph[("in", 1)]["piece"])
            pool.dma_start(level_mask[:, :, :], A["c_masks"]).then_inc(mask_landed, 16)
            state = A["state_gla"][0].rearrange("b h k v -> k b h v")
            pool.dma_start(states[:, :, :, :], state[:, 0:4]).then_inc(state_landed, 16)
            did(pool.memset(qf[:, :, :], 0.0), "qf0s")
            did(pool.memset(kf[:, :, :], 0.0), "kf0s")
            wv(pool, "cum3")
            did(pool.tensor_tensor(decay[1][:, :, :], cum[:, :, SEQ - 1:SEQ].broadcast_to([P, GH, SEQ]),
                                   cum[:, :, :], ALU.subtract), "dk")
            ws(pool, "edk")
            ws(pool, "kc")
            did(pool.tensor_tensor(kd[:, :, :], kc[:, :, :], decay[1][:, :, :], ALU.mult), "kd")
            for lv, m in enumerate(LEVELS):
                c, d = halves_of(cum, m), halves_of(decay[lv % 2], m)
                n = GH * SEQ // (2 * m)
                ref = c[:, :, 0, m - 1:m].broadcast_to([P, n, m])
                if lv == 1:
                    gla_g.wait(pool, "kd")
                if lv > 1:
                    wv(pool, f"qf{lv - 2}")
                    gla_g.wait(pool, f"kf{lv - 2}")
                did(pool.tensor_tensor(d[:, :, 0, :], ref, c[:, :, 0, :], ALU.subtract), f"dl{lv}")
                did(pool.tensor_tensor(d[:, :, 1, :], c[:, :, 1, :], ref, ALU.subtract), f"dr{lv}")
                ws(pool, f"ed{lv}")
                if lv:
                    wt(pool, f"lv{lv - 1}")
                else:
                    gla_g.wait(pool, "kf0s")
                did(pool.tensor_tensor(halves_of(kf, m)[:, :, 0, :], halves_of(kc, m)[:, :, 0, :],
                                       d[:, :, 0, :], ALU.mult), f"kf{lv}")
            ws(pool, "sf1")
            store(pool, A["gla_state_prompt"][0, 0].rearrange("h k v -> k h v"), s_fin[:, :, :])
            out = A["gla_state_sample"][0].rearrange("b h k v -> k b h v")
            for half in range(2):
                wv(pool, f"sn{4 * half + 3}_{GH - 1}")
                pool.dma_start(out[:, 4 * half:4 * half + 4], states[:, :, :, :])\
                    .then_inc(state_stored, 16)
                pool.wait_ge(state_stored, 16 * (half + 1))
                if half == 0:
                    wt(pool, "so3")
                    pool.dma_start(states[:, :, :, :], state[:, 4:8]).then_inc(state_landed, 16)
            pool.wait_ge(stored, 32)
            wv(pool, "os")
            did(pool.tensor_tensor(o_sq[:, :, :], feat[:, DC:2 * DC, :], feat[:, DC:2 * DC, :],
                                   ALU.mult), "osq")

        M0 = ph[("mix", 2)]
        NPG = NSAMP * NPAGES
        moba_v = Steps(sem("moba_vector"),
                       ["rows", "rowneg", "bs", "onehot", "nk", "z0", "z1"]
                       + [f"rd{n}" for n in range(NPG)]
                       + ["sl", "sln", "smx", "sri", "spn", "own", "np"]
                       + [n for k in range(MH + 3) for n in (
                           ([f"la{k}", f"lb{k}", f"mxa{k}", f"mxb{k}"] if k < MH else [])
                           + ([f"ri{k - 1}", f"na{k - 1}", f"nb{k - 1}"] if 1 <= k <= MH else [])
                           + ([f"oc{(k - 3) // 2}"] if k >= 3 and k % 2 == 0 else []))]
                       + ["os0", "os1"])
        moba_s = Steps(sem("moba_scalar"),
                       [f"{n}{b}" for b in range(NSAMP) for n in ("qa", "q")] + ["sex", "spt"]
                       + [n for k in range(MH + 1) for n in (
                           ([f"ea{k}", f"eb{k}"] if k < MH else [])
                           + ([f"pt{k - 1}"] if k >= 1 else []))])
        moba_g = Steps(sem("moba_gpsimd"), [f"pr{n}" for n in range(NPG)])
        moba_t = Steps(sem("moba_tensor"),
                       ["rows", "bs", "zn"] + [f"qb{b}" for b in range(NSAMP)] + ["sct", "spt", "pnt"]
                       + [n for k in range(MH + 2) for n in (
                           ([f"s{k}"] if k < MH else []) + ([f"t{k - 1}"] if 1 <= k <= MH else [])
                           + ([f"o{k - 2}"] if k >= 2 else [])
                           + ([f"pv{(k - 2) // 2}"] if k >= 2 and k % 2 == 1 else []))])
        QB = [[ps[2], ps[3]], [ps[5], ps[6]]]
        SB, TB, OB, PVB = [ps[0], ps[2]], [ps[5], ps[6]], [ps[3], ps[7]], ps[1]

        def by_key(h, n):
            last = strip[:, h, n - 1:n]
            return bass.AP(tensor=last.tensor, offset=last.offset, ap=[last.ap[0], [-1, n]])

        def pool_moba(pool):
            pool.wait_ge(mm_done, 2 * ph[("out", 2)]["piece"])
            for b in range(NSAMP):
                pool.dma_start(relb[:, b, :], A["rel_bias"]).then_inc(bias_landed, 16)
            pool.dma_start(of_strip[:, 0:STRIP], A["c_of_strip"]).then_inc(bias_landed, 16)
            pool.dma_start(of_past[:, :], A["c_of_past"]).then_inc(bias_landed, 16)
            turns = ph[("in", 2)]["turn"] + 3 * DC
            for n in range(NPG):
                b = n // NPAGES
                moba_s.wait(pool, f"q{b}")
                pool.wait_ge(page_landed[n % PAGE_SLOTS], 16 * (n // PAGE_SLOTS + 1))
                if n >= 2:
                    moba_v.wait(pool, f"rd{n - 2}")
                moba_g.did(pool.tensor_tensor(prod[n % 2][:, :], pages[:, n % PAGE_SLOTS, :],
                                              q_row[:, :], ALU.mult), f"pr{n}")
            pool.wait_ge(unturned, 2 * turns)
            for name, at in (("k_new", D), ("v_new", 2 * D)):
                store(pool, A[name + "_prompt"][0, 0].rearrange("(b p) h d -> p b (h d)", p=P),
                      vt[:, :, at:at + D])
                store(pool, A[name + "_sample"][0].rearrange("b o h d -> (b o) (h d)"),
                      vts[:, at:at + D])

        def sp_pages(sp):
            sp.wait_ge(table_landed, 16)
            sp.wait_ge(mm_done, 2 * ph[("in", 2)]["piece"])
            for n in range(2 * NPG):
                page = n % NPG
                if n == PAGE_SLOTS:
                    moba_v.wait(sp, "rowneg")
                    sp.dma_start(scratch.ap()[:, 0:STRIP], rows[:, 0:STRIP])\
                        .then_inc(scratch_landed, 16)
                    sp.wait_ge(scratch_landed, 16)
                    flat = scratch.ap()
                    shifted = bass.AP(tensor=flat.tensor, offset=0,
                                      ap=[[1, P], [STRIP + 1, MH], [1, 2 * P]])
                    sp.dma_start(strip[:, :, :], shifted).then_inc(strip_landed, 16)
                if PAGE_SLOTS <= n < NPG + PAGE_SLOTS:
                    moba_g.wait(sp, f"pr{n - PAGE_SLOTS}")
                elif n >= NPG + PAGE_SLOTS:
                    moba_t.wait(sp, f"pv{(page - PAGE_SLOTS) // NPAGES}")
                cache = A["cache_k"] if n < NPG else A["cache_v"]
                number = sp.value_load(table[0:1, page:page + 1], min_val=0, max_val=NPOOL - 1)
                sp.dma_start(pages[:, n % PAGE_SLOTS, :], cache[0][bass.ds(number, 1), :, :, :]
                             .rearrange("a p h d -> p (a h d)"))\
                    .then_inc(page_landed[n % PAGE_SLOTS], 16)

        def pe_moba(pe):
            did, wv, ws = moba_t.did, moba_v.wait, moba_s.wait
            pe.wait_ge(bank_read, M0["tile"])
            pe.wait_ge(bias_landed, 16 * (NSAMP + 2))
            did(pe.matmul(ps[0][0:MH, 0:STRIP], relb[:, 0, :], of_strip[:, 0:STRIP], start=True,
                          stop=True), "rows")
            did(pe.matmul(ps[1][:, 0:SEQ + 1], relb[:, :, :].rearrange("p b h -> p (b h)"),
                          of_past[:, :], start=True, stop=True), "bs")
            wv(pe, "z1")
            did(pe.matmul(ps[4][:, 0:1], new_z[:, :, :, :].rearrange("p b c e -> p (b c e)"),
                          ones[:, 0:1], start=True, stop=True), "zn")
            pe.wait_ge(unturned, 2 * (ph[("in", 2)]["turn"] + 3 * DC))
            for b in range(NSAMP):
                if b >= 2:
                    ws(pe, f"q{b - 2}")
                for e in range(2):
                    mm = pe.matmul(QB[b % 2][e][:, :], onehot[:, b, :], vts[:, e * 512:(e + 1) * 512],
                                   start=True, stop=True)
                did(mm, f"qb{b}")
            wv(pe, f"rd{NPG - 1}")
            for pg in range(NPAGES):
                mm = pe.transpose(ps[7][:, pg * P:(pg + 1) * P], sc[:, pg, :], ident[:, :])
            did(mm, "sct")
            wv(pe, "spn")
            for pg in range(NPAGES):
                mm = pe.transpose(ps[7][:, pg * P:(pg + 1) * P], slog[:, pg * P:(pg + 1) * P],
                                  ident[:, :])
            did(mm, "spt")
            wv(pe, "own")
            did(pe.transpose(ps[4][0:NSAMP, 0:P], new_own[:, :], ident[:, :]), "pnt")
            ws(pe, "spt")
            wv(pe, "np")
            ws(pe, f"q{NSAMP - 1}")
            for k in range(MH + 2):
                if k < MH:
                    c, r = k // 2, slice(DH * (k % 2), DH * (k % 2) + DH)
                    if k >= 2:
                        wv(pe, f"lb{k - 2}")
                    pe.matmul(SB[k % 2][:, 0:SEQ], feat[r, c, P:SEQ], feat[r, DC + c, 0:SEQ],
                              start=True, stop=True, skip_group_check=True)
                    did(pe.matmul(SB[k % 2][:, SEQ:SEQ + P], feat[r, c, 0:P], feat[r, DC + c, 0:P],
                                  start=True, stop=True, skip_group_check=True), f"s{k}")
                if 1 <= k <= MH:
                    h = k - 1
                    wv(pe, f"nb{h}")
                    if h >= 2:
                        ws(pe, f"pt{h - 2}")
                    for e in range(3):
                        mm = pe.transpose(TB[h % 2][:, e * P:(e + 1) * P],
                                          logit[:, h % 2, e * P:(e + 1) * P], ident[:, :])
                    did(mm, f"t{h}")
                if k >= 2:
                    h = k - 2
                    ws(pe, f"pt{h}")
                    if h >= 4 and h % 2 == 0:
                        wv(pe, f"oc{h // 2 - 2}")
                    bank, r = OB[h // 2 % 2], slice(DH * (h % 2), DH * (h % 2) + DH)
                    v = [vt[:, b, 2 * D + h * DH:2 * D + (h + 1) * DH] for b in range(NBLK)]
                    pe.matmul(bank[r, 0:P], v[0], prob_t[:, h % 2, SEQ:SEQ + P], start=True,
                              stop=True, skip_group_check=True)
                    pe.matmul(bank[r, P:SEQ], v[0], prob_t[:, h % 2, 0:P], start=True, stop=False,
                              skip_group_check=True)
                    did(pe.matmul(bank[r, P:SEQ], v[1], prob_t[:, h % 2, P:SEQ], start=False,
                                  stop=True, skip_group_check=True), f"o{h}")
                    if k % 2:
                        b = (k - 2) // 2
                        for pg in range(NPAGES):
                            n = NPG + NPAGES * b + pg
                            pe.wait_ge(page_landed[n % PAGE_SLOTS], 16 * (n // PAGE_SLOTS + 1))
                        for c in range(DC):
                            at = slice(b * MH + 2 * c, b * MH + 2 * c + 2)
                            for pg in range(NPAGES):
                                pe.matmul(PVB[:, at], pages[:, (NPAGES * b + pg) % PAGE_SLOTS,
                                                            c * P:(c + 1) * P],
                                          sp_tok[:, pg, at], start=(pg == 0), stop=False,
                                          skip_group_check=True)
                            mm = pe.matmul(PVB[:, at], vts[:, 2 * D + c * P:2 * D + (c + 1) * P],
                                           new_p[:, at], start=False, stop=True,
                                           skip_group_check=True)
                        did(mm, f"pv{b}")

        def vector_moba(dve):
            did, wt, ws, wg = moba_v.did, moba_t.wait, moba_s.wait, moba_g.wait
            scale = DH ** -0.5
            wt(dve, "rows")
            did(dve.tensor_copy(rows[:, P - 1:STRIP], ps[0][0:MH, P - 1:STRIP]), "rows")
            did(dve.memset(rows[:, 0:P - 1], NEG), "rowneg")
            wt(dve, "bs")
            did(dve.tensor_copy(sbias[:, :], ps[1][:, 0:SEQ + 1]), "bs")
            did(dve.tensor_copy(onehot[:, :, :], ident[0:NSAMP, 0:NSAMP].unsqueeze(2)
                                .broadcast_to([NSAMP, NSAMP, P])), "onehot")
            did(dve.tensor_tensor(new_qk[:, :, :], feat[:, 0:DC, SEQ:TOK], feat[:, DC:2 * DC, SEQ:TOK],
                                  ALU.mult), "nk")
            moba_v.wait(dve, "nk")
            for e in range(2):
                did(dve.tensor_scalar(new_z[:, :, :, e], new_qk[:, :, :].rearrange("p c b -> p b c"),
                                      halves[:, e:e + 1], None, ALU.mult), f"z{e}")
            for n in range(NPG):
                wg(dve, f"pr{n}")
                b, pg = n // NPAGES, n % NPAGES
                did(dve.tensor_reduce(sc[:, pg, b * MH:(b + 1) * MH],
                                      prod[n % 2][:, :].rearrange("p (h d) -> p h d", h=MH),
                                      AX.X, ALU.add), f"rd{n}")
            wt(dve, "sct")
            did(dve.scalar_tensor_tensor(out=slog[:, 0:SEQ], in0=ps[7][:, 0:SEQ], scalar=scale,
                                         in1=sbias[:, 0:SEQ], op0=ALU.mult, op1=ALU.add), "sl")
            wt(dve, "zn")
            did(dve.scalar_tensor_tensor(out=slog[:, SEQ:SEQ + 1], in0=ps[4][:, 0:1], scalar=scale,
                                         in1=sbias[:, SEQ:SEQ + 1], op0=ALU.mult, op1=ALU.add), "sln")
            moba_v.wait(dve, "sln")
            did(dve.tensor_reduce(small[:, 0:1], slog[:, :], AX.X, ALU.max, negate=True), "smx")
            ws(dve, "sex")
            did(dve.reciprocal(small[:, 2:3], small[:, 1:2]), "sri")
            moba_v.wait(dve, "sri")
            did(dve.tensor_scalar(slog[:, :], slog[:, :], small[:, 2:3], None, ALU.mult), "spn")
            moba_v.wait(dve, "spn")
            did(dve.tensor_scalar(new_own[:, :], own[:, :], slog[:, SEQ:SEQ + 1], None, ALU.mult),
                "own")
            wt(dve, "pnt")
            did(dve.tensor_copy(new_p[:, :], ps[4][0:NSAMP, 0:P]), "np")
            dve.wait_ge(strip_landed, 16)
            for k in range(MH + 3):
                if k < MH:
                    wt(dve, f"s{k}")
                    if k >= 2:
                        wt(dve, f"t{k - 2}")
                    i = k % 2
                    for e, (lo, hi) in enumerate(((0, SEQ), (SEQ, SEQ + P))):
                        did(dve.scalar_tensor_tensor(
                            out=logit[:, i, lo:hi], in0=SB[i][:, lo:hi], scalar=scale,
                            in1=by_key(k, hi - lo), op0=ALU.mult, op1=ALU.add), f"l{'ab'[e]}{k}")
                    for e, (lo, hi) in enumerate(((0, SEQ), (SEQ, SEQ + P))):
                        moba_v.wait(dve, f"l{'ab'[e]}{k}")
                        did(dve.tensor_reduce(softs[:, i, e:e + 1], logit[:, i, lo:hi], AX.X, ALU.max,
                                              negate=True), f"mx{'ab'[e]}{k}")
                if 1 <= k <= MH:
                    h, i = k - 1, (k - 1) % 2
                    ws(dve, f"eb{h}")
                    did(dve.reciprocal(softs[:, i, 4:6], softs[:, i, 2:4]), f"ri{h}")
                    moba_v.wait(dve, f"ri{h}")
                    for e, (lo, hi) in enumerate(((0, SEQ), (SEQ, SEQ + P))):
                        did(dve.tensor_scalar(logit[:, i, lo:hi], logit[:, i, lo:hi],
                                              softs[:, i, 4 + e:5 + e], None, ALU.mult),
                            f"n{'ab'[e]}{h}")
                if k >= 3 and k % 2 == 0:
                    c = (k - 3) // 2
                    wt(dve, f"o{2 * c + 1}")
                    did(dve.tensor_copy(feat[:, c, 0:SEQ], OB[c % 2][:, 0:SEQ]), f"oc{c}")
            wt(dve, f"pv{NSAMP - 1}")
            view = PVB[:, 0:P].rearrange("p (b c e) -> p c b e", b=NSAMP, e=2)
            for e in range(2):
                r = slice(DH * e, DH * e + DH)
                did(dve.tensor_copy(feat[r, 0:DC, SEQ:TOK], view[r, :, :, e]), f"os{e}")
            for c in range(DC):
                dve.wait_ge(ah_done, M0["act"] + c + 1)
                dve.tensor_tensor(actl[:, c, :], feat[:, c, :], acth[:, c, :].bitcast(F32),
                                  ALU.subtract).then_inc(al_done, 1)

        def scalar_moba(act):
            did, wt, wv = moba_s.did, moba_t.wait, moba_v.wait
            for b in range(NSAMP):
                wt(act, f"qb{b}")
                if b:
                    moba_g.wait(act, f"pr{2 * b - 1}")
                for e in range(2):
                    did(act.activation(q_row[:, e * 512:(e + 1) * 512], QB[b % 2][e][:, :], ACT.Copy),
                        f"q{b}" if e else f"qa{b}")
            wv(act, "smx")
            did(act.activation(slog[:, :], slog[:, :], ACT.Exp, bias=small[:, 0:1],
                               accum_out=small[:, 1:2]), "sex")
            wt(act, "spt")
            did(act.activation(sp_tok[:, :, :], ps[7][:, 0:SEQ].rearrange("p (g t) -> p g t", g=NPAGES),
                               ACT.Copy), "spt")
            for k in range(MH + 1):
                if k < MH:
                    i = k % 2
                    for e, (lo, hi) in enumerate(((0, SEQ), (SEQ, SEQ + P))):
                        wv(act, f"mx{'ab'[e]}{k}")
                        did(act.activation(logit[:, i, lo:hi], logit[:, i, lo:hi], ACT.Exp,
                                           bias=softs[:, i, e:e + 1],
                                           accum_out=softs[:, i, 2 + e:3 + e]), f"e{'ab'[e]}{k}")
                if k >= 1:
                    h = k - 1
                    wt(act, f"t{h}")
                    if h >= 2:
                        wt(act, f"o{h - 2}")
                    did(act.activation(prob_t[:, h % 2, :], TB[h % 2][:, 0:3 * P], ACT.Copy), f"pt{h}")
            wv(act, "os1")
            for c in range(DC):
                act.activation(acth[:, c, :], feat[:, c, :], ACT.Copy).then_inc(ah_done, 1)

        block = ctx.enter_context(nc.Block())

        @block.sync
        def _(sp):
            for layer in range(DEPTH):
                for kind in ("in", "out", "up", "down"):
                    stream(sp, (kind, layer))

        @block.gpsimd
        def _(pool):
            pool_setup(pool)
            pool_squares(pool, "load")
            for layer in range(DEPTH):
                if layer % 3 == 0:
                    pool_sgu(pool, layer)
                elif layer % 3 == 1:
                    pool_gla(pool)
                else:
                    pool_moba(pool)
                if layer == DEPTH - 1:
                    pool.wait_ge(al_done, ph[("mix", layer)]["act"] + HC)
                    pool.dma_start(gain_fin[:, :], A["norm_final"].rearrange("(o d) -> o d", o=1)
                                   .broadcast_to([P, D])).then_inc(fin_landed, 16)
                pool_squares(pool, ("out", layer))
                if layer < DEPTH - 1:
                    pool_squares(pool, ("down", layer))
            pool_final(pool)
            pool.wait_ge(stored, 16 * len(STORES))

        @block.scalar
        def _(act):
            scalar_setup(act)
            scalar_load(act)
            for layer in range(DEPTH):
                name = ("in", layer)
                if layer % 3 == 0:
                    scalar_in(act, name, 0, 6, ACT.Gelu, turns=True, first_of_phase=True)
                    scalar_lnstd(act, layer)
                    scalar_in(act, name, 6, 12, ACT.Gelu, into_feat=-HC)
                    scalar_sgu(act, layer)
                elif layer % 3 == 1:
                    scalar_in(act, name, 0, 2, None, first_of_phase=True)
                    scalar_in(act, name, 2, 4, ACT.Copy, turns=True, reads_feat=True)
                    scalar_in(act, name, 4, 6, None)
                    scalar_gla(act)
                else:
                    scalar_in(act, name, 0, 6, ACT.Copy, turns=True, reads_feat=True,
                              first_of_phase=True)
                    scalar_moba(act)
                scalar_out(act, ("out", layer))
                scalar_up(act, layer)
                scalar_out(act, ("down", layer))
            scalar_final(act)

        @block.tensor
        def _(pe):
            pe_load(pe)
            for layer in range(DEPTH):
                name = ("in", layer)
                new_norm = ph[name]["norm"] - 1
                if layer % 3 == 0:
                    pe_project(pe, name, 0, 6, turns_from=0, new_norm=new_norm)
                    pe_project(pe, name, 6, 12)
                    pe_sgu(pe, layer)
                elif layer % 3 == 1:
                    pe_project(pe, name, 0, 2, new_norm=new_norm)
                    pe_project(pe, name, 2, 4, turns_from=2)
                    pe_project(pe, name, 4, 6)
                    pe_gla(pe)
                else:
                    pe_project(pe, name, 0, 6, turns_from=0, new_norm=new_norm)
                    pe_moba(pe)
                pe_out(pe, ("out", layer))
                pe_project(pe, ("up", layer), 0, FC // 2, new_norm=ph[("up", layer)]["norm"] - 1)
                pe_out(pe, ("down", layer))
            pe_final(pe)

        @block.vector
        def _(dve):
            vector_load(dve)
            for layer in range(DEPTH):
                name = ("in", layer)
                if layer % 3 == 0:
                    vector_in(dve, name, 0, 6, stats_of=True, first_of_phase=True)
                    vector_moments(dve, layer)
                    vector_in(dve, name, 6, 12)
                    vector_sgu(dve, layer)
                elif layer % 3 == 1:
                    vector_in(dve, name, 0, 6, whole=True, first_of_phase=True)
                    vector_gla(dve)
                else:
                    vector_in(dve, name, 0, 6, whole=True, first_of_phase=True)
                    vector_moba(dve)
                vector_out(dve, ("out", layer))
                vector_up(dve, layer)
                vector_out(dve, ("down", layer))
            vector_final(dve)


def _constants():
    s, t = np.arange(P)[:, None], np.arange(P)[None, :]
    masks = [(s // (2 * m) == t // (2 * m)) & (s % (2 * m) < m) & (t % (2 * m) >= m)
             for m in LEVELS[1:]] + [s == t]

    def buckets(dist):
        exact = BUCKETS // 2
        far = np.maximum(dist, exact).astype(np.float32)
        large = exact + (np.log(far / exact) / np.float32(np.log(MAXDIST / exact))
                         * (BUCKETS - exact)).astype(np.int32)
        bucket = np.where(dist < exact, dist, np.minimum(large, BUCKETS - 1))
        return (np.arange(BUCKETS)[:, None] == bucket[None]) & (dist >= 0)[None]

    f = np.float32
    return {
        "c_ident": np.eye(P, dtype=f),
        "c_halves": (np.arange(P)[:, None] // DH == np.arange(2)[None]).astype(f),
        "c_own": (np.arange(P)[:, None] // MH == np.arange(NSAMP)[None]).astype(f),
        "c_masks": np.stack(masks, 1).astype(np.int32),
        "c_of_strip": buckets(np.arange(STRIP) - (P - 1)).astype(f),
        "c_of_past": buckets(SEQ - np.arange(SEQ + 1)).astype(f),
    }


_INS = ["x_prompt", "x_sample", "cache_k", "cache_v", "page_table", "state_gla",
        "norm_mix", "norm_ffn", "norm_final", "w_in_a", "ln_a_g", "ln_a_b", "w_s_a", "b_s_a",
        "w_out_a", "w_in_b", "w_gate_b", "b_gate_b", "gn_b", "w_out_b", "w_in_c", "w_out_c",
        "rel_bias", "w_up", "w_down"]
_OUTS = [("y_prompt", (1, SEQ, D)), ("y_sample", (NSAMP, 1, D)),
         ("k_new_prompt", (1, 1, SEQ, MH, DH)), ("v_new_prompt", (1, 1, SEQ, MH, DH)),
         ("k_new_sample", (1, NSAMP, 1, MH, DH)), ("v_new_sample", (1, NSAMP, 1, MH, DH)),
         ("gla_state_prompt", (1, 1, GH, DK, DV)), ("gla_state_sample", (1, NSAMP, GH, DK, DV)),
         ("sgu_v_sample", (2, NSAMP, 1, HALF))]


def kernel(**inputs):
    import concourse.bacc as bacc
    from concourse.bass_utils import run_bass_kernel_spmd

    nc = bacc.Bacc("TRN2", target_bir_lowering=False, num_devices=1)
    arrays, A = {}, {}
    for name, a in [(n, inputs[n]) for n in _INS] + list(_constants().items()):
        a = np.ascontiguousarray(a)
        arrays[f"in_{name}"] = a
        A[name] = nc.dram_tensor(f"in_{name}", a.shape, mybir.dt.from_np(a.dtype),
                                 kind="ExternalInput").ap()
    for name, shape in _OUTS:
        A[name] = nc.dram_tensor(f"out_{name}", shape, F32, kind="ExternalOutput").ap()
    build(nc, A)
    got = run_bass_kernel_spmd(nc, [arrays], core_ids=[0]).results[0]
    return tuple(got[f"out_{name}"] for name, _ in _OUTS)
```

```python
from contextlib import ExitStack

import concourse.bass as bass
from concourse import mybir
import numpy as np

F32 = mybir.dt.float32
F32R = mybir.dt.float32r
I32 = mybir.dt.int32
ALU = mybir.AluOpType
ACT = mybir.ActivationFunctionType
AX = mybir.AxisListType

P = 128
D = 1024
DC = D // P
SEQ = 256
NSAMP = 8
TOK = SEQ + NSAMP
NBLK = SEQ // P
DEPTH = 4
EPS = 1e-6

HALF = 3 * D
HC = HALF // P
GROUPS = 8
GC = HC // GROUPS

GH, DK, DV = 4, 128, 256
RANK = 16
GLA_PROJ = 2 * GH * DK + 2 * GH * DV + RANK
GATE_NORM = 16.0
LEVELS = [128, 64, 32, 16, 8, 4, 2, 1]

MH, DH = 16, 64
NPAGES = 2
NPOOL = NSAMP * NPAGES * 5 // 4
BUCKETS = 32
MAXDIST = 128
STRIP = 3 * P - 1
NEG = -1e30

DFF = 2816
FC = DFF // P

KC = 8
PW = 256
SLOTS = 2
BANKS = 4
PAGE_SLOTS = 4
SQ_STEPS = 2 * DC + 1


def need(eng, sem, value):
    if not isinstance(value, int) or value > 0:
        eng.wait_ge(sem, value)


def run_loop(eng, start, end, body, peel=False):
    if peel:
        body(start, True)
        start += 1
    if end - start == 1:
        body(start, False)
    elif start < end:
        with eng.Fori(start, end) as i:
            body(i, False)


def cut(i, size):
    return slice(i * size, (i + 1) * size) if isinstance(i, int) else bass.ds(i * size, size)


def one(i):
    return slice(i, i + 1) if isinstance(i, int) else bass.ds(i, 1)


def chunk(tensor, m):
    return tensor[:, one(m), :].rearrange("p a t -> p (a t)")


class Steps:

    def __init__(self, sem, names):
        self.sem, self.names, self.at = sem, names, 0
        self.number = {n: k + 1 for k, n in enumerate(names)}
        assert len(self.number) == len(names)

    def did(self, instruction, name):
        assert self.names[self.at] == name, (self.names[self.at], name)
        self.at += 1
        instruction.then_inc(self.sem, 1)

    def wait(self, eng, name):
        eng.wait_ge(self.sem, self.number[name])


def make_plan():
    now = dict(piece=0, tile=0, norm=0, func=0, turn=0, act=0)
    phases = {}

    def add(name, **count):
        phases[name] = dict(now)
        for k, v in count.items():
            now[k] += v

    add("load", tile=DC, norm=1)
    for layer in range(DEPTH):
        if layer % 3 == 0:
            add(("in", layer), piece=2 * HC // 2, tile=2 * HC, func=2 * HC, turn=HC)
            add(("mix", layer), tile=HC, act=HC)
            add(("out", layer), piece=4 * HC // KC, tile=DC, norm=1)
        else:
            turns = 2 * DC // 2 if layer % 3 == 1 else 3 * DC
            add(("in", layer), piece=3 * DC // 2, tile=3 * DC, func=turns, turn=turns)
            add(("mix", layer), act=DC)
            add(("out", layer), piece=DC // 2, tile=DC, norm=1)
        add(("up", layer), piece=FC, tile=2 * FC, func=FC, act=FC)
        add(("down", layer), piece=12, tile=DC, norm=int(layer < DEPTH - 1))
    add("final", tile=DC)
    return phases


def build(nc, A):
    ph = make_plan()
    with ExitStack() as ctx:
        def sem(name):
            return ctx.enter_context(nc.semaphore(name))

        allps = ctx.enter_context(nc.psum_tensor("banks", [P, 8, 512], F32))
        ps = [allps[:, b, :] for b in range(8)]
        SS = ps[4]
        TURN = [ps[5], ps[6]]

        start_of, top = {}, [16640]

        def sb(name, shape, dt=F32):
            size = int(np.prod(shape[1:])) * 4
            start_of[name] = top[0]
            top[0] += -(-size // 32) * 32
            return nc.alloc_sbuf_tensor_at(name, shape, dt, offset=start_of[name])

        def over(name, host, offset, shape, dt=F32):
            start_of[name] = start_of[host] + offset
            return nc.alloc_sbuf_tensor_at(name, shape, dt, offset=start_of[host] + offset)

        raw = sb("raw", [P, SLOTS, KC, PW])
        whi = sb("whi", [P, SLOTS, KC, PW], F32R)
        wlo = sb("wlo", [P, SLOTS, KC, PW], F32R)
        x = sb("x", [P, DC, TOK])
        xh = sb("xh", [P, DC, TOK], F32R)
        xl = sb("xl", [P, DC, TOK], F32R)
        xg = sb("xg", [P, 2, TOK])
        tbuf = sb("tbuf", [P, BANKS, TOK])
        gbuf = sb("gbuf", [P, BANKS, TOK])
        gs = sb("gs", [P, 2, TOK])
        abuf = sb("abuf", [P, 2, TOK])
        rms = sb("rms", [P, TOK])
        rinv = sb("rinv", [P, TOK])
        sqsum = sb("sqsum", [P, TOK])
        sq = sb("sq", [P, TOK])
        ones = sb("ones", [P, SEQ])
        ident = sb("ident", [P, P])
        halves = sb("halves", [P, 2])
        own = sb("own", [P, NSAMP])
        head_of = sb("head_of", [P, MH])
        cols = sb("cols", [P, 70])
        w_rank = sb("w_rank", [P, DC, RANK])
        w_gate = sb("w_gate", [RANK, GH * DK])
        table = sb("table", [1, NSAMP * NPAGES], I32)
        w00 = sb("w00", [NSAMP, GROUPS])
        ws_diag = sb("ws_diag", [NSAMP, GROUPS, NSAMP])
        stats = sb("stats", [P, NBLK + 1, 6, 6])
        moments = sb("moments", [P, NBLK + 1, 2])
        lnstd = sb("lnstd", [P, NBLK + 1])
        lninv = sb("lninv", [P, NBLK + 1])
        lnshift = sb("lnshift", [P, NBLK + 1])
        small = sb("small", [P, 16])
        eps = sb("eps", [P, 1])
        softs = sb("softs", [P, 2, 3, NBLK, 2])
        acth = sb("acth", [P, HC, TOK], F32R)
        actl = sb("actl", [P, HC, TOK], F32R)
        feat = sb("feat", [P, HC, TOK])
        vt = sb("vt", [P, NBLK, HALF])
        vts = sb("vts", [NSAMP, HALF])
        assert top[0] <= 229344, top[0]

        TAIL = DC * TOK * 4
        xin = over("xin", "vt", 0, [P, NBLK + 1, D])
        col_rows = over("col_rows", "vt", 4 * 3 * D, [70, P])
        ytok = over("ytok", "vt", 0, [P, NBLK + 1, D])
        yout = over("yout", "acth", 0, [P, NBLK + 1, D])
        gain_fin = over("gain_fin", "feat", 0, [P, D])
        ln_gain = over("ln_gain", "acth", 0, [P, HALF])
        ln_bias = over("ln_bias", "acth", 4 * HALF, [P, HALF])
        ws_nat = over("ws_nat", "acth", 8 * HALF, [P, GROUPS, P])
        ws_t = over("ws_t", "xh", 0, [P, GROUPS, P])
        ws_bias = over("ws_bias", "xl", 0, [1, GROUPS, TOK])
        v_tok = over("v_tok", "vt", 0, [P, NBLK, GH * DV])
        vs_tok = over("vs_tok", "vt", 8192, [NSAMP, GH * DV])
        kd_tok = over("kd_tok", "vt", 12288, [P, NBLK, GH * DK])
        att = over("att", "vt", 16384, [P, GH, NBLK, P])
        att01 = over("att01", "vt", 20480, [P, GH, P])
        cum = over("cum", "vt", 22528, [P, GH, SEQ])
        qf = over("qf", "vt", 26624, [P, GH, SEQ])
        kf = over("kf", "vt", 30720, [P, GH, SEQ])
        loga = over("loga", "acth", TAIL, [P, GH, TOK])
        zt = over("zt", "acth", TAIL + 4224, [P, GH, TOK])
        decay = [over("decay0", "acth", TAIL + 4224, [P, GH, SEQ]),
                 over("decay1", "acth", TAIL + 8448, [P, GH, SEQ])]
        level_mask = over("level_mask", "gs", 0, [P, len(LEVELS), P], I32)
        gl = over("gl", "acth", TAIL + 13568, [RANK, TOK])
        ea = over("ea", "acth", TAIL + 14624, [P, GH, NSAMP])
        states = over("states", "actl", TAIL, [P, NSAMP // 2, GH, DV])
        onehot = over("onehot", "xh", 0, [NSAMP, NSAMP, P])
        kc = over("kc", "xh", 4096, [P, GH, SEQ])
        kd = over("kd", "xl", 0, [P, GH, SEQ])
        qc = over("qc", "xl", 4096, [P, GH, SEQ])
        o_sq = over("o_sq", "xl", 0, [P, DC, TOK])
        head_std = over("head_std", "acth", TAIL, [P, GH, TOK])
        s_fin = over("s_fin", "acth", TAIL + 4224, [P, GH, DV])
        strip = over("strip", "acth", TAIL, [P, MH, 2 * P])
        pages = over("pages", "actl", TAIL, [P, PAGE_SLOTS, D])
        q_row = over("q_row", "acth", 0, [P, 2, D])
        prod = over("prod", "actl", 0, [P, 2, D])
        relb = over("relb", "gs", 0, [BUCKETS, NSAMP, MH])
        of_strip = over("of_strip", "gs", 512, [BUCKETS, STRIP + 1])
        rows = over("rows", "gs", 2048, [MH, STRIP + 1])
        of_past = over("of_past", "sqsum", 0, [BUCKETS, SEQ + 1])
        sc = over("sc", "sq", 0, [P, NPAGES, P])
        logit = over("logit", "tbuf", 0, [P, 2, 2, 3 * P])
        prob_t = over("prob_t", "xl", 0, [P, 2, 2, 3 * P])
        slog = over("slog", "xl", 6144, [P, SEQ + 1])
        sbias = over("sbias", "xl", 7200, [P, SEQ + 1])
        ext = over("ext", "xh", 0, [P, D])
        new_qk = over("new_qk", "xh", 4096, [P, DC, NSAMP])
        new_z = over("new_z", "xh", 4352, [P, NSAMP, DC, 2])
        new_own = over("new_own", "xh", 4864, [P, NSAMP])
        new_p = over("new_p", "xh", 4896, [NSAMP, P])
        sp_tok = over("sp_tok", "xh", 5408, [P, NPAGES, NSAMP, 2 * MH])
        scratch = nc.dram_tensor("bias_by_distance", [MH, STRIP + 1], F32)
        q_scratch = nc.dram_tensor("sample_queries", [NSAMP, D], F32)

        raw_landed = [sem(f"raw_landed{s}") for s in range(SLOTS)]
        w_hi = sem("w_hi")
        w_lo = sem("w_lo")
        mm_done = sem("mm_done")
        tile_made = sem("tile_made")
        bank_read = sem("bank_read")
        gained = sem("gained")
        xh_done = sem("xh_done")
        xl_done = sem("xl_done")
        sq_done = sem("sq_done")
        ss_done = sem("ss_done")
        rms_done = sem("rms_done")
        rinv_done = sem("rinv_done")
        func_done = sem("func_done")
        turned = sem("turned")
        unturned = sem("unturned")
        gs_done = sem("gs_done")
        a_done = sem("a_done")
        ah_done = sem("ah_done")
        al_done = sem("al_done")
        in_landed = sem("in_landed")
        cols_landed = sem("cols_landed")
        const_landed = sem("const_landed")
        gate_landed = sem("gate_landed")
        table_landed = sem("table_landed")
        ones_done = sem("ones_done")
        cols_turned = sem("cols_turned")
        cols_done = sem("cols_done")
        ln_landed = sem("ln_landed")
        ws_landed = sem("ws_landed")
        w00_landed = sem("w00_landed")
        ws_masked = sem("ws_masked")
        ws_turned = sem("ws_turned")
        ws_ready = sem("ws_ready")
        ws_bias_landed = sem("ws_bias_landed")
        ws_bias_done = sem("ws_bias_done")
        diag_done = sem("diag_done")
        stats_done = sem("stats_done")
        moments_done = sem("moments_done")
        lnstd_done = sem("lnstd_done")
        lninv_done = sem("lninv_done")
        lnshift_done = sem("lnshift_done")
        ln_scaled = sem("ln_scaled")
        lnormed = sem("lnormed")
        samples_normed = sem("samples_normed")
        stored = sem("stored")
        state_landed = sem("state_landed")
        state_stored = sem("state_stored")
        mask_landed = sem("mask_landed")
        keys_landed = [sem(f"keys_landed{s}") for s in range(PAGE_SLOTS)]
        values_landed = [sem(f"values_landed{s}") for s in range(PAGE_SLOTS)]
        bias_landed = sem("bias_landed")
        q_landed = [sem(f"q_landed{b}") for b in range(2)]
        scratch_landed = sem("scratch_landed")
        strip_landed = sem("strip_landed")
        fsq_done = sem("fsq_done")
        fstd_done = sem("fstd_done")
        finv_done = sem("finv_done")
        y_done = sem("y_done")
        fin_landed = sem("fin_landed")

        STORES = []

        def store(eng, out, src):
            eng.dma_start(out, src).then_inc(stored, 16)
            STORES.append(1)

        def pieces_of(name):
            kind, layer = name
            j = layer // 3

            def by_chunk(w):
                return w.rearrange("(c p) n -> p c n", p=P)

            if kind == "up":
                w = by_chunk(A["w_up"][layer])
                return [(w, 0, KC, t * DFF) for t in range(2)], PW, FC // 2
            if kind == "in":
                w = by_chunk(A[("w_in_a", "w_in_b", "w_in_c")[layer % 3]][j])
                return [(w, 0, KC, t * PW) for t in range(2)], 2 * PW, 12 if layer % 3 == 0 else 6
            if kind == "out" and layer % 3:
                w = by_chunk(A[("", "w_out_b", "w_out_c")[layer % 3]][j])
                return [(w, 0, KC, t * PW) for t in range(2)], 2 * PW, 2
            w = by_chunk(A["w_out_a"][j] if kind == "out" else A["w_down"][layer])
            depth = HC if kind == "out" else FC
            return [(w, c, min(KC, depth - c), t * PW) for t in range(2)
                    for c in range(0, depth, KC)], 2 * PW, 2

        def stream(sp, name):
            pieces, step, n = pieces_of(name)
            base, per = ph[name]["piece"], len(pieces)

            def body(i, shift):
                for t, (w, c, k, col) in enumerate(pieces):
                    need(sp, w_lo, 2 * per * i + 2 * (base + t - SLOTS + 1))
                    at = i * step + (col + shift)
                    columns = slice(at, at + PW) if isinstance(at, int) else bass.ds(at, PW)
                    sp.dma_start(raw[:, t % SLOTS, 0:k, :], w[:, c:c + k, columns])\
                        .then_inc(raw_landed[t % SLOTS], 16)

            if name == ("out", 2):
                body(0, 0)
                sp_pages(sp)
                body(1, 0)
            elif name[0] == "in" and name[1] % 3 == 0:
                run_loop(sp, 0, n // 2, lambda i, f: body(i, HALF), peel=base == 0)
                run_loop(sp, n // 2, n, lambda i, f: body(i, -HALF))
            else:
                run_loop(sp, 0, n, lambda i, f: body(i, 0))

        def split_hi(act, landed, used, slot, half, k):
            act.wait_ge(raw_landed[slot], landed)
            need(act, mm_done, used)
            side = slice(half * P, half * P + P)
            act.activation(whi[:, slot, 0:k, side], raw[:, slot, 0:k, side], ACT.Copy)\
                .then_inc(w_hi, 1)

        def split_lo(dve, number, slot, half, k):
            dve.wait_ge(w_hi, number)
            side = slice(half * P, half * P + P)
            dve.tensor_tensor(wlo[:, slot, 0:k, side], raw[:, slot, 0:k, side],
                              whi[:, slot, 0:k, side].bitcast(F32), ALU.subtract)\
                .then_inc(w_lo, 1)

        def split_next(eng, name, i, t, half, last=False):
            pieces, base = pieces_of(name)[0], ph[name]["piece"]
            per = len(pieces)
            if last and t + SLOTS >= per:
                return
            k = pieces[t + SLOTS][2] if t + SLOTS < per else KC
            at = base + t
            number = 2 * per * i + (2 * (at + SLOTS) + half + 1)
            if eng is nc.vector:
                split_lo(eng, number, t % SLOTS, half, k)
            else:
                landed = i * (16 * per // SLOTS) + 16 * (at // SLOTS + 2)
                split_hi(eng, landed, 2 * per * i + (2 * at + half + 1), t % SLOTS, half, k)

        def tile_mms(pe, bank, slot, half, chunks, rh, rl, c0, depth):
            side = slice(half * P, half * P + P)
            for c in chunks:
                pe.matmul(bank[:, 0:TOK], whi[:, slot, c, side], rh[:, c0 + c, :],
                          start=(c0 + c == 0), stop=False)
                pe.matmul(bank[:, 0:TOK], whi[:, slot, c, side], rl[:, c0 + c, :],
                          start=False, stop=False)
                mm = pe.matmul(bank[:, 0:TOK], wlo[:, slot, c, side], rh[:, c0 + c, :],
                               start=False, stop=(c0 + c == depth - 1))
            return mm

        def sum_squares(pe, norm):
            pe.wait_ge(sq_done, SQ_STEPS * (norm + 1))
            need(pe, rms_done, norm)
            pe.matmul(SS[:, 0:TOK], ones[:, 0:P], sqsum[:, :], start=True, stop=True)\
                .then_inc(ss_done, 1)

        def turn_tile(pe, turn, func, j):
            pe.wait_ge(func_done, func + 1)
            need(pe, unturned, 2 * (turn - 1))
            out = TURN[j % 2]
            for b in range(NBLK):
                pe.transpose(out[:, b * P:(b + 1) * P], gbuf[:, j, b * P:(b + 1) * P], ident[:, :])
            pe.transpose(out[0:NSAMP, SEQ:SEQ + P], gbuf[:, j, SEQ:TOK], ident[:, :])\
                .then_inc(turned, 1)

        def pe_project(pe, name, start, end, turns_from=None, new_norm=None):
            at = ph[name]
            p0, t0 = at["piece"], at["tile"]

            def turn(i, j):
                step = i + (-turns_from)
                q = 4 * step + (at["turn"] + j)
                f = 4 * i + (at["func"] + j) if name[1] % 3 != 1 else 4 * step + (at["func"] + j)
                turn_tile(pe, q, f, j % BANKS)

            def body(i, first):
                for t in range(2):
                    for half in range(2):
                        pe.wait_ge(w_lo, 4 * i + (2 * (p0 + t) + half + 1))
                        j = 2 * t + half
                        need(pe, bank_read, t0 + 4 * i + j - BANKS + 1)
                        if first and new_norm is not None and j == 0:
                            for c in range(DC):
                                pe.wait_ge(xl_done, DC * new_norm + c + 1)
                                mm = tile_mms(pe, ps[j], t, half, [c], xh, xl, 0, DC)
                        else:
                            mm = tile_mms(pe, ps[j], t, half, range(KC), xh, xl, 0, DC)
                        mm.then_inc(mm_done, 1)
                        if first and new_norm is not None and j == 0:
                            sum_squares(pe, new_norm)
                        if turns_from is not None and not (first and j == 0):
                            turn(i, j - 1)

            run_loop(pe, start, end, body, peel=turns_from is not None or new_norm is not None)
            if turns_from is not None:
                turn(end - 1, BANKS - 1)

        def pe_out(pe, name):
            at = ph[name]
            pieces, _, steps = pieces_of(name)
            per = len(pieces)
            depth = sum(k for _, _, k, _ in pieces) // 2
            acts = ph[("mix", name[1])] if name[0] == "out" else ph[("up", name[1])]

            def body(i, first):
                for t, (_, c0, k, _) in enumerate(pieces):
                    panel = t // (per // 2)
                    for half in range(2):
                        pe.wait_ge(w_lo, 2 * per * i + (2 * (at["piece"] + t) + half + 1))
                        j = 2 * panel + half
                        if c0 == 0:
                            need(pe, bank_read, at["tile"] + 4 * i + j - BANKS + 1)
                        if first and panel == 0 and half == 0:
                            for c in range(k):
                                pe.wait_ge(al_done, acts["act"] + c0 + c + 1)
                                mm = tile_mms(pe, ps[j], t % SLOTS, half, [c], acth, actl, c0, depth)
                        else:
                            mm = tile_mms(pe, ps[j], t % SLOTS, half, range(k), acth, actl, c0, depth)
                        mm.then_inc(mm_done, 1)

            run_loop(pe, 0, steps, body, peel=True)

        def mm_value(name, i, j):
            pieces = pieces_of(name)[0]
            per, p0 = len(pieces), ph[name]["piece"]
            each = per // 2
            return 2 * per * i + (2 * p0 + 2 * each * (j // 2) + 2 * (each - 1) + j % 2 + 1)

        def new_chunk_vector(dve, norm, gain, m, j, tile, tile_wait, add):
            dve.wait_ge(*tile_wait)
            if add:
                dve.tensor_tensor(chunk(x, m), chunk(x, m), ps[j % BANKS][:, 0:TOK],
                                  ALU.add).then_inc(bank_read, 1)
            else:
                dve.tensor_copy(chunk(x, m), ps[j % BANKS][:, 0:TOK]).then_inc(bank_read, 1)
            if norm is None:
                return
            need(dve, xl_done, DC * norm + m - 1)
            dve.wait_ge(bank_read, tile + 1)
            dve.tensor_scalar(xg[:, j % 2, :], chunk(x, m),
                              cols[:, one(m + gain)], None, ALU.mult).then_inc(gained, 1)

        def new_chunk_lo(dve, norm, m, j):
            dve.wait_ge(xh_done, DC * norm + m + 1)
            dve.tensor_tensor(chunk(xl, m), xg[:, j % 2, :],
                              chunk(xh, m).bitcast(F32), ALU.subtract).then_inc(xl_done, 1)

        def new_chunk_scalar(act, norm, m, j):
            act.wait_ge(gained, DC * norm + m + 1)
            act.activation(chunk(xh, m), xg[:, j % 2, :], ACT.Copy)\
                .then_inc(xh_done, 1)

        def gain_of(name):
            if name == "load":
                return 0
            kind, layer = name
            return DC * (DEPTH + layer) if kind == "out" else DC * (layer + 1)

        def has_norm(name):
            return name != ("down", DEPTH - 1)

        def vector_out(dve, name):
            at = ph[name]
            per = len(pieces_of(name)[0])
            norm = at["norm"] if has_norm(name) else None

            def body(i, last):
                for t in range(per):
                    for half in range(2):
                        whole = t % (per // 2) == per // 2 - 1
                        j = 2 * (t // (per // 2)) + half
                        if whole:
                            new_chunk_vector(dve, norm, gain_of(name), 4 * i + j, j,
                                             at["tile"] + 4 * i + j,
                                             (mm_done, mm_value(name, i, j)), True)
                        if half == 0:
                            split_next(dve, name, i, t, half, last)
                        if whole and norm is not None:
                            new_chunk_lo(dve, norm, 4 * i + j, j)
                        if half == 1:
                            split_next(dve, name, i, t, half, last)

            if norm is None:
                body(0, False)
                body(1, True)
            else:
                run_loop(dve, 0, 2, lambda i, f: body(i, False))

        def scalar_out(act, name):
            at = ph[name]
            per = len(pieces_of(name)[0])

            def body(i, last):
                for t in range(per):
                    for half in range(2):
                        if half == 0:
                            split_next(act, name, i, t, half, last)
                        if has_norm(name) and t % (per // 2) == per // 2 - 1:
                            j = 2 * (t // (per // 2)) + half
                            new_chunk_scalar(act, at["norm"], 4 * i + j, j)
                        if half == 1:
                            split_next(act, name, i, t, half, last)

            if not has_norm(name):
                body(0, False)
                body(1, True)
            else:
                run_loop(act, 0, 2, lambda i, f: body(i, False))

        def pool_squares(pool, name):
            at = ph[name]
            norm = at["norm"]
            base = SQ_STEPS * norm
            need(pool, ss_done, norm)
            pool.memset(sqsum[:, :], 0.0).then_inc(sq_done, 1)
            for_tiles = at["tile"]

            def body(m, first):
                pool.wait_ge(bank_read, m + (for_tiles + 1))
                pool.tensor_tensor(sq[:, :], chunk(x, m), chunk(x, m), ALU.mult)\
                    .then_inc(sq_done, 1)
                pool.wait_ge(sq_done, 2 * m + (base + 2))
                pool.tensor_tensor(sqsum[:, :], sqsum[:, :], sq[:, :], ALU.add).then_inc(sq_done, 1)
                pool.wait_ge(sq_done, 2 * m + (base + 3))

            run_loop(pool, 0, DC, body)

        def scalar_rms(act, norm):
            act.wait_ge(ss_done, norm + 1)
            need(act, rinv_done, norm)
            act.activation(rms[:, :], SS[:, 0:TOK], ACT.Sqrt, scale=1.0 / D, bias=eps[:, :])\
                .then_inc(rms_done, 1)

        def vector_rinv(dve, norm):
            dve.wait_ge(rms_done, norm + 1)
            dve.reciprocal(rinv[:, :], rms[:, :]).then_inc(rinv_done, 1)
            dve.wait_ge(rinv_done, norm + 1)

        def vector_up(dve, layer):
            name = ("up", layer)
            at = ph[name]
            f0, a0, g0 = at["func"], at["act"], FC * layer

            def act_lo(i, j):
                dve.wait_ge(ah_done, a0 + 2 * i + j + 1)
                dve.tensor_tensor(chunk(actl, 2 * i + j), abuf[:, j, :],
                                  chunk(acth, 2 * i + j).bitcast(F32), ALU.subtract)\
                    .then_inc(al_done, 1)

            def body(i, first):
                if first:
                    vector_rinv(dve, at["norm"] - 1)
                for j in range(2):
                    need(dve, func_done, f0 + 2 * i + j - 1)
                    dve.wait_ge(mm_done, mm_value(name, i, j))
                    dve.tensor_tensor(tbuf[:, j, :], ps[j][:, 0:TOK], rinv[:, :], ALU.mult)\
                        .then_inc(bank_read, 1)
                    split_next(dve, name, i, 0, j)
                for j in range(2):
                    dve.wait_ge(func_done, f0 + 2 * i + j + 1)
                    dve.tensor_tensor(gs[:, j, :], gbuf[:, j, :], rinv[:, :], ALU.mult)\
                        .then_inc(gs_done, 1)
                for j in range(2):
                    dve.wait_ge(gs_done, g0 + 2 * i + j + 1)
                    dve.wait_ge(mm_done, mm_value(name, i, 2 + j))
                    need(dve, al_done, a0 + 2 * i + j - 1)
                    dve.tensor_tensor(abuf[:, j, :], ps[2 + j][:, 0:TOK], gs[:, j, :], ALU.mult)\
                        .then_inc(bank_read, 1)
                    if j == 1:
                        act_lo(i, 0)
                    split_next(dve, name, i, 1, j)
                act_lo(i, 1)

            run_loop(dve, 0, FC // 2, body, peel=True)

        def scalar_up(act, layer):
            name = ("up", layer)
            at = ph[name]
            t0, a0, g0 = at["tile"], at["act"], FC * layer

            def body(i, first):
                if first:
                    scalar_rms(act, at["norm"] - 1)
                for j in range(2):
                    split_next(act, name, i, 0, j)
                    act.wait_ge(bank_read, t0 + 4 * i + j + 1)
                    if not first:
                        act.wait_ge(gs_done, g0 + 2 * i + j - 1)
                    act.activation(gbuf[:, j, :], tbuf[:, j, :], ACT.Silu).then_inc(func_done, 1)
                for j in range(2):
                    split_next(act, name, i, 1, j)
                    act.wait_ge(bank_read, t0 + 4 * i + 2 + j + 1)
                    act.activation(chunk(acth, 2 * i + j), abuf[:, j, :], ACT.Copy)\
                        .then_inc(ah_done, 1)

            run_loop(act, 0, FC // 2, body, peel=True)

        def pool_setup(pool):
            pool.dma_start(xin[:, 0:NBLK, :], A["x_prompt"][0].rearrange("(b p) d -> p b d", p=P))\
                .then_inc(in_landed, 16)
            pool.dma_start(xin[0:NSAMP, NBLK, :], A["x_sample"].rearrange("b s d -> (b s) d"))\
                .then_inc(in_landed, 16)
            for src, row in (("norm_mix", 0), ("norm_ffn", 32), ("b_gate_b", 64), ("gn_b", 68)):
                flat = A[src].rearrange("a (c p) -> (a c) p", p=P)
                pool.dma_start(col_rows[row:row + flat.shape[0], :], flat).then_inc(cols_landed, 16)
            pool.dma_start(w_rank[:, :, :], A["w_in_b"][0].rearrange("(c p) n -> p c n", p=P)
                           [:, :, GLA_PROJ - RANK:GLA_PROJ]).then_inc(gate_landed, 16)
            pool.dma_start(w_gate[:, :], A["w_gate_b"][0]).then_inc(gate_landed, 16)

        def scalar_setup(act):
            act.dma_start(ident[:, :], A["c_ident"]).then_inc(const_landed, 16)
            act.dma_start(halves[:, :], A["c_halves"]).then_inc(const_landed, 16)
            act.dma_start(own[:, :], A["c_own"]).then_inc(const_landed, 16)
            act.dma_start(head_of[:, :], A["c_head_of"]).then_inc(const_landed, 16)
            act.dma_start(table[:, :], A["page_table"].rearrange("(o b) n -> o (b n)", o=1))\
                .then_inc(table_landed, 16)

        def pe_load(pe):
            pe.wait_ge(const_landed, 64)
            pe.wait_ge(cols_landed, 64)
            pe.transpose(TURN[0][:, 0:70], col_rows[:, :], ident[0:70, 0:70]).then_inc(cols_turned, 1)
            pe.wait_ge(in_landed, 32)
            for m in range(DC):
                need(pe, bank_read, m - BANKS + 1)
                bank = ps[m % BANKS]
                for b in range(NBLK):
                    pe.transpose(bank[:, b * P:(b + 1) * P], xin[:, b, m * P:(m + 1) * P], ident[:, :])
                pe.transpose(bank[:, SEQ:TOK], xin[0:NSAMP, NBLK, m * P:(m + 1) * P],
                             ident[0:NSAMP, 0:NSAMP]).then_inc(tile_made, 1)

        def vector_load(dve):
            dve.memset(eps[:, :], EPS).then_inc(ones_done, 1)
            dve.memset(ones[:, :], 1.0).then_inc(ones_done, 1)
            dve.wait_ge(cols_turned, 1)
            dve.tensor_copy(cols[:, :], TURN[0][:, 0:70]).then_inc(cols_done, 1)
            dve.wait_ge(cols_done, 1)
            for number in range(2 * SLOTS):
                split_lo(dve, number + 1, number // 2, number % 2, KC)
            for m in range(DC):
                new_chunk_vector(dve, 0, 0, m, m, m, (tile_made, m + 1), False)
                if m:
                    new_chunk_lo(dve, 0, m - 1, m - 1)
            new_chunk_lo(dve, 0, DC - 1, DC - 1)

        def scalar_load(act):
            for number in range(2 * SLOTS):
                split_hi(act, 16, 0, number // 2, number % 2, KC)
            for m in range(DC):
                new_chunk_scalar(act, 0, m, m)

        def vector_in(dve, name, start, end, whole=False, stats_of=None, norm_v=False,
                      sum_keys=False, first_of_phase=False):
            at = ph[name]

            def body(i, first):
                for t in range(2):
                    if first and first_of_phase and t == 0:
                        vector_rinv(dve, at["norm"] - 1)
                    for j in (2 * t, 2 * t + 1):
                        dve.wait_ge(mm_done, mm_value(name, i, j))
                        out = chunk(feat, 4 * i + j) if whole else tbuf[:, j, :]
                        if not whole:
                            need(dve, func_done, at["func"] + 4 * i + j - BANKS + 1)
                        dve.tensor_tensor(out, ps[j][:, 0:TOK], rinv[:, :], ALU.mult)\
                            .then_inc(bank_read, 1)
                        split_next(dve, name, i, t, j % 2)
                        if sum_keys:
                            at_b = MH * NPAGES * (i + (-start)) + MH * (j // 2)
                            vector_sum_keys(dve, SUMS * (i + (-start)) + j, j % 2,
                                            bass.ds(at_b, MH), j % NPAGES)
                    if stats_of is not None and t == 0 and not first:
                        vector_stats(dve, name, i + (-1))
                    if norm_v and t == 1:
                        vector_norm_v(dve, sgu_number(name[1]), i + (-start))

            run_loop(dve, start, end, body, peel=first_of_phase or stats_of is not None)
            if stats_of is not None:
                vector_stats(dve, name, end - 1)

        def vector_stats(dve, name, i):
            dve.wait_ge(unturned, 8 * i + (2 * ph[name]["turn"] + 8))
            for b in range(NBLK + 1):
                src = vt[:, b, cut(i, 4 * P)] if b < NBLK else vts[:, cut(i, 4 * P)]
                n = P if b < NBLK else NSAMP
                dve.bn_stats(stats[0:n, b, one(i), :].rearrange("p a s -> p (a s)"), src)\
                    .then_inc(stats_done, 1)

        def scalar_in(act, name, start, end, func, turns=False, into_feat=None, reads_feat=False,
                      norm_v=False, first_of_phase=False):
            at = ph[name]
            partial = name[1] % 3 == 1

            def finish_turn(i, j):
                step = i + (-start)
                q = 4 * step + (at["turn"] + j)
                act.wait_ge(turned, q + 1)
                m = 4 * step + j
                if partial:
                    prompts, samples = v_tok, vs_tok
                else:
                    prompts, samples = vt, vts
                bank = TURN[j % 2]
                act.activation(prompts[:, :, cut(m, P)],
                               bank[:, 0:SEQ].rearrange("p (b t) -> p b t", b=NBLK), ACT.Copy)\
                    .then_inc(unturned, 1)
                act.activation(samples[:, cut(m, P)], bank[0:NSAMP, SEQ:SEQ + P], ACT.Copy)\
                    .then_inc(unturned, 1)

            def body(i, first):
                for t in range(2):
                    if first and first_of_phase and t == 0:
                        scalar_rms(act, at["norm"] - 1)
                    for j in (2 * t, 2 * t + 1):
                        split_next(act, name, i, t, j % 2)
                        if func is None:
                            continue
                        act.wait_ge(bank_read, at["tile"] + 4 * i + j + 1)
                        src = chunk(feat, 4 * i + j) if reads_feat else tbuf[:, j, :]
                        if turns:
                            need(act, turned, 4 * (i + (-start)) + (at["turn"] + j - BANKS + 1))
                            out = gbuf[:, j, :]
                        else:
                            out = chunk(feat, 4 * i + (j + into_feat))
                        act.activation(out, src, func).then_inc(func_done, 1)
                        if turns and not (first and j == 0):
                            finish_turn(i, j - 1)
                    if norm_v and t == 0:
                        scalar_norm_v(act, i + (-start))

            if turns and name[1]:
                act.wait_ge(stored, 16 * (0, 1, 2, 6)[name[1]])
            run_loop(act, start, end, body, peel=turns or first_of_phase)
            if turns:
                finish_turn(end - 1, BANKS - 1)

        def sgu_number(layer):
            return layer // 3

        def pool_sgu(pool, layer):
            s = sgu_number(layer)
            at = ph[("in", layer)]
            need(pool, tile_made, 1) if layer == 0 else pool.wait_ge(mm_done, 2 * at["piece"])
            pool.dma_start(ln_gain[:, :], A["ln_a_g"][s:s + 1, :].broadcast_to([P, HALF]))\
                .then_inc(ln_landed, 16)
            pool.dma_start(ln_bias[:, :], A["ln_a_b"][s:s + 1, :].broadcast_to([P, HALF]))\
                .then_inc(ln_landed, 16)
            pool.dma_start(ws_nat[:, :, :], A["w_s_a"][s].rearrange("g i j -> i g j"))\
                .then_inc(ws_landed, 16)
            if s:
                pool.wait_ge(diag_done, s)
            pool.dma_start(w00[:, :], A["w_s_a"][s].rearrange("g i j -> (i j) g")[0:1, :]
                           .broadcast_to([NSAMP, GROUPS]), allow_slow_non_contiguous=True)\
                .then_inc(w00_landed, 16)
            pool.wait_ge(ws_landed, 16 * (s + 1))
            pool.affine_select(out=ws_nat[:, :, :], in_=ws_nat[:, :, :], compare_op=ALU.is_ge,
                               fill=0.0, base=0, pattern=[[0, GROUPS], [-1, P]],
                               channel_multiplier=1).then_inc(ws_masked, 1)
            pool.wait_ge(ln_landed, 32 * (s + 1))
            pool.wait_ge(lnshift_done, (NBLK + 1) * (s + 1))
            v, n = vts[:, :], 3 * s
            pool.tensor_scalar(v, v, moments[0:NSAMP, NBLK, 0:1], lninv[0:NSAMP, NBLK:NBLK + 1],
                               ALU.subtract, ALU.mult).then_inc(samples_normed, 1)
            pool.wait_ge(samples_normed, n + 1)
            pool.tensor_tensor(v, v, ln_gain[0:NSAMP, :], ALU.mult).then_inc(samples_normed, 1)
            pool.wait_ge(samples_normed, n + 2)
            pool.tensor_tensor(v, v, ln_bias[0:NSAMP, :], ALU.add).then_inc(samples_normed, 1)
            pool.wait_ge(samples_normed, n + 3)
            store(pool, A["sgu_v_sample"][s].rearrange("b o d -> (b o) d"), vts[:, :])
            pool.wait_ge(mm_done, 2 * (at["piece"] + HC))
            b_s = A["b_s_a"][s:s + 1]
            for b in range(NBLK):
                pool.dma_start(ws_bias[:, :, b * P:(b + 1) * P], b_s).then_inc(ws_bias_landed, 16)
            pool.wait_ge(ws_bias_landed, 32 * (s + 1))
            pool.tensor_copy(ws_bias[:, :, SEQ:TOK], ws_bias[:, :, 0:1]
                             .broadcast_to([1, GROUPS, NSAMP])).then_inc(ws_bias_done, 1)

        def vector_moments(dve, layer):
            s = sgu_number(layer)
            dve.wait_ge(stats_done, 6 * (NBLK + 1) * (s + 1))
            for b in range(NBLK + 1):
                n = P if b < NBLK else NSAMP
                dve.bn_aggr(moments[0:n, b, :], stats[0:n, b, :, :].rearrange("p a s -> p (a s)"))\
                    .then_inc(moments_done, 1)
            for b in range(NBLK + 1):
                n = P if b < NBLK else NSAMP
                dve.wait_ge(lnstd_done, (NBLK + 1) * s + b + 1)
                dve.reciprocal(lninv[0:n, b:b + 1], lnstd[0:n, b:b + 1]).then_inc(lninv_done, 1)
            for b in range(NBLK + 1):
                n = P if b < NBLK else NSAMP
                dve.wait_ge(lninv_done, (NBLK + 1) * s + b + 1)
                dve.scalar_tensor_tensor(out=lnshift[0:n, b:b + 1], in0=moments[0:n, b, 0:1],
                                         scalar=-1.0, in1=lninv[0:n, b:b + 1], op0=ALU.mult,
                                         op1=ALU.mult).then_inc(lnshift_done, 1)
            dve.wait_ge(ln_landed, 32 * (s + 1))

        def scalar_norm_v(act, step):
            for b in range(NBLK):
                v = vt[:, b, cut(step, 4 * P)]
                act.activation(v, v, ACT.Identity, scale=lninv[:, b:b + 1],
                               bias=lnshift[:, b:b + 1]).then_inc(ln_scaled, 1)

        def vector_norm_v(dve, s, step):
            v, side = vt[:, :, cut(step, 4 * P)], cut(step, 4 * P)
            dve.wait_ge(ln_scaled, 2 * step + (HC // 2 * s + 2))
            for n, (row, op) in enumerate(((ln_gain, ALU.mult), (ln_bias, ALU.add))):
                if n:
                    dve.wait_ge(lnormed, 2 * step + (HC // 2 * s + 1))
                dve.tensor_tensor(v, v, row[:, side].unsqueeze(1).broadcast_to([P, NBLK, 4 * P]), op)\
                    .then_inc(lnormed, 1)

        def scalar_lnstd(act, layer):
            s = sgu_number(layer)
            for b in range(NBLK + 1):
                n = P if b < NBLK else NSAMP
                act.wait_ge(moments_done, (NBLK + 1) * s + b + 1)
                act.activation(lnstd[0:n, b:b + 1], moments[0:n, b, 1:2], ACT.Sqrt, scale=1.0,
                               bias=eps[0:n, :]).then_inc(lnstd_done, 1)
            act.wait_ge(lnshift_done, (NBLK + 1) * (s + 1))
            act.wait_ge(unturned, 2 * (ph[("in", layer)]["turn"] + HC))

        def pe_sgu(pe, layer):
            s = sgu_number(layer)
            at = ph[("mix", layer)]
            pe.wait_ge(ws_masked, s + 1)
            for g in range(GROUPS):
                pe.transpose(TURN[g // 4][:, (g % 4) * P:(g % 4 + 1) * P], ws_nat[:, g, :],
                             ident[:, :]).then_inc(ws_turned, 1)
            pe.wait_ge(ws_ready, 2 * (s + 1))
            pe.wait_ge(ws_bias_done, s + 1)
            pe.wait_ge(diag_done, s + 1)
            pe.wait_ge(lnormed, HC // 2 * (s + 1))
            pe.wait_ge(samples_normed, 3 * (s + 1))
            for c in range(HC):
                g = c // GC
                bank = ps[c % BANKS]
                side = slice(c * P, (c + 1) * P)
                need(pe, bank_read, at["tile"] + c - BANKS + 1)
                pe.matmul(bank[:, 0:TOK], ones[0:1, 0:P], ws_bias[0:1, g, :], start=True, stop=False,
                          skip_group_check=True)
                for b in range(NBLK):
                    pe.matmul(bank[:, b * P:(b + 1) * P], vt[:, b, side], ws_t[:, g, :],
                              start=False, stop=False, skip_group_check=True)
                pe.matmul(bank[:, SEQ:TOK], vts[:, side], ws_diag[:, g, :], start=False, stop=True,
                          skip_group_check=True).then_inc(tile_made, 1)

        def made_before(layer):
            return DC + HC * (layer // 3)

        def vector_sgu(dve, layer):
            s = sgu_number(layer)
            at = ph[("mix", layer)]
            dve.wait_ge(w00_landed, 16 * (s + 1))
            dve.tensor_tensor(ws_diag[:, :, :],
                              ident[0:NSAMP, 0:NSAMP].unsqueeze(1).broadcast_to([NSAMP, GROUPS, NSAMP]),
                              w00[:, :].unsqueeze(2).broadcast_to([NSAMP, GROUPS, NSAMP]), ALU.mult)\
                .then_inc(diag_done, 1)
            dve.wait_ge(func_done, ph[("in", layer)]["func"] + 2 * HC)

            def body(i, first):
                for j in range(BANKS):
                    dve.wait_ge(tile_made, made_before(layer) + 4 * i + j + 1)
                    need(dve, al_done, at["act"] + 4 * i + j - 1)
                    dve.tensor_tensor(abuf[:, j % 2, :], ps[j][:, 0:TOK], chunk(feat, 4 * i + j),
                                      ALU.mult).then_inc(bank_read, 1)
                    if j % 2:
                        for e in (j - 1, j):
                            dve.wait_ge(ah_done, at["act"] + 4 * i + e + 1)
                            dve.tensor_tensor(chunk(actl, 4 * i + e), abuf[:, e % 2, :],
                                              chunk(acth, 4 * i + e).bitcast(F32), ALU.subtract)\
                                .then_inc(al_done, 1)

            run_loop(dve, 0, HC // BANKS, body, peel=at["act"] == 0)

        def scalar_sgu(act, layer):
            s = sgu_number(layer)
            at = ph[("mix", layer)]
            for h in range(2):
                act.wait_ge(ws_turned, GROUPS * s + 4 * (h + 1))
                act.activation(ws_t[:, 4 * h:4 * h + 4, :],
                               TURN[h][:, :].rearrange("p (g t) -> p g t", g=4), ACT.Copy)\
                    .then_inc(ws_ready, 1)
            act.wait_ge(lnormed, HC // 2 * (s + 1))
            act.wait_ge(samples_normed, 3 * (s + 1))

            def body(i, first):
                for j in range(BANKS):
                    act.wait_ge(bank_read, at["tile"] + 4 * i + j + 1)
                    act.activation(chunk(acth, 4 * i + j), abuf[:, j % 2, :], ACT.Copy)\
                        .then_inc(ah_done, 1)

            run_loop(act, 0, HC // BANKS, body)

        def pe_final(pe):
            at = ph["final"]["tile"]
            for m in range(DC):
                pe.wait_ge(bank_read, at + m - BANKS + 1)
                pe.wait_ge(bank_read, ph[("down", DEPTH - 1)]["tile"] + m + 1)
                bank = ps[m % BANKS]
                for b in range(NBLK):
                    pe.transpose(bank[:, b * P:(b + 1) * P], x[:, m, b * P:(b + 1) * P], ident[:, :])
                pe.transpose(bank[0:NSAMP, SEQ:SEQ + P], x[:, m, SEQ:TOK], ident[:, :])\
                    .then_inc(tile_made, 1)

        def vector_final(dve):
            base = made_before(DEPTH - 1) + HC
            for m in range(DC):
                dve.wait_ge(tile_made, base + m + 1)
                bank = ps[m % BANKS]
                side = slice(m * P, (m + 1) * P)
                dve.tensor_copy(ytok[0:NSAMP, NBLK, side], bank[0:NSAMP, SEQ:SEQ + P])\
                    .then_inc(y_done, 1)
                dve.tensor_copy(ytok[:, 0:NBLK, side],
                                bank[:, 0:SEQ].rearrange("p (b t) -> p b t", b=NBLK))\
                    .then_inc(bank_read, 1)
            dve.wait_ge(y_done, DC)
            dve.wait_ge(bank_read, ph["final"]["tile"] + DC)
            for b in range(NBLK + 1):
                n = P if b < NBLK else NSAMP
                dve.wait_ge(fstd_done, b + 1)
                dve.reciprocal(small[0:n, 8 + b:9 + b], small[0:n, 4 + b:5 + b]).then_inc(finv_done, 1)
            dve.wait_ge(fin_landed, 16)
            for b in range(NBLK + 1):
                n = P if b < NBLK else NSAMP
                dve.wait_ge(finv_done, b + 1)
                dve.wait_ge(fsq_done, b + 1)
                dve.scalar_tensor_tensor(out=yout[0:n, b, :], in0=ytok[0:n, b, :],
                                         scalar=small[0:n, 8 + b:9 + b], in1=gain_fin[0:n, :],
                                         op0=ALU.mult, op1=ALU.mult).then_inc(y_done, 1)

        def scalar_final(act):
            act.wait_ge(bank_read, ph["final"]["tile"] + DC)
            act.wait_ge(y_done, DC)
            for b in range(NBLK + 1):
                n = P if b < NBLK else NSAMP
                act.activation(yout[0:n, b, :], ytok[0:n, b, :], ACT.Square,
                               accum_out=small[0:n, b:b + 1]).then_inc(fsq_done, 1)
            for b in range(NBLK + 1):
                n = P if b < NBLK else NSAMP
                act.wait_ge(fsq_done, b + 1)
                act.activation(small[0:n, 4 + b:5 + b], small[0:n, b:b + 1], ACT.Sqrt,
                               scale=1.0 / D, bias=eps[0:n, :]).then_inc(fstd_done, 1)

        def pool_final(pool):
            pool.wait_ge(y_done, DC + NBLK)
            store(pool, A["y_prompt"][0].rearrange("(b p) d -> p b d", p=P), yout[:, 0:NBLK, :])
            pool.wait_ge(y_done, DC + NBLK + 1)
            store(pool, A["y_sample"].rearrange("b s d -> (b s) d"), yout[0:NSAMP, NBLK, :])

        G0 = ph[("mix", 1)]
        inner = range(1, len(LEVELS))
        V_NAMES = (["onehot", "gl"] + [f"z{h}" for h in range(GH)] + ["minz", "loga"]
                   + [f"cum{h}" for h in range(GH)] + ["att0", "cpd0", "cpd1", "qf0"]
                   + [n for lv in inner for n in ([f"qf{lv}"] + (["cp0_0"] if lv == 1 else
                                                                  [f"cp{lv - 1}_0", f"cp{lv - 1}_1"]))]
                   + [f"cp{inner[-1]}_{e}" for e in range(2)]
                   + [f"sn{b}_{h}" for b in range(NSAMP) for h in range(GH)]
                   + [f"o{i}" for i in range(DC)] + ["os", "hinv"]
                   + [f"og{i}" for i in range(DC)])
        S_NAMES = (["qs", "kc", "qss", "absz", "e", "ln", "ea", "edk", "kt0", "kt1"]
                   + [f"ed{lv}" for lv in range(len(LEVELS))] + ["sf0", "sf1"]
                   + [f"sm{b}_{h}" for b in range(NSAMP) for h in range(GH)] + ["silu"]
                   + [f"hstd{h}" for h in range(GH)])
        G_NAMES = (["qf0s", "kf0s", "dk", "kd"]
                   + [f"{n}{lv}" for lv in range(len(LEVELS)) for n in ("dl", "dr", "kf")] + ["osq"])
        T_NAMES = (["gl"] + [f"z{h}" for h in range(GH)] + ["dg", "kt0", "kt1"]
                   + [f"lv{lv}" for lv in range(len(LEVELS))] + ["st0", "st1"]
                   + [n for b in range(NSAMP) for n in (f"vb{b}", f"so{b}")]
                   + [f"o{i}" for i in range(DC)] + [f"hs{h}" for h in range(GH)])
        gla_v = Steps(sem("gla_vector"), V_NAMES)
        gla_s = Steps(sem("gla_scalar"), S_NAMES)
        gla_g = Steps(sem("gla_gpsimd"), G_NAMES)
        gla_t = Steps(sem("gla_tensor"), T_NAMES)

        def level_banks(lv):
            return [ps[1], ps[2]] if lv % 2 == 0 else [ps[3], ps[7]]

        def halves_of(t, m):
            return t[:, :, :].rearrange("p h (n e m) -> p (h n) e m", e=2, m=m)

        def pe_gla(pe):
            w = gla_v.wait
            pe.wait_ge(gate_landed, 32)
            pe.wait_ge(bank_read, G0["tile"])
            for c in range(DC):
                pe.matmul(ps[0][0:RANK, 0:TOK], w_rank[:, c, :], xh[:, c, :].bitcast(F32),
                          start=(c == 0), stop=False)
                mm = pe.matmul(ps[0][0:RANK, 0:TOK], w_rank[:, c, :], xl[:, c, :].bitcast(F32),
                               start=False, stop=(c == DC - 1))
            gla_t.did(mm, "gl")
            w(pe, "gl")
            for h in range(GH):
                gla_t.did(pe.matmul(ps[h][:, 0:TOK], w_gate[:, h * DK:(h + 1) * DK], gl[:, :],
                                    start=True, stop=True), f"z{h}")
            gla_s.wait(pe, "kc")
            w(pe, "z3")
            scores(pe, level_banks(0), kc, qc, "dg")
            gla_g.wait(pe, "kd")
            pe.wait_ge(unturned, 2 * (ph[("in", 1)]["turn"] + DC))
            for b in range(NBLK):
                for h in range(GH):
                    mm = pe.transpose(TURN[b][:, h * P:(h + 1) * P], kd[:, h, b * P:(b + 1) * P],
                                      ident[:, :])
                gla_t.did(mm, f"kt{b}")
            for lv in range(len(LEVELS)):
                w(pe, f"qf{lv}")
                gla_g.wait(pe, f"kf{lv}")
                if lv == 0:
                    for h in range(GH):
                        mm = pe.matmul(ps[0][:, h * P:(h + 1) * P], kf[:, h, 0:P], qf[:, h, P:SEQ],
                                       start=True, stop=True, skip_group_check=True)
                    gla_t.did(mm, "lv0")
                    continue
                if lv == 2:
                    w(pe, "cpd1")
                if lv > 2:
                    w(pe, f"cp{lv - 2}_1")
                scores(pe, level_banks(lv), kf, qf, f"lv{lv}")
            gla_s.wait(pe, "kt1")
            for h in range(GH):
                for b in range(NBLK):
                    mm = pe.matmul(TURN[h // 2][:, (h % 2) * DV:(h % 2 + 1) * DV],
                                   kd_tok[:, b, h * DK:(h + 1) * DK],
                                   v_tok[:, b, h * DV:(h + 1) * DV], start=(b == 0),
                                   stop=(b == NBLK - 1), skip_group_check=True)
                if h % 2:
                    gla_t.did(mm, f"st{h // 2}")
            w(pe, "onehot")
            w(pe, "cp0_0")
            for b in range(NSAMP):
                if b < 2:
                    w(pe, f"cp{inner[-1] - (inner[-1] + b) % 2}_1")
                else:
                    w(pe, f"sn{b - 2}_{GH - 1}")
                for e in range(2):
                    mm = pe.matmul(level_banks(b)[e][:, :], onehot[:, b, :],
                                   vs_tok[:, e * 512:(e + 1) * 512], start=True, stop=True)
                gla_t.did(mm, f"vb{b}")
                w(pe, f"sn{b}_{GH - 1}")
                gla_s.wait(pe, "qss")
                for i in range(DC):
                    h, e = i // 2, i % 2
                    mm = pe.matmul(ps[0][:, i * NSAMP + b:i * NSAMP + b + 1],
                                   states[:, b % 4, h, e * P:(e + 1) * P],
                                   feat[:, h, SEQ + b:SEQ + b + 1], start=True, stop=True,
                                   skip_group_check=True)
                gla_t.did(mm, f"so{b}")
            for i in range(DC):
                h, side = i // 2, slice(i * P, (i + 1) * P)
                bank = [ps[1], ps[2], ps[3], ps[7]][i % 4]
                if i >= 4:
                    w(pe, f"o{i - 4}")
                pe.matmul(bank[:, 0:P], v_tok[:, 0, side], att[:, h, 0, :], start=True, stop=True,
                          skip_group_check=True)
                pe.matmul(bank[:, P:SEQ], v_tok[:, 0, side], att01[:, h, :], start=True, stop=False,
                          skip_group_check=True)
                gla_t.did(pe.matmul(bank[:, P:SEQ], v_tok[:, 1, side], att[:, h, 1, :], start=False,
                                    stop=True, skip_group_check=True), f"o{i}")
            gla_g.wait(pe, "osq")
            for h in range(GH):
                bank = [ps[4], ps[5], ps[6], ps[0]][h]
                if h == 1:
                    gla_s.wait(pe, "sf1")
                for e in range(2):
                    mm = pe.matmul(bank[:, 0:TOK], ones[:, 0:P], o_sq[:, 2 * h + e, :],
                                   start=(e == 0), stop=(e == 1))
                gla_t.did(mm, f"hs{h}")

        def scores(pe, banks, k, q, name):
            for h in range(GH):
                for b in range(NBLK):
                    at = (h % 2) * SEQ + b * P
                    side = slice(b * P, (b + 1) * P)
                    mm = pe.matmul(banks[h // 2][:, at:at + P], k[:, h, side], q[:, h, side],
                                   start=True, stop=True, skip_group_check=True)
            gla_t.did(mm, name)

        def vector_gla(dve):
            did, wt = gla_v.did, gla_t.wait
            dve.wait_ge(mm_done, 2 * ph[("out", 1)]["piece"])
            wt(dve, "gl")
            did(dve.tensor_copy(onehot[:, :, :], ident[0:NSAMP, 0:NSAMP].unsqueeze(2)
                                .broadcast_to([NSAMP, NSAMP, P])), "onehot")
            did(dve.tensor_tensor(gl[:, :], ps[0][0:RANK, 0:TOK], rinv[0:RANK, :], ALU.mult), "gl")
            for h in range(GH):
                wt(dve, f"z{h}")
                did(dve.tensor_scalar(zt[:, h, :], ps[h][:, 0:TOK], cols[:, 64 + h:65 + h], None,
                                      ALU.add), f"z{h}")
            gla_v.wait(dve, "z3")
            gla_s.wait(dve, "absz")
            did(dve.tensor_scalar(zt[:, :, :], zt[:, :, :], 0.0, 1.0 / GATE_NORM, ALU.min, ALU.mult),
                "minz")
            gla_s.wait(dve, "ln")
            gla_v.wait(dve, "minz")
            did(dve.scalar_tensor_tensor(out=loga[:, :, :], in0=loga[:, :, :],
                                         scalar=-1.0 / GATE_NORM, in1=zt[:, :, :], op0=ALU.mult,
                                         op1=ALU.add), "loga")
            gla_v.wait(dve, "loga")
            for h in range(GH):
                did(dve.tensor_tensor_scan(cum[:, h, :], ones[:, 0:SEQ], loga[:, h, 0:SEQ], 0.0,
                                           ALU.mult, ALU.add), f"cum{h}")
            did(dve.memset(att[:, :, :, :], 0.0), "att0")
            wt(dve, "dg")
            gla_v.wait(dve, "att0")
            dve.wait_ge(mask_landed, 16)
            copy_level(dve, len(LEVELS) - 1, level_banks(0), "cpd")
            for lv, m in enumerate(LEVELS):
                gla_s.wait(dve, f"ed{lv}")
                if lv:
                    wt(dve, f"lv{lv - 1}")
                else:
                    gla_g.wait(dve, "qf0s")
                    gla_s.wait(dve, "qs")
                did(dve.tensor_tensor(halves_of(qf, m)[:, :, 1, :], halves_of(qc, m)[:, :, 1, :],
                                      halves_of(decay[lv % 2], m)[:, :, 1, :], ALU.mult), f"qf{lv}")
                if lv == 1:
                    wt(dve, "lv0")
                    did(dve.tensor_copy(att01[:, :, :], ps[0][:, :].rearrange("p (h t) -> p h t", h=GH)),
                        "cp0_0")
                elif lv > 1:
                    copy_level(dve, lv - 2, level_banks(lv - 1), f"cp{lv - 1}_")
            wt(dve, f"lv{inner[-1]}")
            copy_level(dve, inner[-1] - 1, level_banks(inner[-1]), f"cp{inner[-1]}_")
            for b in range(NSAMP):
                wt(dve, f"vb{b}")
                for h in range(GH):
                    gla_s.wait(dve, f"sm{b}_{h}")
                    bank = level_banks(b)[h // 2]
                    did(dve.scalar_tensor_tensor(
                        out=states[:, b % 4, h, :], in0=bank[:, (h % 2) * DV:(h % 2 + 1) * DV],
                        scalar=feat[:, GH + h, SEQ + b:SEQ + b + 1], in1=states[:, b % 4, h, :],
                        op0=ALU.mult, op1=ALU.add), f"sn{b}_{h}")
            for i in range(DC):
                wt(dve, f"o{i}")
                bank = [ps[1], ps[2], ps[3], ps[7]][i % 4]
                did(dve.tensor_copy(feat[:, DC + i, 0:SEQ], bank[:, 0:SEQ]), f"o{i}")
            did(dve.tensor_copy(feat[:, DC:2 * DC, SEQ:TOK],
                                ps[0][:, 0:DC * NSAMP].rearrange("p (i b) -> p i b", i=DC)), "os")
            gla_s.wait(dve, "hstd3")
            did(dve.reciprocal(head_std[:, :, :], head_std[:, :, :]), "hinv")
            gla_v.wait(dve, "hinv")
            for i in range(DC):
                need(dve, al_done, G0["act"] + i - 1)
                did(dve.scalar_tensor_tensor(out=feat[:, DC + i, :], in0=feat[:, DC + i, :],
                                             scalar=cols[:, 68 + i % 2:69 + i % 2],
                                             in1=head_std[:, i // 2, :], op0=ALU.mult, op1=ALU.mult),
                    f"og{i}")
                gla_v.wait(dve, f"og{i}")
                dve.tensor_tensor(abuf[:, i % 2, :], feat[:, DC + i, :], feat[:, 2 * DC + i, :],
                                  ALU.mult).then_inc(a_done, 1)
                if i:
                    mixer_lo(dve, G0["act"], i - 1)
            mixer_lo(dve, G0["act"], DC - 1)

        def copy_level(dve, mask, banks, name):
            for e in range(2):
                if e == 0 and name != "cpd":
                    gla_t.wait(dve, f"lv{name[2:-1]}")
                if name != "cpd":
                    former = "cpd" if name == "cp1_" else f"cp{mask}_"
                    gla_v.wait(dve, f"{former}{e}")
                gla_v.did(dve.copy_predicated(
                    att[:, 2 * e:2 * e + 2, :, :].rearrange("p h b t -> p (h b) t"),
                    level_mask[:, mask:mask + 1, :].broadcast_to([P, 2 * NBLK, P]),
                    banks[e][:, :].rearrange("p (n t) -> p n t", t=P)), f"{name}{e}")

        def mixer_lo(dve, act0, c):
            dve.wait_ge(ah_done, act0 + c + 1)
            dve.tensor_tensor(actl[:, c, :], abuf[:, c % 2, :], acth[:, c, :].bitcast(F32),
                              ALU.subtract).then_inc(al_done, 1)

        def mixer_hi(act, act0, c, number):
            act.wait_ge(a_done, number + 1)
            act.activation(acth[:, c, :], abuf[:, c % 2, :], ACT.Copy).then_inc(ah_done, 1)

        def scalar_gla(act):
            did, wv, wg, wt = gla_s.did, gla_v.wait, gla_g.wait, gla_t.wait
            act.wait_ge(bank_read, G0["tile"])
            wt(act, "gl")
            did(act.activation(qc[:, :, :], feat[:, 0:GH, 0:SEQ], ACT.Copy, scale=DK ** -0.5), "qs")
            did(act.activation(kc[:, :, :], feat[:, GH:2 * GH, 0:SEQ], ACT.Copy), "kc")
            did(act.activation(feat[:, 0:GH, SEQ:TOK], feat[:, 0:GH, SEQ:TOK], ACT.Copy,
                               scale=DK ** -0.5), "qss")
            wv(act, "z3")
            did(act.activation(loga[:, :, :], zt[:, :, :], ACT.Abs), "absz")
            gla_s.wait(act, "absz")
            did(act.activation(loga[:, :, :], loga[:, :, :], ACT.Exp, scale=-1.0), "e")
            gla_s.wait(act, "e")
            did(act.activation(loga[:, :, :], loga[:, :, :], ACT.Ln, bias=1.0), "ln")
            wv(act, "loga")
            did(act.activation(ea[:, :, :], loga[:, :, SEQ:TOK], ACT.Exp), "ea")
            wg(act, "dk")
            did(act.activation(decay[1][:, :, :], decay[1][:, :, :], ACT.Exp), "edk")
            for b in range(NBLK):
                wt(act, f"kt{b}")
                did(act.activation(kd_tok[:, b, :], TURN[b][:, :], ACT.Copy), f"kt{b}")
            for lv in range(len(LEVELS)):
                wg(act, f"dr{lv}")
                did(act.activation(decay[lv % 2][:, :, :], decay[lv % 2][:, :, :], ACT.Exp), f"ed{lv}")
            wv(act, f"qf{len(LEVELS) - 1}")
            wg(act, f"kf{len(LEVELS) - 1}")
            for e in range(2):
                wt(act, f"st{e}")
                did(act.activation(s_fin[:, 2 * e:2 * e + 2, :],
                                   TURN[e][:, :].rearrange("p (h v) -> p h v", h=2), ACT.Copy),
                    f"sf{e}")
            gla_s.wait(act, "ea")
            for b in range(NSAMP):
                if b % 4 == 0:
                    act.wait_ge(state_landed, 16 * (b // 4 + 1))
                for h in range(GH):
                    did(act.activation(states[:, b % 4, h, :], states[:, b % 4, h, :], ACT.Copy,
                                       scale=ea[:, h, b:b + 1]), f"sm{b}_{h}")
            did(act.activation(feat[:, 2 * DC:3 * DC, :], feat[:, 2 * DC:3 * DC, :], ACT.Silu), "silu")
            for h in range(GH):
                bank = [ps[4], ps[5], ps[6], ps[0]][h]
                wt(act, f"hs{h}")
                did(act.activation(head_std[:, h, :], bank[:, 0:TOK], ACT.Sqrt, scale=1.0 / DV,
                                   bias=eps[:, :]), f"hstd{h}")
            for c in range(DC):
                mixer_hi(act, G0["act"], c, c)

        def pool_gla(pool):
            did, wv, ws, wt = gla_g.did, gla_v.wait, gla_s.wait, gla_t.wait
            pool.wait_ge(mm_done, 2 * ph[("in", 1)]["piece"])
            pool.dma_start(level_mask[:, :, :], A["c_masks"]).then_inc(mask_landed, 16)
            state = A["state_gla"][0].rearrange("b h k v -> k b h v")
            pool.dma_start(states[:, :, :, :], state[:, 0:4]).then_inc(state_landed, 16)
            did(pool.memset(qf[:, :, :], 0.0), "qf0s")
            did(pool.memset(kf[:, :, :], 0.0), "kf0s")
            wv(pool, "cum3")
            did(pool.tensor_tensor(decay[1][:, :, :], cum[:, :, SEQ - 1:SEQ].broadcast_to([P, GH, SEQ]),
                                   cum[:, :, :], ALU.subtract), "dk")
            ws(pool, "edk")
            ws(pool, "kc")
            did(pool.tensor_tensor(kd[:, :, :], kc[:, :, :], decay[1][:, :, :], ALU.mult), "kd")
            for lv, m in enumerate(LEVELS):
                c, d = halves_of(cum, m), halves_of(decay[lv % 2], m)
                n = GH * SEQ // (2 * m)
                ref = c[:, :, 0, m - 1:m].broadcast_to([P, n, m])
                if lv == 1:
                    gla_g.wait(pool, "kd")
                if lv > 1:
                    wv(pool, f"qf{lv - 2}")
                    gla_g.wait(pool, f"kf{lv - 2}")
                did(pool.tensor_tensor(d[:, :, 0, :], ref, c[:, :, 0, :], ALU.subtract), f"dl{lv}")
                did(pool.tensor_tensor(d[:, :, 1, :], c[:, :, 1, :], ref, ALU.subtract), f"dr{lv}")
                ws(pool, f"ed{lv}")
                if lv:
                    wt(pool, f"lv{lv - 1}")
                else:
                    gla_g.wait(pool, "kf0s")
                did(pool.tensor_tensor(halves_of(kf, m)[:, :, 0, :], halves_of(kc, m)[:, :, 0, :],
                                       d[:, :, 0, :], ALU.mult), f"kf{lv}")
            ws(pool, "sf1")
            store(pool, A["gla_state_prompt"][0, 0].rearrange("h k v -> k h v"), s_fin[:, :, :])
            out = A["gla_state_sample"][0].rearrange("b h k v -> k b h v")
            for half in range(2):
                wv(pool, f"sn{4 * half + 3}_{GH - 1}")
                pool.dma_start(out[:, 4 * half:4 * half + 4], states[:, :, :, :])\
                    .then_inc(state_stored, 16)
                pool.wait_ge(state_stored, 16 * (half + 1))
                if half == 0:
                    wt(pool, "so3")
                    pool.dma_start(states[:, :, :, :], state[:, 4:8]).then_inc(state_landed, 16)
            pool.wait_ge(stored, 32)
            wv(pool, "os")
            did(pool.tensor_tensor(o_sq[:, :, :], feat[:, DC:2 * DC, :], feat[:, DC:2 * DC, :],
                                   ALU.mult), "osq")

        M0, IN2 = ph[("mix", 2)], ph[("in", 2)]
        NPG = NSAMP * NPAGES
        MP = MH // 2
        SUMS_FROM, SUMS = 3, 4
        SUMS_LEFT = NPG - SUMS * (3 * DC // 4 - SUMS_FROM)
        extras = {0: ["bs"], 2: ["sl", "sln", "smx"], 3: ["sri", "spn", "own"], 4: ["np"]}
        moba_v = Steps(sem("moba_vector"),
                       ["rows", "rowneg", "spz", "nk", "z0", "z1"]
                       + [n for k in range(MP + 5) for n in (
                           ([f"la{k}", f"lb{k}", f"mxa{k}", f"mxb{k}"] if k < MP else [])
                           + ([f"oc{k - 3}"] if 3 <= k < MP + 3 else [])
                           + ([f"ri{k - 1}", f"na{k - 1}", f"nb{k - 1}"] if 1 <= k <= MP else [])
                           + extras.get(k, [])
                           + ([f"lo{k - 5}"] if k >= 5 else []))]
                       + ["ext", "os"])
        moba_s = Steps(sem("moba_scalar"),
                       [n for k in range(MP + 4) for n in (
                           ([f"{n}{k}_{e}" for n in ("ea", "eb") for e in range(2)] if k < MP else [])
                           + ([f"pt{k - 1}"] if 1 <= k <= MP else [])
                           + {2: ["sex"], 3: ["spt0", "spt1"]}.get(k, [])
                           + ([f"hi{k - 4}"] if k >= 4 else []))])
        moba_t = Steps(sem("moba_tensor"),
                       ["rows"] + [n for k in range(MP + 4) for n in (
                           ([f"s{k}"] if k < MP else []) + ([f"t{k - 1}"] if 1 <= k <= MP else [])
                           + ([f"o{k - 2}"] if 2 <= k < MP + 2 else [])
                           + {0: ["bs", "zn"], 2: ["sct"], 3: ["spt", "pnt"]}.get(k, [])
                           + ([f"pv{k - 4}"] if k >= 4 else []))] + ["os"])
        keys_multiplied = sem("keys_multiplied")
        keys_summed = sem("keys_summed")
        SB, ACC, MISC, TB, OB = allps[:, 0:2, :], allps[:, 2:4, :], ps[4], allps[:, 5:7, :], ps[7]
        BLOCKS = ((0, SEQ), (SEQ, SEQ + P))

        def load_page(eng, n):
            page = n % NPG
            cache = A["cache_k"] if n < NPG else A["cache_v"]
            number = eng.value_load(table[0:1, page:page + 1], min_val=0, max_val=NPOOL - 1)
            eng.dma_start(pages[:, n % PAGE_SLOTS, :], cache[0][bass.ds(number, 1), :, :, :]
                          .rearrange("a p h d -> p (a h d)"))\
                .then_inc((keys_landed if n < NPG else values_landed)[n % PAGE_SLOTS], 16)

        def by_key(g, n):
            last = strip[:, 2 * g:2 * g + 2, n - 1:n]
            return bass.AP(tensor=last.tensor, offset=last.offset,
                           ap=[last.ap[0], last.ap[1], [-1, n]])

        def pool_moba(pool):
            pool.wait_ge(mm_done, 2 * IN2["piece"])
            pool.wait_ge(ss_done, IN2["norm"])
            for b in range(NSAMP):
                pool.dma_start(relb[:, b, :], A["rel_bias"]).then_inc(bias_landed, 16)
            pool.dma_start(of_strip[:, 0:STRIP], A["c_of_strip"]).then_inc(bias_landed, 16)
            pool.dma_start(of_past[:, :], A["c_of_past"]).then_inc(bias_landed, 16)
            pool.wait_ge(table_landed, 16)
            for n in range(PAGE_SLOTS):
                load_page(pool, n)
            pool.wait_ge(unturned, 2 * (IN2["turn"] + DC))
            pool.dma_start(q_scratch.ap(), vts[:, 0:D]).then_inc(scratch_landed, 16)
            pool.wait_ge(scratch_landed, 16)
            for b in range(2):
                pool.dma_start(q_row[:, b, :], q_scratch.ap()[b:b + 1, :].broadcast_to([P, D]))\
                    .then_inc(q_landed[b], 16)
            for n in range(NPG):
                b = n // NPAGES
                pool.wait_ge(q_landed[b % 2], 16 * (b // 2 + 1))
                pool.wait_ge(keys_landed[n % PAGE_SLOTS], 16 * (n // PAGE_SLOTS + 1))
                if n >= 2:
                    pool.wait_ge(keys_summed, n - 1)
                pool.tensor_tensor(prod[:, n % 2, :], pages[:, n % PAGE_SLOTS, :],
                                   q_row[:, b % 2, :], ALU.mult).then_inc(keys_multiplied, 1)
                if n == 0:
                    moba_v.wait(pool, "rowneg")
                    pool.dma_start(scratch.ap()[:, 0:STRIP], rows[:, 0:STRIP])\
                        .then_inc(scratch_landed, 16)
                if n == 3:
                    pool.wait_ge(scratch_landed, 32)
                    shifted = bass.AP(tensor=scratch.ap().tensor, offset=0,
                                      ap=[[1, P], [STRIP + 1, MH], [1, 2 * P]])
                    pool.dma_start(strip[:, :, :], shifted).then_inc(strip_landed, 16)
                if n + PAGE_SLOTS < NPG:
                    pool.wait_ge(keys_multiplied, n + 1)
                    load_page(pool, n + PAGE_SLOTS)
                if n % NPAGES == NPAGES - 1 and b + 2 < NSAMP:
                    pool.wait_ge(keys_multiplied, n + 1)
                    pool.dma_start(q_row[:, b % 2, :], q_scratch.ap()[b + 2:b + 3, :]
                                   .broadcast_to([P, D])).then_inc(q_landed[b % 2], 16)
            pool.wait_ge(unturned, 2 * (IN2["turn"] + 3 * DC))
            for name, at in (("k_new", D), ("v_new", 2 * D)):
                store(pool, A[name + "_prompt"][0, 0].rearrange("(b p) h d -> p b (h d)", p=P),
                      vt[:, :, at:at + D])
                store(pool, A[name + "_sample"][0].rearrange("b o h d -> (b o) (h d)"),
                      vts[:, at:at + D])

        def sp_pages(sp):
            sp.wait_ge(table_landed, 16)
            for n in range(NPG, 2 * NPG):
                page = n - NPG
                if page < PAGE_SLOTS:
                    sp.wait_ge(keys_multiplied, n - PAGE_SLOTS + 1)
                else:
                    moba_t.wait(sp, f"pv{(page - PAGE_SLOTS) // NPAGES}")
                load_page(sp, n)

        def pe_rows(pe):
            pe.wait_ge(bias_landed, 16 * (NSAMP + 2))
            moba_t.did(pe.matmul(ps[7][0:MH, 0:STRIP], relb[:, 0, :], of_strip[:, 0:STRIP],
                                 start=True, stop=True), "rows")

        def vector_rows(dve):
            moba_t.wait(dve, "rows")
            moba_v.did(dve.tensor_copy(rows[:, P - 1:STRIP], ps[7][0:MH, P - 1:STRIP]), "rows")
            moba_v.did(dve.memset(rows[:, 0:P - 1], NEG), "rowneg")

        def vector_sum_keys(dve, n, slot, column, page):
            dve.wait_ge(keys_multiplied, n + 1)
            dve.tensor_reduce(sc[:, page, column], prod[:, slot, :]
                              .rearrange("p (h d) -> p h d", h=MH), AX.X, ALU.add)\
                .then_inc(keys_summed, 1)

        def pe_moba(pe):
            did, wv, ws = moba_t.did, moba_v.wait, moba_s.wait
            pe.wait_ge(bank_read, M0["tile"])
            for k in range(MP + 4):
                if k < MP:
                    if k:
                        wv(pe, f"lb{k - 1}")
                    for e in range(2):
                        r = slice(DH * e, DH * e + DH)
                        pe.matmul(SB[:, e, 0:SEQ], feat[r, k, P:SEQ], feat[r, DC + k, 0:SEQ],
                                  start=True, stop=True, skip_group_check=True)
                        mm = pe.matmul(SB[:, e, SEQ:SEQ + P], feat[r, k, 0:P], feat[r, DC + k, 0:P],
                                       start=True, stop=True, skip_group_check=True)
                    did(mm, f"s{k}")
                if 1 <= k <= MP:
                    g = k - 1
                    wv(pe, f"nb{g}")
                    if g:
                        ws(pe, f"pt{g - 1}")
                    for e in range(2):
                        for t in range(3):
                            mm = pe.transpose(TB[:, e, t * P:(t + 1) * P],
                                              logit[:, g % 2, e, t * P:(t + 1) * P], ident[:, :])
                    did(mm, f"t{g}")
                if 2 <= k < MP + 2:
                    g = k - 2
                    ws(pe, f"pt{g}")
                    if g == 0:
                        pe.wait_ge(unturned, 2 * (IN2["turn"] + 3 * DC))
                    if g:
                        wv(pe, f"oc{g - 1}")
                    for e in range(2):
                        h, r = 2 * g + e, slice(DH * e, DH * e + DH)
                        v = [vt[:, b, 2 * D + h * DH:2 * D + (h + 1) * DH] for b in range(NBLK)]
                        pr = prob_t[:, g % 2, e, :]
                        pe.matmul(OB[r, 0:P], v[0], pr[:, SEQ:SEQ + P], start=True,
                                  stop=True, skip_group_check=True)
                        pe.matmul(OB[r, P:SEQ], v[0], pr[:, 0:P], start=True, stop=False,
                                  skip_group_check=True)
                        mm = pe.matmul(OB[r, P:SEQ], v[1], pr[:, P:SEQ], start=False,
                                       stop=True, skip_group_check=True)
                    did(mm, f"o{g}")
                if k == 0:
                    did(pe.matmul(MISC[:, 0:SEQ + 1], relb[:, :, :].rearrange("p b h -> p (b h)"),
                                  of_past[:, :], start=True, stop=True, skip_group_check=True), "bs")
                    wv(pe, "z1")
                    did(pe.matmul(MISC[:, 384:385], new_z[:, :, :, :].rearrange("p b c e -> p (b c e)"),
                                  ones[:, 0:1], start=True, stop=True, skip_group_check=True), "zn")
                if k == 2:
                    wv(pe, "bs")
                    pe.wait_ge(keys_summed, NPG)
                    for pg in range(NPAGES):
                        mm = pe.transpose(MISC[:, pg * P:(pg + 1) * P], sc[:, pg, :], ident[:, :])
                    did(mm, "sct")
                if k == 3:
                    wv(pe, "spn")
                    for pg in range(NPAGES):
                        mm = pe.transpose(MISC[:, pg * P:(pg + 1) * P],
                                          slog[:, pg * P:(pg + 1) * P], ident[:, :])
                    did(mm, "spt")
                    wv(pe, "own")
                    did(pe.transpose(MISC[0:NSAMP, 384:512], new_own[:, :], ident[:, :]), "pnt")
                if k >= 4:
                    b = k - 4
                    if b == 0:
                        wv(pe, "np")
                        ws(pe, "spt1")
                        for e in range(2):
                            pe.matmul(ACC[:, e, :], new_p[:, :],
                                      vts[:, 2 * D + e * 512:2 * D + (e + 1) * 512], start=True,
                                      stop=False, skip_group_check=True)
                    r = slice(32 * (b // 2), 32 * (b // 2) + 32)
                    for pg in range(NPAGES):
                        n = NPAGES * b + pg
                        pe.wait_ge(values_landed[n % PAGE_SLOTS], 16 * (n // PAGE_SLOTS + 1))
                        for e in range(2):
                            mm = pe.matmul(ACC[r, e, :], sp_tok[:, pg, b, :],
                                           pages[:, n % PAGE_SLOTS, e * 512:(e + 1) * 512],
                                           start=False, stop=(b % 2 == 1 and pg == NPAGES - 1),
                                           skip_group_check=True,
                                           tile_position=(0, 32 * (b // 2)))
                    did(mm, f"pv{b}")
            wv(pe, "ext")
            for c in range(DC):
                mm = pe.matmul(MISC[:, c * NSAMP:(c + 1) * NSAMP], ext[:, c * P:(c + 1) * P],
                               own[:, :], start=True, stop=True, skip_group_check=True)
            did(mm, "os")

        def vector_moba(dve):
            did, wt, ws = moba_v.did, moba_t.wait, moba_s.wait
            scale = DH ** -0.5
            dve.wait_ge(mm_done, 2 * ph[("out", 2)]["piece"])
            did(dve.memset(sp_tok[:, :, :, :], 0.0), "spz")
            did(dve.tensor_tensor(new_qk[:, :, :], feat[:, 0:DC, SEQ:TOK], feat[:, DC:2 * DC, SEQ:TOK],
                                  ALU.mult), "nk")
            moba_v.wait(dve, "nk")
            for e in range(2):
                did(dve.tensor_scalar(new_z[:, :, :, e], new_qk[:, :, :].rearrange("p c b -> p b c"),
                                      halves[:, e:e + 1], None, ALU.mult), f"z{e}")
            dve.wait_ge(strip_landed, 16)
            for k in range(MP + 5):
                if k < MP:
                    wt(dve, f"s{k}")
                    if k >= 2:
                        wt(dve, f"t{k - 2}")
                    i = k % 2
                    for n, (lo, hi) in enumerate(BLOCKS):
                        did(dve.scalar_tensor_tensor(
                            out=logit[:, i, :, lo:hi], in0=SB[:, :, lo:hi], scalar=scale,
                            in1=by_key(k, hi - lo), op0=ALU.mult, op1=ALU.add), f"l{'ab'[n]}{k}")
                    for n, (lo, hi) in enumerate(BLOCKS):
                        moba_v.wait(dve, f"l{'ab'[n]}{k}")
                        did(dve.tensor_reduce(softs[:, i, 0, n, :], logit[:, i, :, lo:hi], AX.X,
                                              ALU.max, negate=True), f"mx{'ab'[n]}{k}")
                if 3 <= k < MP + 3:
                    g = k - 3
                    wt(dve, f"o{g}")
                    did(dve.tensor_copy(feat[:, g, 0:SEQ], OB[:, 0:SEQ]), f"oc{g}")
                if 1 <= k <= MP:
                    g, i = k - 1, (k - 1) % 2
                    ws(dve, f"eb{g}_1")
                    did(dve.reciprocal(softs[:, i, 2, :, :], softs[:, i, 1, :, :]), f"ri{g}")
                    moba_v.wait(dve, f"ri{g}")
                    for n, (lo, hi) in enumerate(BLOCKS):
                        inverse = softs[:, i, 2, n, :].unsqueeze(2).broadcast_to([P, 2, hi - lo])
                        did(dve.tensor_tensor(logit[:, i, :, lo:hi], logit[:, i, :, lo:hi], inverse,
                                              ALU.mult), f"n{'ab'[n]}{g}")
                if k == 0:
                    wt(dve, "zn")
                    did(dve.tensor_copy(sbias[:, :], MISC[:, 0:SEQ + 1]), "bs")
                if k < 2:
                    left = -(-SUMS_LEFT // 2)
                    for n in range(NPG)[NPG - SUMS_LEFT:][k * left:(k + 1) * left]:
                        b = n // NPAGES
                        vector_sum_keys(dve, n, n % 2, slice(b * MH, (b + 1) * MH), n % NPAGES)
                if k == 2:
                    wt(dve, "sct")
                    did(dve.scalar_tensor_tensor(
                        out=slog[:, 0:SEQ], in0=MISC[:, 0:SEQ], scalar=scale, in1=sbias[:, 0:SEQ],
                        op0=ALU.mult, op1=ALU.add), "sl")
                    did(dve.scalar_tensor_tensor(
                        out=slog[:, SEQ:SEQ + 1], in0=MISC[:, 384:385], scalar=scale,
                        in1=sbias[:, SEQ:SEQ + 1], op0=ALU.mult, op1=ALU.add), "sln")
                    moba_v.wait(dve, "sln")
                    did(dve.tensor_reduce(small[:, 0:1], slog[:, :], AX.X, ALU.max, negate=True),
                        "smx")
                if k == 3:
                    ws(dve, "sex")
                    did(dve.reciprocal(small[:, 2:3], small[:, 1:2]), "sri")
                    moba_v.wait(dve, "sri")
                    did(dve.tensor_scalar(slog[:, :], slog[:, :], small[:, 2:3], None, ALU.mult),
                        "spn")
                    moba_v.wait(dve, "spn")
                    did(dve.tensor_scalar(new_own[:, :], own[:, :], slog[:, SEQ:SEQ + 1], None,
                                          ALU.mult), "own")
                if k == 4:
                    ws(dve, "spt1")
                    did(dve.tensor_copy(new_p[:, :], MISC[0:NSAMP, 384:512]), "np")
                if k >= 5:
                    c = k - 5
                    ws(dve, f"hi{c}")
                    did(dve.tensor_tensor(actl[:, c, 0:SEQ], feat[:, c, 0:SEQ],
                                          acth[:, c, 0:SEQ].bitcast(F32), ALU.subtract), f"lo{c}")
            wt(dve, f"pv{NSAMP - 1}")
            did(dve.tensor_tensor(ext[:, :].rearrange("p (h d) -> p h d", h=MH),
                                  ACC[:, :, :].rearrange("p e (h d) -> p (e h) d", d=DH),
                                  head_of[:, :].unsqueeze(2).broadcast_to([P, MH, DH]), ALU.mult),
                "ext")
            wt(dve, "os")
            did(dve.tensor_copy(feat[:, 0:DC, SEQ:TOK], MISC[:, 0:DC * NSAMP]
                                .rearrange("p (c b) -> p c b", c=DC)), "os")
            dve.wait_ge(ah_done, M0["act"] + DC)
            dve.tensor_tensor(actl[:, 0:DC, SEQ:TOK], feat[:, 0:DC, SEQ:TOK],
                              acth[:, 0:DC, SEQ:TOK].bitcast(F32), ALU.subtract).then_inc(al_done, DC)

        def scalar_moba(act):
            did, wt, wv = moba_s.did, moba_t.wait, moba_v.wait
            for k in range(MP + 4):
                if k < MP:
                    i = k % 2
                    for n, (lo, hi) in enumerate(BLOCKS):
                        wv(act, f"mx{'ab'[n]}{k}")
                        for e in range(2):
                            did(act.activation(logit[:, i, e, lo:hi], logit[:, i, e, lo:hi], ACT.Exp,
                                               bias=softs[:, i, 0, n, e:e + 1],
                                               accum_out=softs[:, i, 1, n, e:e + 1]),
                                f"e{'ab'[n]}{k}_{e}")
                if 1 <= k <= MP:
                    g = k - 1
                    wt(act, f"t{g}")
                    if g >= 2:
                        wt(act, f"o{g - 2}")
                    did(act.activation(prob_t[:, g % 2, :, :], TB[:, :, 0:3 * P], ACT.Copy), f"pt{g}")
                if k == 2:
                    wv(act, "smx")
                    did(act.activation(slog[:, :], slog[:, :], ACT.Exp, bias=small[:, 0:1],
                                       accum_out=small[:, 1:2]), "sex")
                if k == 3:
                    wt(act, "pnt")
                    for e in range(2):
                        did(act.activation(
                            sp_tok[:, :, e::2, MH * e:MH * e + MH],
                            MISC[:, 0:SEQ].rearrange("p (g b e h) -> p g b e h", g=NPAGES, e=2, h=MH)
                            [:, :, :, e, :], ACT.Copy), f"spt{e}")
                if k >= 4:
                    c = k - 4
                    wv(act, f"oc{c}")
                    did(act.activation(acth[:, c, 0:SEQ], feat[:, c, 0:SEQ], ACT.Copy), f"hi{c}")
            wv(act, "os")
            act.activation(acth[:, 0:DC, SEQ:TOK], feat[:, 0:DC, SEQ:TOK], ACT.Copy)\
                .then_inc(ah_done, DC)

        block = ctx.enter_context(nc.Block())

        @block.sync
        def _(sp):
            for layer in range(DEPTH):
                for kind in ("in", "out", "up", "down"):
                    stream(sp, (kind, layer))

        @block.gpsimd
        def _(pool):
            pool_setup(pool)
            pool_squares(pool, "load")
            for layer in range(DEPTH):
                if layer % 3 == 0:
                    pool_sgu(pool, layer)
                elif layer % 3 == 1:
                    pool_gla(pool)
                else:
                    pool_moba(pool)
                if layer == DEPTH - 1:
                    pool.wait_ge(al_done, ph[("mix", layer)]["act"] + HC)
                    pool.dma_start(gain_fin[:, :], A["norm_final"].rearrange("(o d) -> o d", o=1)
                                   .broadcast_to([P, D])).then_inc(fin_landed, 16)
                pool_squares(pool, ("out", layer))
                if layer < DEPTH - 1:
                    pool_squares(pool, ("down", layer))
            pool_final(pool)
            pool.wait_ge(stored, 16 * len(STORES))

        @block.scalar
        def _(act):
            scalar_setup(act)
            scalar_load(act)
            for layer in range(DEPTH):
                name = ("in", layer)
                if layer % 3 == 0:
                    scalar_in(act, name, 0, 6, ACT.Gelu, turns=True, first_of_phase=True)
                    scalar_lnstd(act, layer)
                    scalar_in(act, name, 6, 12, ACT.Gelu, into_feat=-HC, norm_v=True)
                    scalar_sgu(act, layer)
                elif layer % 3 == 1:
                    scalar_in(act, name, 0, 2, None, first_of_phase=True)
                    scalar_in(act, name, 2, 4, ACT.Copy, turns=True, reads_feat=True)
                    scalar_in(act, name, 4, 6, None)
                    scalar_gla(act)
                else:
                    scalar_in(act, name, 0, 6, ACT.Copy, turns=True, reads_feat=True,
                              first_of_phase=True)
                    scalar_moba(act)
                scalar_out(act, ("out", layer))
                scalar_up(act, layer)
                scalar_out(act, ("down", layer))
            scalar_final(act)

        @block.tensor
        def _(pe):
            pe_load(pe)
            for layer in range(DEPTH):
                name = ("in", layer)
                new_norm = ph[name]["norm"] - 1
                if layer % 3 == 0:
                    pe_project(pe, name, 0, 6, turns_from=0, new_norm=new_norm)
                    pe_project(pe, name, 6, 12)
                    pe_sgu(pe, layer)
                elif layer % 3 == 1:
                    pe_project(pe, name, 0, 2, new_norm=new_norm)
                    pe_project(pe, name, 2, 4, turns_from=2)
                    pe_project(pe, name, 4, 6)
                    pe_gla(pe)
                else:
                    pe_project(pe, name, 0, SUMS_FROM, turns_from=0, new_norm=new_norm)
                    pe_rows(pe)
                    pe_project(pe, name, SUMS_FROM, 6, turns_from=0)
                    pe_moba(pe)
                pe_out(pe, ("out", layer))
                pe_project(pe, ("up", layer), 0, FC // 2, new_norm=ph[("up", layer)]["norm"] - 1)
                pe_out(pe, ("down", layer))
            pe_final(pe)

        @block.vector
        def _(dve):
            vector_load(dve)
            for layer in range(DEPTH):
                name = ("in", layer)
                if layer % 3 == 0:
                    vector_in(dve, name, 0, 6, stats_of=True, first_of_phase=True)
                    vector_moments(dve, layer)
                    vector_in(dve, name, 6, 12, norm_v=True)
                    vector_sgu(dve, layer)
                elif layer % 3 == 1:
                    vector_in(dve, name, 0, 6, whole=True, first_of_phase=True)
                    vector_gla(dve)
                else:
                    vector_in(dve, name, 0, SUMS_FROM, whole=True, first_of_phase=True)
                    vector_rows(dve)
                    vector_in(dve, name, SUMS_FROM, 6, whole=True, sum_keys=True)
                    vector_moba(dve)
                vector_out(dve, ("out", layer))
                vector_up(dve, layer)
                vector_out(dve, ("down", layer))
            vector_final(dve)


def _constants():
    s, t = np.arange(P)[:, None], np.arange(P)[None, :]
    masks = [(s // (2 * m) == t // (2 * m)) & (s % (2 * m) < m) & (t % (2 * m) >= m)
             for m in LEVELS[1:]] + [s == t]

    def buckets(dist):
        exact = BUCKETS // 2
        far = np.maximum(dist, exact).astype(np.float32)
        large = exact + (np.log(far / exact) / np.float32(np.log(MAXDIST / exact))
                         * (BUCKETS - exact)).astype(np.int32)
        bucket = np.where(dist < exact, dist, np.minimum(large, BUCKETS - 1))
        return (np.arange(BUCKETS)[:, None] == bucket[None]) & (dist >= 0)[None]

    f = np.float32
    return {
        "c_ident": np.eye(P, dtype=f),
        "c_halves": (np.arange(P)[:, None] // DH == np.arange(2)[None]).astype(f),
        "c_own": (np.arange(P)[:, None] // MH == np.arange(NSAMP)[None]).astype(f),
        "c_head_of": (np.arange(P)[:, None] % MH == np.arange(MH)[None]).astype(f),
        "c_masks": np.stack(masks, 1).astype(np.int32),
        "c_of_strip": buckets(np.arange(STRIP) - (P - 1)).astype(f),
        "c_of_past": buckets(SEQ - np.arange(SEQ + 1)).astype(f),
    }


_INS = ["x_prompt", "x_sample", "cache_k", "cache_v", "page_table", "state_gla",
        "norm_mix", "norm_ffn", "norm_final", "w_in_a", "ln_a_g", "ln_a_b", "w_s_a", "b_s_a",
        "w_out_a", "w_in_b", "w_gate_b", "b_gate_b", "gn_b", "w_out_b", "w_in_c", "w_out_c",
        "rel_bias", "w_up", "w_down"]
_OUTS = [("y_prompt", (1, SEQ, D)), ("y_sample", (NSAMP, 1, D)),
         ("k_new_prompt", (1, 1, SEQ, MH, DH)), ("v_new_prompt", (1, 1, SEQ, MH, DH)),
         ("k_new_sample", (1, NSAMP, 1, MH, DH)), ("v_new_sample", (1, NSAMP, 1, MH, DH)),
         ("gla_state_prompt", (1, 1, GH, DK, DV)), ("gla_state_sample", (1, NSAMP, GH, DK, DV)),
         ("sgu_v_sample", (2, NSAMP, 1, HALF))]


def kernel(**inputs):
    import concourse.bacc as bacc
    from concourse.bass_utils import run_bass_kernel_spmd

    nc = bacc.Bacc("TRN2", target_bir_lowering=False, num_devices=1)
    arrays, A = {}, {}
    for name, a in [(n, inputs[n]) for n in _INS] + list(_constants().items()):
        a = np.ascontiguousarray(a)
        arrays[f"in_{name}"] = a
        A[name] = nc.dram_tensor(f"in_{name}", a.shape, mybir.dt.from_np(a.dtype),
                                 kind="ExternalInput").ap()
    for name, shape in _OUTS:
        A[name] = nc.dram_tensor(f"out_{name}", shape, F32, kind="ExternalOutput").ap()
    build(nc, A)
    got = run_bass_kernel_spmd(nc, [arrays], core_ids=[0]).results[0]
    return tuple(got[f"out_{name}"] for name, _ in _OUTS)
```

```python
from contextlib import ExitStack

import concourse.bass as bass
from concourse import mybir
import numpy as np

F32 = mybir.dt.float32
F32R = mybir.dt.float32r
I32 = mybir.dt.int32
ALU = mybir.AluOpType
ACT = mybir.ActivationFunctionType
AX = mybir.AxisListType

P = 128
D = 1024
DC = D // P
SEQ = 256
NSAMP = 8
TOK = SEQ + NSAMP
NBLK = SEQ // P
DEPTH = 4
EPS = 1e-6

HALF = 3 * D
HC = HALF // P
GROUPS = 8
GC = HC // GROUPS

GH, DK, DV = 4, 128, 256
RANK = 16
GLA_PROJ = 2 * GH * DK + 2 * GH * DV + RANK
GATE_NORM = 16.0
LEVELS = [128, 64, 32, 16, 8, 4, 2, 1]

MH, DH = 16, 64
NPAGES = 2
NPOOL = NSAMP * NPAGES * 5 // 4
BUCKETS = 32
MAXDIST = 128
STRIP = 3 * P - 1
NEG = -1e30

DFF = 2816
FC = DFF // P

KC = 8
PW = 256
SLOTS = 2
BANKS = 4
PAGE_SLOTS = 4
NORM_STEPS = 4
SQ_STEPS = 2 * DC + 1


def need(eng, sem, value):
    if not isinstance(value, int) or value > 0:
        eng.wait_ge(sem, value)


def run_loop(eng, start, end, body, peel=False):
    if peel:
        body(start, True)
        start += 1
    if end - start == 1:
        body(start, False)
    elif start < end:
        with eng.Fori(start, end) as i:
            body(i, False)


def cut(i, size):
    return slice(i * size, (i + 1) * size) if isinstance(i, int) else bass.ds(i * size, size)


def one(i):
    return slice(i, i + 1) if isinstance(i, int) else bass.ds(i, 1)


def chunk(tensor, m):
    return tensor[:, one(m), :].rearrange("p a t -> p (a t)")


class Steps:

    def __init__(self, sem, names):
        self.sem, self.names, self.at = sem, names, 0
        self.number = {n: k + 1 for k, n in enumerate(names)}
        assert len(self.number) == len(names)

    def did(self, instruction, name):
        assert self.names[self.at] == name, (self.names[self.at], name)
        self.at += 1
        instruction.then_inc(self.sem, 1)

    def wait(self, eng, name):
        eng.wait_ge(self.sem, self.number[name])


def make_plan():
    now = dict(piece=0, tile=0, norm=0, func=0, turn=0, act=0)
    phases = {}

    def add(name, **count):
        phases[name] = dict(now)
        for k, v in count.items():
            now[k] += v

    add("load", tile=DC, norm=1)
    for layer in range(DEPTH):
        if layer % 3 == 0:
            add(("in", layer), piece=2 * HC // 2, tile=2 * HC, func=2 * HC, turn=HC)
            add(("mix", layer), tile=HC, act=HC)
            add(("out", layer), piece=4 * HC // KC, tile=DC, norm=1)
        else:
            turns = 2 * DC // 2 if layer % 3 == 1 else 3 * DC
            add(("in", layer), piece=3 * DC // 2, tile=3 * DC, func=turns, turn=turns)
            add(("mix", layer), act=DC)
            add(("out", layer), piece=DC // 2, tile=DC, norm=1)
        add(("up", layer), piece=FC, tile=2 * FC, func=FC, act=FC)
        add(("down", layer), piece=12, tile=DC, norm=int(layer < DEPTH - 1))
    add("final", tile=DC)
    return phases


def build(nc, A):
    ph = make_plan()
    with ExitStack() as ctx:
        def sem(name):
            return ctx.enter_context(nc.semaphore(name))

        allps = ctx.enter_context(nc.psum_tensor("banks", [P, 8, 512], F32))
        ps = [allps[:, b, :] for b in range(8)]
        SS = ps[4]
        TURN = [ps[5], ps[6]]

        start_of, top = {}, [16640]

        def sb(name, shape, dt=F32):
            size = int(np.prod(shape[1:])) * 4
            start_of[name] = top[0]
            top[0] += -(-size // 32) * 32
            return nc.alloc_sbuf_tensor_at(name, shape, dt, offset=start_of[name])

        def over(name, host, offset, shape, dt=F32):
            start_of[name] = start_of[host] + offset
            return nc.alloc_sbuf_tensor_at(name, shape, dt, offset=start_of[host] + offset)

        raw = sb("raw", [P, SLOTS, KC, PW])
        whi = sb("whi", [P, SLOTS, KC, PW], F32R)
        wlo = sb("wlo", [P, SLOTS, KC, PW], F32R)
        x = sb("x", [P, DC, TOK])
        xh = sb("xh", [P, DC, TOK], F32R)
        xl = sb("xl", [P, DC, TOK], F32R)
        xg = sb("xg", [P, 2, TOK])
        tbuf = sb("tbuf", [P, BANKS, TOK])
        gbuf = sb("gbuf", [P, BANKS, TOK])
        gs = sb("gs", [P, 2, TOK])
        abuf = sb("abuf", [P, 2, TOK])
        rms = sb("rms", [P, TOK])
        rinv = sb("rinv", [P, TOK])
        sqsum = sb("sqsum", [P, TOK])
        sq = sb("sq", [P, TOK])
        ones = sb("ones", [P, SEQ])
        ident = sb("ident", [P, P])
        halves = sb("halves", [P, 2])
        own = sb("own", [P, NSAMP])
        head_of = sb("head_of", [P, MH])
        cols = sb("cols", [P, 70])
        w_rank = sb("w_rank", [P, DC, RANK])
        w_gate = sb("w_gate", [RANK, GH * DK])
        table = sb("table", [1, NSAMP * NPAGES], I32)
        w00 = sb("w00", [NSAMP, GROUPS])
        ws_diag = sb("ws_diag", [NSAMP, GROUPS, NSAMP])
        stats = sb("stats", [P, NBLK + 1, 6, 6])
        moments = sb("moments", [P, NBLK + 1, 2])
        lnstd = sb("lnstd", [P, NBLK + 1])
        lninv = sb("lninv", [P, NBLK + 1])
        lnshift = sb("lnshift", [P, NBLK + 1])
        small = sb("small", [P, 16])
        eps = sb("eps", [P, 1])
        softs = sb("softs", [P, 2, 3, NBLK, 2])
        acth = sb("acth", [P, HC, TOK], F32R)
        actl = sb("actl", [P, HC, TOK], F32R)
        feat = sb("feat", [P, HC, TOK])
        vt = sb("vt", [P, NBLK, HALF])
        vts = sb("vts", [NSAMP, HALF])
        assert top[0] <= 229344, top[0]

        TAIL = DC * TOK * 4
        xin = over("xin", "vt", 0, [P, NBLK + 1, D])
        col_rows = over("col_rows", "vt", 4 * 3 * D, [70, P])
        ytok = over("ytok", "vt", 0, [P, NBLK + 1, D])
        yout = over("yout", "acth", 0, [P, NBLK + 1, D])
        gain_fin = over("gain_fin", "feat", 0, [P, D])
        x_sq = over("x_sq", "feat", 0, [P, DC, TOK])
        ln_gain = over("ln_gain", "acth", 0, [P, HALF])
        ln_bias = over("ln_bias", "acth", 4 * HALF, [P, HALF])
        ws_nat = over("ws_nat", "acth", 8 * HALF, [P, GROUPS, P])
        ws_t = over("ws_t", "xh", 0, [P, GROUPS, P])
        mixbuf = over("mixbuf", "gs", 0, [P, 4, TOK])
        ws_bias = over("ws_bias", "actl", 2 * GROUPS * TOK * 4, [P, GROUPS, TOK])
        v_tok = over("v_tok", "vt", 0, [P, NBLK, GH * DV])
        vs_tok = over("vs_tok", "vt", 8192, [NSAMP, GH * DV])
        kd_tok = over("kd_tok", "vt", 12288, [P, NBLK, GH * DK])
        att = over("att", "vt", 16384, [P, GH, NBLK, P])
        att01 = over("att01", "vt", 20480, [P, GH, P])
        cum = over("cum", "vt", 22528, [P, GH, SEQ])
        qf = over("qf", "vt", 26624, [P, GH, SEQ])
        kf = over("kf", "vt", 30720, [P, GH, SEQ])
        loga = over("loga", "acth", TAIL, [P, GH, TOK])
        zt = over("zt", "acth", TAIL + 4224, [P, GH, TOK])
        decay = [over("decay0", "acth", TAIL + 4224, [P, GH, SEQ]),
                 over("decay1", "acth", TAIL + 8448, [P, GH, SEQ])]
        level_mask = over("level_mask", "gs", 0, [P, len(LEVELS), P], I32)
        rank_hi = over("rank_hi", "acth", TAIL + 12544, [P, DC, RANK], F32R)
        rank_lo = over("rank_lo", "acth", TAIL + 13056, [P, DC, RANK], F32R)
        gl = over("gl", "acth", TAIL + 13568, [RANK, TOK])
        ea = over("ea", "acth", TAIL + 14624, [P, GH, NSAMP])
        states = over("states", "actl", TAIL, [P, NSAMP // 2, GH, DV])
        v_row = over("v_row", "tbuf", 0, [P, 2, D])
        v_scratch = nc.dram_tensor("sample_values", [NSAMP, D], F32)
        kc = over("kc", "acth", 0, [P, GH, SEQ])
        kd = over("kd", "actl", 0, [P, GH, SEQ])
        qc = over("qc", "acth", 4096, [P, GH, SEQ])
        o_sq = over("o_sq", "xl", 0, [P, DC, TOK])
        qz = over("qz", "xh", 0, [P, GH, NSAMP, NSAMP])
        o_tok = over("o_tok", "xh", 1024, [NSAMP, GH * DV])
        head_std = over("head_std", "acth", TAIL, [P, GH, TOK])
        s_fin = over("s_fin", "acth", TAIL + 4224, [P, GH, DV])
        strip = over("strip", "acth", TAIL, [P, MH, 2 * P])
        pages = over("pages", "actl", TAIL, [P, PAGE_SLOTS, D])
        q_row = over("q_row", "acth", 0, [P, 2, D])
        prod = over("prod", "actl", 0, [P, 2, D])
        relb = over("relb", "gs", 0, [BUCKETS, NSAMP, MH])
        of_strip = over("of_strip", "gs", 512, [BUCKETS, STRIP + 1])
        rows = over("rows", "gs", 2048, [MH, STRIP + 1])
        of_past = over("of_past", "sqsum", 0, [BUCKETS, SEQ + 1])
        sc = over("sc", "sq", 0, [P, NPAGES, P])
        logit = over("logit", "tbuf", 0, [P, 2, 2, 3 * P])
        prob_t = over("prob_t", "xl", 0, [P, 2, 2, 3 * P])
        slog = over("slog", "xl", 6144, [P, SEQ + 1])
        sbias = over("sbias", "xl", 7200, [P, SEQ + 1])
        ext = over("ext", "xh", 0, [P, D])
        new_qk = over("new_qk", "xh", 4096, [P, DC, NSAMP])
        new_z = over("new_z", "xh", 4352, [P, NSAMP, DC, 2])
        new_own = over("new_own", "xh", 4864, [P, NSAMP])
        new_p = over("new_p", "xh", 4896, [NSAMP, P])
        sp_tok = over("sp_tok", "xh", 5408, [P, NPAGES, NSAMP, 2 * MH])
        scratch = nc.dram_tensor("bias_by_distance", [MH, STRIP + 1], F32)
        q_scratch = nc.dram_tensor("sample_queries", [NSAMP, D], F32)

        raw_landed = [sem(f"raw_landed{s}") for s in range(SLOTS)]
        w_hi = sem("w_hi")
        w_lo = sem("w_lo")
        mm_done = sem("mm_done")
        tile_made = sem("tile_made")
        bank_read = sem("bank_read")
        gained = sem("gained")
        xh_done = sem("xh_done")
        xl_done = sem("xl_done")
        x_sq_done = sem("x_sq_done")
        sq_done = sem("sq_done")
        ss_done = sem("ss_done")
        rms_done = sem("rms_done")
        rinv_done = sem("rinv_done")
        func_done = sem("func_done")
        turned = sem("turned")
        unturned = sem("unturned")
        gs_done = sem("gs_done")
        a_done = sem("a_done")
        ah_done = sem("ah_done")
        al_done = sem("al_done")
        in_landed = sem("in_landed")
        cols_landed = sem("cols_landed")
        const_landed = sem("const_landed")
        gate_landed = sem("gate_landed")
        table_landed = sem("table_landed")
        ones_done = sem("ones_done")
        cols_turned = sem("cols_turned")
        cols_done = sem("cols_done")
        ln_landed = sem("ln_landed")
        ws_landed = sem("ws_landed")
        w00_landed = sem("w00_landed")
        ws_masked = sem("ws_masked")
        ws_turned = sem("ws_turned")
        ws_ready = sem("ws_ready")
        ws_bias_landed = sem("ws_bias_landed")
        ws_bias_done = sem("ws_bias_done")
        mixed = sem("mixed")
        diag_done = sem("diag_done")
        stats_done = sem("stats_done")
        moments_done = sem("moments_done")
        lnstd_done = sem("lnstd_done")
        lninv_done = sem("lninv_done")
        lnshift_done = sem("lnshift_done")
        ln_scaled = sem("ln_scaled")
        lnormed = sem("lnormed")
        samples_normed = sem("samples_normed")
        stored = sem("stored")
        state_landed = [sem(f"state_landed{s}") for s in range(4)]
        state_stored = [sem(f"state_stored{s}") for s in range(4)]
        mask_landed = sem("mask_landed")
        keys_landed = [sem(f"keys_landed{s}") for s in range(PAGE_SLOTS)]
        values_landed = [sem(f"values_landed{s}") for s in range(PAGE_SLOTS)]
        bias_landed = sem("bias_landed")
        q_landed = [sem(f"q_landed{b}") for b in range(2)]
        scratch_landed = sem("scratch_landed")
        strip_landed = sem("strip_landed")
        fsq_done = sem("fsq_done")
        fstd_done = sem("fstd_done")
        finv_done = sem("finv_done")
        y_done = sem("y_done")
        fin_landed = sem("fin_landed")

        STORES = []

        def store(eng, out, src):
            eng.dma_start(out, src).then_inc(stored, 16)
            STORES.append(1)

        def pieces_of(name):
            kind, layer = name
            j = layer // 3

            def by_chunk(w):
                return w.rearrange("(c p) n -> p c n", p=P)

            if kind == "up":
                w = by_chunk(A["w_up"][layer])
                return [(w, 0, KC, t * DFF) for t in range(2)], PW, FC // 2
            if kind == "in":
                w = by_chunk(A[("w_in_a", "w_in_b", "w_in_c")[layer % 3]][j])
                return [(w, 0, KC, t * PW) for t in range(2)], 2 * PW, 12 if layer % 3 == 0 else 6
            if kind == "out" and layer % 3:
                w = by_chunk(A[("", "w_out_b", "w_out_c")[layer % 3]][j])
                return [(w, 0, KC, t * PW) for t in range(2)], 2 * PW, 2
            w = by_chunk(A["w_out_a"][j] if kind == "out" else A["w_down"][layer])
            depth = HC if kind == "out" else FC
            return [(w, c, min(KC, depth - c), t * PW) for t in range(2)
                    for c in range(0, depth, KC)], 2 * PW, 2

        def stream(sp, name):
            pieces, step, n = pieces_of(name)
            base, per = ph[name]["piece"], len(pieces)

            def body(i, shift, between=None):
                for t, (w, c, k, col) in enumerate(pieces):
                    need(sp, w_lo, 2 * per * i + 2 * (base + t - SLOTS + 1))
                    at = i * step + (col + shift)
                    columns = slice(at, at + PW) if isinstance(at, int) else bass.ds(at, PW)
                    sp.dma_start(raw[:, t % SLOTS, 0:k, :], w[:, c:c + k, columns])\
                        .then_inc(raw_landed[t % SLOTS], 16)
                    if between is not None:
                        sp_keys(sp, between + per * i + t)

            if name[0] == "out" and name[1] % 3:
                body(0, 0, ph[name]["piece"] - ph[("in", 2)]["piece"] if name[1] == 2 else None)
                (sp_states if name[1] == 1 else sp_pages)(sp)
                body(1, 0)
            elif name == ("in", 2):
                for i in range(n):
                    body(i, 0, 0)
            elif name[0] == "in" and name[1] % 3 == 0:
                run_loop(sp, 0, n // 2, lambda i, f: body(i, HALF), peel=base == 0)
                run_loop(sp, n // 2, n, lambda i, f: body(i, -HALF))
            else:
                run_loop(sp, 0, n, lambda i, f: body(i, 0))

        def split_hi(act, landed, used, slot, half, k):
            act.wait_ge(raw_landed[slot], landed)
            need(act, mm_done, used)
            side = slice(half * P, half * P + P)
            act.activation(whi[:, slot, 0:k, side], raw[:, slot, 0:k, side], ACT.Copy)\
                .then_inc(w_hi, 1)

        def split_lo(dve, number, slot, half, k):
            dve.wait_ge(w_hi, number)
            side = slice(half * P, half * P + P)
            dve.tensor_tensor(wlo[:, slot, 0:k, side], raw[:, slot, 0:k, side],
                              whi[:, slot, 0:k, side].bitcast(F32), ALU.subtract)\
                .then_inc(w_lo, 1)

        def split_next(eng, name, i, t, half, last=False):
            pieces, base = pieces_of(name)[0], ph[name]["piece"]
            per = len(pieces)
            if last and t + SLOTS >= per:
                return
            k = pieces[t + SLOTS][2] if t + SLOTS < per else KC
            at = base + t
            number = 2 * per * i + (2 * (at + SLOTS) + half + 1)
            if eng is nc.vector:
                split_lo(eng, number, t % SLOTS, half, k)
            else:
                landed = i * (16 * per // SLOTS) + 16 * (at // SLOTS + 2)
                split_hi(eng, landed, 2 * per * i + (2 * at + half + 1), t % SLOTS, half, k)

        def tile_mms(pe, bank, slot, half, chunks, rh, rl, c0, depth):
            side = slice(half * P, half * P + P)
            for c in chunks:
                pe.matmul(bank[:, 0:TOK], whi[:, slot, c, side], rh[:, c0 + c, :],
                          start=(c0 + c == 0), stop=False)
                pe.matmul(bank[:, 0:TOK], whi[:, slot, c, side], rl[:, c0 + c, :],
                          start=False, stop=False)
                mm = pe.matmul(bank[:, 0:TOK], wlo[:, slot, c, side], rh[:, c0 + c, :],
                               start=False, stop=(c0 + c == depth - 1))
            return mm

        def sum_squares(pe, norm):
            if norm == 0:
                pe.wait_ge(x_sq_done, DC)
                for c in range(DC):
                    mm = pe.matmul(SS[:, 0:TOK], ones[:, 0:P], x_sq[:, c, :], start=(c == 0),
                                   stop=(c == DC - 1))
                mm.then_inc(ss_done, 1)
                return
            pe.wait_ge(sq_done, SQ_STEPS * norm)
            need(pe, rms_done, norm)
            pe.matmul(SS[:, 0:TOK], ones[:, 0:P], sqsum[:, :], start=True, stop=True)\
                .then_inc(ss_done, 1)

        def turn_tile(pe, turn, func, j):
            pe.wait_ge(func_done, func + 1)
            need(pe, unturned, 2 * (turn - 1))
            out = TURN[j % 2]
            for b in range(NBLK):
                pe.transpose(out[:, b * P:(b + 1) * P], gbuf[:, j, b * P:(b + 1) * P], ident[:, :])
            pe.transpose(out[0:NSAMP, SEQ:SEQ + P], gbuf[:, j, SEQ:TOK], ident[:, :])\
                .then_inc(turned, 1)

        def pe_project(pe, name, start, end, turns_from=None, new_norm=None):
            at = ph[name]
            p0, t0 = at["piece"], at["tile"]

            def turn(i, j):
                step = i + (-turns_from)
                q = 4 * step + (at["turn"] + j)
                f = 4 * i + (at["func"] + j) if name[1] % 3 != 1 else 4 * step + (at["func"] + j)
                turn_tile(pe, q, f, j % BANKS)

            def body(i, first):
                for t in range(2):
                    for half in range(2):
                        pe.wait_ge(w_lo, 4 * i + (2 * (p0 + t) + half + 1))
                        j = 2 * t + half
                        need(pe, bank_read, t0 + 4 * i + j - BANKS + 1)
                        if first and new_norm is not None and j == 0:
                            for c in range(DC):
                                pe.wait_ge(xl_done, DC * new_norm + c + 1)
                                mm = tile_mms(pe, ps[j], t, half, [c], xh, xl, 0, DC)
                        else:
                            mm = tile_mms(pe, ps[j], t, half, range(KC), xh, xl, 0, DC)
                        mm.then_inc(mm_done, 1)
                        if first and new_norm is not None and j == 0:
                            sum_squares(pe, new_norm)
                        if turns_from is not None and not (first and j == 0):
                            turn(i, j - 1)

            run_loop(pe, start, end, body, peel=turns_from is not None or new_norm is not None)
            if turns_from is not None:
                turn(end - 1, BANKS - 1)

        def pe_out(pe, name):
            at = ph[name]
            pieces, _, steps = pieces_of(name)
            per = len(pieces)
            depth = sum(k for _, _, k, _ in pieces) // 2
            acts = ph[("mix", name[1])] if name[0] == "out" else ph[("up", name[1])]

            def body(i, first):
                for t, (_, c0, k, _) in enumerate(pieces):
                    panel = t // (per // 2)
                    for half in range(2):
                        pe.wait_ge(w_lo, 2 * per * i + (2 * (at["piece"] + t) + half + 1))
                        j = 2 * panel + half
                        if c0 == 0:
                            need(pe, bank_read, at["tile"] + 4 * i + j - BANKS + 1)
                        if first and panel == 0 and half == 0:
                            for c in range(k):
                                pe.wait_ge(al_done, acts["act"] + c0 + c + 1)
                                mm = tile_mms(pe, ps[j], t % SLOTS, half, [c], acth, actl, c0, depth)
                        else:
                            mm = tile_mms(pe, ps[j], t % SLOTS, half, range(k), acth, actl, c0, depth)
                        mm.then_inc(mm_done, 1)

            run_loop(pe, 0, steps, body, peel=True)

        def mm_value(name, i, j):
            pieces = pieces_of(name)[0]
            per, p0 = len(pieces), ph[name]["piece"]
            each = per // 2
            return 2 * per * i + (2 * p0 + 2 * each * (j // 2) + 2 * (each - 1) + j % 2 + 1)

        def new_chunk_vector(dve, norm, gain, m, j, tile, tile_wait, add):
            dve.wait_ge(*tile_wait)
            if add:
                dve.tensor_tensor(chunk(x, m), chunk(x, m), ps[j % BANKS][:, 0:TOK],
                                  ALU.add).then_inc(bank_read, 1)
            else:
                dve.tensor_copy(chunk(x, m), ps[j % BANKS][:, 0:TOK]).then_inc(bank_read, 1)
            if norm is None:
                return
            need(dve, xl_done, DC * norm + m - 1)
            dve.wait_ge(bank_read, tile + 1)
            dve.tensor_scalar(xg[:, j % 2, :], chunk(x, m),
                              cols[:, one(m + gain)], None, ALU.mult).then_inc(gained, 1)

        def new_chunk_lo(dve, norm, m, j):
            dve.wait_ge(xh_done, DC * norm + m + 1)
            dve.tensor_tensor(chunk(xl, m), xg[:, j % 2, :],
                              chunk(xh, m).bitcast(F32), ALU.subtract).then_inc(xl_done, 1)

        def new_chunk_scalar(act, norm, m, j):
            act.wait_ge(gained, DC * norm + m + 1)
            act.activation(chunk(xh, m), xg[:, j % 2, :], ACT.Copy)\
                .then_inc(xh_done, 1)

        def gain_of(name):
            if name == "load":
                return 0
            kind, layer = name
            return DC * (DEPTH + layer) if kind == "out" else DC * (layer + 1)

        def has_norm(name):
            return name != ("down", DEPTH - 1)

        def vector_out(dve, name):
            at = ph[name]
            per = len(pieces_of(name)[0])
            norm = at["norm"] if has_norm(name) else None

            def body(i, last):
                for t in range(per):
                    for half in range(2):
                        whole = t % (per // 2) == per // 2 - 1
                        j = 2 * (t // (per // 2)) + half
                        if whole:
                            new_chunk_vector(dve, norm, gain_of(name), 4 * i + j, j,
                                             at["tile"] + 4 * i + j,
                                             (mm_done, mm_value(name, i, j)), True)
                        if half == 0:
                            split_next(dve, name, i, t, half, last)
                        if whole and norm is not None:
                            new_chunk_lo(dve, norm, 4 * i + j, j)
                        if half == 1:
                            split_next(dve, name, i, t, half, last)

            if norm is None:
                body(0, False)
                body(1, True)
            else:
                run_loop(dve, 0, 2, lambda i, f: body(i, False))

        def scalar_out(act, name):
            at = ph[name]
            per = len(pieces_of(name)[0])

            def body(i, last):
                for t in range(per):
                    for half in range(2):
                        if half == 0:
                            split_next(act, name, i, t, half, last)
                        if has_norm(name) and t % (per // 2) == per // 2 - 1:
                            j = 2 * (t // (per // 2)) + half
                            new_chunk_scalar(act, at["norm"], 4 * i + j, j)
                        if half == 1:
                            split_next(act, name, i, t, half, last)

            if not has_norm(name):
                body(0, False)
                body(1, True)
            else:
                run_loop(act, 0, 2, lambda i, f: body(i, False))

        def pool_squares(pool, name):
            at = ph[name]
            norm = at["norm"]
            base = SQ_STEPS * (norm - 1)
            need(pool, ss_done, norm)
            pool.memset(sqsum[:, :], 0.0).then_inc(sq_done, 1)
            for_tiles = at["tile"]

            def body(m, first):
                pool.wait_ge(bank_read, m + (for_tiles + 1))
                pool.tensor_tensor(sq[:, :], chunk(x, m), chunk(x, m), ALU.mult)\
                    .then_inc(sq_done, 1)
                pool.wait_ge(sq_done, 2 * m + (base + 2))
                pool.tensor_tensor(sqsum[:, :], sqsum[:, :], sq[:, :], ALU.add).then_inc(sq_done, 1)
                pool.wait_ge(sq_done, 2 * m + (base + 3))

            run_loop(pool, 0, DC, body)

        def scalar_rms(act, norm):
            act.wait_ge(ss_done, norm + 1)
            need(act, rinv_done, norm)
            act.activation(rms[:, :], SS[:, 0:TOK], ACT.Sqrt, scale=1.0 / D, bias=eps[:, :])\
                .then_inc(rms_done, 1)

        def vector_rinv(dve, norm):
            dve.wait_ge(rms_done, norm + 1)
            dve.reciprocal(rinv[:, :], rms[:, :]).then_inc(rinv_done, 1)
            dve.wait_ge(rinv_done, norm + 1)

        def vector_up(dve, layer):
            name = ("up", layer)
            at = ph[name]
            f0, a0, g0 = at["func"], at["act"], FC * layer

            def act_lo(i, j):
                dve.wait_ge(ah_done, a0 + 2 * i + j + 1)
                dve.tensor_tensor(chunk(actl, 2 * i + j), abuf[:, j, :],
                                  chunk(acth, 2 * i + j).bitcast(F32), ALU.subtract)\
                    .then_inc(al_done, 1)

            def body(i, first):
                if first:
                    vector_rinv(dve, at["norm"] - 1)
                for j in range(2):
                    need(dve, func_done, f0 + 2 * i + j - 1)
                    dve.wait_ge(mm_done, mm_value(name, i, j))
                    dve.tensor_tensor(tbuf[:, j, :], ps[j][:, 0:TOK], rinv[:, :], ALU.mult)\
                        .then_inc(bank_read, 1)
                    split_next(dve, name, i, 0, j)
                for j in range(2):
                    dve.wait_ge(func_done, f0 + 2 * i + j + 1)
                    dve.tensor_tensor(gs[:, j, :], gbuf[:, j, :], rinv[:, :], ALU.mult)\
                        .then_inc(gs_done, 1)
                for j in range(2):
                    dve.wait_ge(gs_done, g0 + 2 * i + j + 1)
                    dve.wait_ge(mm_done, mm_value(name, i, 2 + j))
                    need(dve, al_done, a0 + 2 * i + j - 1)
                    dve.tensor_tensor(abuf[:, j, :], ps[2 + j][:, 0:TOK], gs[:, j, :], ALU.mult)\
                        .then_inc(bank_read, 1)
                    if j == 1:
                        act_lo(i, 0)
                    split_next(dve, name, i, 1, j)
                act_lo(i, 1)

            run_loop(dve, 0, FC // 2, body, peel=True)

        def scalar_up(act, layer):
            name = ("up", layer)
            at = ph[name]
            t0, a0, g0 = at["tile"], at["act"], FC * layer

            def body(i, first):
                if first:
                    scalar_rms(act, at["norm"] - 1)
                for j in range(2):
                    split_next(act, name, i, 0, j)
                    act.wait_ge(bank_read, t0 + 4 * i + j + 1)
                    if not first:
                        act.wait_ge(gs_done, g0 + 2 * i + j - 1)
                    act.activation(gbuf[:, j, :], tbuf[:, j, :], ACT.Silu).then_inc(func_done, 1)
                for j in range(2):
                    split_next(act, name, i, 1, j)
                    act.wait_ge(bank_read, t0 + 4 * i + 2 + j + 1)
                    act.activation(chunk(acth, 2 * i + j), abuf[:, j, :], ACT.Copy)\
                        .then_inc(ah_done, 1)

            run_loop(act, 0, FC // 2, body, peel=True)

        def pool_setup(pool):
            pool.dma_start(w_rank[:, :, :], A["w_in_b"][0].rearrange("(c p) n -> p c n", p=P)
                           [:, :, GLA_PROJ - RANK:GLA_PROJ]).then_inc(gate_landed, 16)
            pool.dma_start(w_gate[:, :], A["w_gate_b"][0]).then_inc(gate_landed, 16)

        def sp_input(sp):
            for src, row in (("norm_mix", 0), ("norm_ffn", 32), ("b_gate_b", 64), ("gn_b", 68)):
                flat = A[src].rearrange("a (c p) -> (a c) p", p=P)
                sp.dma_start(col_rows[row:row + flat.shape[0], :], flat).then_inc(cols_landed, 16)
            sp.dma_start(xin[:, 0:NBLK, :], A["x_prompt"][0].rearrange("(b p) d -> p b d", p=P))\
                .then_inc(in_landed, 16)
            sp.dma_start(xin[0:NSAMP, NBLK, :], A["x_sample"].rearrange("b s d -> (b s) d"))\
                .then_inc(in_landed, 16)

        def scalar_setup(act):
            act.dma_start(ident[:, :], A["c_ident"]).then_inc(const_landed, 16)
            act.dma_start(halves[:, :], A["c_halves"]).then_inc(const_landed, 16)
            act.dma_start(own[:, :], A["c_own"]).then_inc(const_landed, 16)
            act.dma_start(head_of[:, :], A["c_head_of"]).then_inc(const_landed, 16)
            act.dma_start(table[:, :], A["page_table"].rearrange("(o b) n -> o (b n)", o=1))\
                .then_inc(table_landed, 16)

        def pe_load(pe):
            pe.wait_ge(const_landed, 64)
            pe.wait_ge(cols_landed, 64)
            pe.transpose(TURN[0][:, 0:70], col_rows[:, :], ident[0:70, 0:70]).then_inc(cols_turned, 1)
            pe.wait_ge(in_landed, 32)
            for m in range(DC):
                need(pe, bank_read, m - BANKS + 1)
                bank = ps[m % BANKS]
                for b in range(NBLK):
                    pe.transpose(bank[:, b * P:(b + 1) * P], xin[:, b, m * P:(m + 1) * P], ident[:, :])
                pe.transpose(bank[:, SEQ:TOK], xin[0:NSAMP, NBLK, m * P:(m + 1) * P],
                             ident[0:NSAMP, 0:NSAMP]).then_inc(tile_made, 1)

        def vector_load(dve):
            dve.memset(eps[:, :], EPS).then_inc(ones_done, 1)
            dve.memset(ones[:, :], 1.0).then_inc(ones_done, 1)
            for half in range(2):
                split_lo(dve, half + 1, 0, half, KC)
            dve.wait_ge(cols_turned, 1)
            dve.tensor_copy(cols[:, :], TURN[0][:, 0:70]).then_inc(cols_done, 1)
            dve.wait_ge(cols_done, 1)
            for m in range(DC):
                new_chunk_vector(dve, 0, 0, m, m, m, (tile_made, m + 1), False)
                if m:
                    new_chunk_lo(dve, 0, m - 1, m - 1)
            new_chunk_lo(dve, 0, DC - 1, DC - 1)
            for half in range(2):
                split_lo(dve, half + 3, 1, half, KC)

        def scalar_load(act):
            for half in range(2):
                split_hi(act, 16, 0, 0, half, KC)
            for m in range(DC):
                new_chunk_scalar(act, 0, m, m)
                act.activation(x_sq[:, m, :], x[:, m, :], ACT.Square).then_inc(x_sq_done, 1)
            for half in range(2):
                split_hi(act, 16, 0, 1, half, KC)

        def vector_in(dve, name, start, end, whole=False, stats_of=None, norm_v=False,
                      sum_keys=False, first_of_phase=False):
            at = ph[name]

            def body(i, first):
                for t in range(2):
                    if first and first_of_phase and t == 0:
                        vector_rinv(dve, at["norm"] - 1)
                    for j in (2 * t, 2 * t + 1):
                        dve.wait_ge(mm_done, mm_value(name, i, j))
                        out = chunk(feat, 4 * i + j) if whole else tbuf[:, j, :]
                        if not whole:
                            need(dve, func_done, at["func"] + 4 * i + j - BANKS + 1)
                        dve.tensor_tensor(out, ps[j][:, 0:TOK], rinv[:, :], ALU.mult)\
                            .then_inc(bank_read, 1)
                        split_next(dve, name, i, t, j % 2)
                        if sum_keys:
                            at_b = MH * NPAGES * (i + (-start)) + MH * (j // 2)
                            vector_sum_keys(dve, SUMS * (i + (-start)) + j, j % 2,
                                            bass.ds(at_b, MH), j % NPAGES)
                    if norm_v and t == 1:
                        vector_norm_v(dve, sgu_number(name[1]), i + (-start))
                    if stats_of is not None and t == 0 and not first:
                        vector_stats(dve, name, i + (-1))

            run_loop(dve, start, end, body, peel=first_of_phase or stats_of is not None)
            if stats_of is not None:
                vector_stats(dve, name, end - 1)

        def vector_stats(dve, name, i):
            dve.wait_ge(unturned, 8 * i + (2 * ph[name]["turn"] + 8))
            for b in range(NBLK + 1):
                src = vt[:, b, cut(i, 4 * P)] if b < NBLK else vts[:, cut(i, 4 * P)]
                n = P if b < NBLK else NSAMP
                dve.bn_stats(stats[0:n, b, one(i), :].rearrange("p a s -> p (a s)"), src)\
                    .then_inc(stats_done, 1)

        def scalar_in(act, name, start, end, func, turns=False, into_feat=None, reads_feat=False,
                      norm_v=False, first_of_phase=False):
            at = ph[name]
            partial = name[1] % 3 == 1

            def finish_turn(i, j):
                step = i + (-start)
                q = 4 * step + (at["turn"] + j)
                act.wait_ge(turned, q + 1)
                m = 4 * step + j
                if partial:
                    prompts, samples = v_tok, vs_tok
                else:
                    prompts, samples = vt, vts
                bank = TURN[j % 2]
                act.activation(prompts[:, :, cut(m, P)],
                               bank[:, 0:SEQ].rearrange("p (b t) -> p b t", b=NBLK), ACT.Copy)\
                    .then_inc(unturned, 1)
                act.activation(samples[:, cut(m, P)], bank[0:NSAMP, SEQ:SEQ + P], ACT.Copy)\
                    .then_inc(unturned, 1)

            def body(i, first):
                for t in range(2):
                    if first and first_of_phase and t == 0:
                        scalar_rms(act, at["norm"] - 1)
                    for j in (2 * t, 2 * t + 1):
                        split_next(act, name, i, t, j % 2)
                        if func is None:
                            continue
                        act.wait_ge(bank_read, at["tile"] + 4 * i + j + 1)
                        src = chunk(feat, 4 * i + j) if reads_feat else tbuf[:, j, :]
                        if turns:
                            need(act, turned, 4 * (i + (-start)) + (at["turn"] + j - BANKS + 1))
                            out = gbuf[:, j, :]
                        else:
                            out = chunk(feat, 4 * i + (j + into_feat))
                        act.activation(out, src, func).then_inc(func_done, 1)
                        if turns and not (first and j == 0):
                            finish_turn(i, j - 1)
                    if norm_v and t == 0:
                        scalar_norm_v(act, i + (-start))
            if turns and name[1]:
                act.wait_ge(stored, 16 * (0, 1, 2, 6)[name[1]])
            run_loop(act, start, end, body, peel=turns or first_of_phase)
            if turns:
                finish_turn(end - 1, BANKS - 1)

        def sgu_number(layer):
            return layer // 3

        def pool_sgu(pool, layer):
            s = sgu_number(layer)
            at = ph[("in", layer)]
            need(pool, tile_made, 1) if layer == 0 else pool.wait_ge(mm_done, 2 * at["piece"])
            pool.dma_start(ln_gain[:, :], A["ln_a_g"][s:s + 1, :].broadcast_to([P, HALF]))\
                .then_inc(ln_landed, 16)
            pool.dma_start(ln_bias[:, :], A["ln_a_b"][s:s + 1, :].broadcast_to([P, HALF]))\
                .then_inc(ln_landed, 16)
            pool.dma_start(ws_nat[:, :, :], A["w_s_a"][s].rearrange("g i j -> i g j"))\
                .then_inc(ws_landed, 16)
            b_s = A["b_s_a"][s:s + 1]
            for b in range(NBLK):
                pool.dma_start(ws_bias[:, :, b * P:(b + 1) * P], b_s.broadcast_to([P, GROUPS, P]))\
                    .then_inc(ws_bias_landed, 16)
            if s:
                pool.wait_ge(diag_done, s)
            pool.dma_start(w00[:, :], A["w_s_a"][s].rearrange("g i j -> (i j) g")[0:1, :]
                           .broadcast_to([NSAMP, GROUPS]), allow_slow_non_contiguous=True)\
                .then_inc(w00_landed, 16)
            pool.wait_ge(ws_landed, 16 * (s + 1))
            pool.affine_select(out=ws_nat[:, :, :], in_=ws_nat[:, :, :], compare_op=ALU.is_ge,
                               fill=0.0, base=0, pattern=[[0, GROUPS], [-1, P]],
                               channel_multiplier=1).then_inc(ws_masked, 1)
            pool.wait_ge(ws_bias_landed, 32 * (s + 1))
            pool.tensor_copy(ws_bias[:, :, SEQ:TOK], ws_bias[:, :, 0:1]
                             .broadcast_to([P, GROUPS, NSAMP])).then_inc(ws_bias_done, 1)
            pool.wait_ge(ln_landed, 32 * (s + 1))
            pool.wait_ge(lnshift_done, (NBLK + 1) * (s + 1))
            v, n = vts[:, :], 3 * s
            pool.tensor_scalar(v, v, moments[0:NSAMP, NBLK, 0:1], lninv[0:NSAMP, NBLK:NBLK + 1],
                               ALU.subtract, ALU.mult).then_inc(samples_normed, 1)
            pool.wait_ge(samples_normed, n + 1)
            pool.tensor_tensor(v, v, ln_gain[0:NSAMP, :], ALU.mult).then_inc(samples_normed, 1)
            pool.wait_ge(samples_normed, n + 2)
            pool.tensor_tensor(v, v, ln_bias[0:NSAMP, :], ALU.add).then_inc(samples_normed, 1)
            pool.wait_ge(samples_normed, n + 3)
            store(pool, A["sgu_v_sample"][s].rearrange("b o d -> (b o) d"), vts[:, :])

        def vector_moments(dve, layer):
            s = sgu_number(layer)
            dve.wait_ge(stats_done, 6 * (NBLK + 1) * (s + 1))
            for b in range(NBLK + 1):
                n = P if b < NBLK else NSAMP
                dve.bn_aggr(moments[0:n, b, :], stats[0:n, b, :, :].rearrange("p a s -> p (a s)"))\
                    .then_inc(moments_done, 1)
            for b in range(NBLK + 1):
                n = P if b < NBLK else NSAMP
                dve.wait_ge(lnstd_done, (NBLK + 1) * s + b + 1)
                dve.reciprocal(lninv[0:n, b:b + 1], lnstd[0:n, b:b + 1]).then_inc(lninv_done, 1)
            for b in range(NBLK + 1):
                n = P if b < NBLK else NSAMP
                dve.wait_ge(lninv_done, (NBLK + 1) * s + b + 1)
                dve.scalar_tensor_tensor(out=lnshift[0:n, b:b + 1], in0=moments[0:n, b, 0:1],
                                         scalar=-1.0, in1=lninv[0:n, b:b + 1], op0=ALU.mult,
                                         op1=ALU.mult).then_inc(lnshift_done, 1)
            dve.wait_ge(ln_landed, 32 * (s + 1))
            dve.wait_ge(w00_landed, 16 * (s + 1))
            dve.tensor_tensor(ws_diag[:, :, :],
                              ident[0:NSAMP, 0:NSAMP].unsqueeze(1).broadcast_to([NSAMP, GROUPS, NSAMP]),
                              w00[:, :].unsqueeze(2).broadcast_to([NSAMP, GROUPS, NSAMP]), ALU.mult)\
                .then_inc(diag_done, 1)

        def scalar_norm_v(act, step):
            for b in range(NBLK):
                v = vt[:, b, cut(step, HALF // NORM_STEPS)]
                act.activation(v, v, ACT.Identity, scale=lninv[:, b:b + 1],
                               bias=lnshift[:, b:b + 1]).then_inc(ln_scaled, 1)

        def vector_norm_v(dve, s, step):
            n_cols = HALF // NORM_STEPS
            v, side = vt[:, :, cut(step, n_cols)], cut(step, n_cols)
            dve.wait_ge(ln_scaled, 2 * step + (2 * NORM_STEPS * s + 2))
            for n, (row, op) in enumerate(((ln_gain, ALU.mult), (ln_bias, ALU.add))):
                if n:
                    dve.wait_ge(lnormed, 2 * step + (2 * NORM_STEPS * s + 1))
                dve.tensor_tensor(v, v, row[:, side].unsqueeze(1).broadcast_to([P, NBLK, n_cols]), op)\
                    .then_inc(lnormed, 1)

        def scalar_lnstd(act, layer):
            s = sgu_number(layer)
            for b in range(NBLK + 1):
                n = P if b < NBLK else NSAMP
                act.wait_ge(moments_done, (NBLK + 1) * s + b + 1)
                act.activation(lnstd[0:n, b:b + 1], moments[0:n, b, 1:2], ACT.Sqrt, scale=1.0,
                               bias=eps[0:n, :]).then_inc(lnstd_done, 1)
            act.wait_ge(lnshift_done, (NBLK + 1) * (s + 1))
            act.wait_ge(unturned, 2 * (ph[("in", layer)]["turn"] + HC))

        def pe_sgu(pe, layer):
            s = sgu_number(layer)
            at = ph[("mix", layer)]
            pe.wait_ge(ws_masked, s + 1)
            for g in range(GROUPS):
                pe.transpose(TURN[g // 4][:, (g % 4) * P:(g % 4 + 1) * P], ws_nat[:, g, :],
                             ident[:, :]).then_inc(ws_turned, 1)
            pe.wait_ge(ws_ready, 2 * (s + 1))
            pe.wait_ge(diag_done, s + 1)
            pe.wait_ge(lnormed, 2 * NORM_STEPS * (s + 1))
            pe.wait_ge(samples_normed, 3 * (s + 1))
            for c in range(HC):
                g = c // GC
                bank = ps[c % BANKS]
                side = slice(c * P, (c + 1) * P)
                need(pe, bank_read, at["tile"] + c - BANKS + 1)
                for b in range(NBLK):
                    pe.matmul(bank[:, b * P:(b + 1) * P], vt[:, b, side], ws_t[:, g, :],
                              start=True, stop=True, skip_group_check=True)
                pe.matmul(bank[:, SEQ:TOK], vts[:, side], ws_diag[:, g, :], start=True, stop=True,
                          skip_group_check=True).then_inc(tile_made, 1)

        def made_before(layer):
            return DC + HC * (layer // 3)

        def vector_sgu(dve, layer):
            s = sgu_number(layer)
            at = ph[("mix", layer)]
            dve.wait_ge(func_done, ph[("in", layer)]["func"] + 2 * HC)

            dve.wait_ge(ws_bias_done, s + 1)

            def lo(c):
                dve.wait_ge(ah_done, at["act"] + c + 1)
                dve.tensor_tensor(actl[:, c, :], mixbuf[:, c % 4, :], acth[:, c, :].bitcast(F32),
                                  ALU.subtract).then_inc(al_done, 1)

            for c in range(HC):
                j = c % 4
                dve.wait_ge(tile_made, made_before(layer) + c + 1)
                if c >= 4:
                    dve.wait_ge(al_done, at["act"] + c - 3)
                dve.tensor_tensor(mixbuf[:, j, :], ps[c % BANKS][:, 0:TOK], ws_bias[:, c // GC, :],
                                  ALU.add).then_inc(bank_read, 1)
                if c >= 2:
                    lo(c - 2)
                dve.wait_ge(bank_read, at["tile"] + c + 1)
                dve.tensor_tensor(mixbuf[:, j, :], mixbuf[:, j, :], feat[:, c, :], ALU.mult)\
                    .then_inc(mixed, 1)
            lo(HC - 2)
            lo(HC - 1)

        def scalar_sgu(act, layer):
            s = sgu_number(layer)
            at = ph[("mix", layer)]
            for h in range(2):
                act.wait_ge(ws_turned, GROUPS * s + 4 * (h + 1))
                act.activation(ws_t[:, 4 * h:4 * h + 4, :],
                               TURN[h][:, :].rearrange("p (g t) -> p g t", g=4), ACT.Copy)\
                    .then_inc(ws_ready, 1)
            act.wait_ge(lnormed, 2 * NORM_STEPS * (s + 1))
            act.wait_ge(samples_normed, 3 * (s + 1))

            def body(i, first):
                for j in range(BANKS):
                    act.wait_ge(mixed, 4 * i + (HC * s + j + 1))
                    act.activation(chunk(acth, 4 * i + j), mixbuf[:, j, :], ACT.Copy)\
                        .then_inc(ah_done, 1)

            run_loop(act, 0, HC // BANKS, body)

        def pe_final(pe):
            at = ph["final"]["tile"]
            for m in range(DC):
                pe.wait_ge(bank_read, at + m - BANKS + 1)
                pe.wait_ge(bank_read, ph[("down", DEPTH - 1)]["tile"] + m + 1)
                bank = ps[m % BANKS]
                for b in range(NBLK):
                    pe.transpose(bank[:, b * P:(b + 1) * P], x[:, m, b * P:(b + 1) * P], ident[:, :])
                pe.transpose(bank[0:NSAMP, SEQ:SEQ + P], x[:, m, SEQ:TOK], ident[:, :])\
                    .then_inc(tile_made, 1)

        def vector_final(dve):
            base = made_before(DEPTH - 1) + HC
            for m in range(DC):
                dve.wait_ge(tile_made, base + m + 1)
                bank = ps[m % BANKS]
                side = slice(m * P, (m + 1) * P)
                dve.tensor_copy(ytok[0:NSAMP, NBLK, side], bank[0:NSAMP, SEQ:SEQ + P])\
                    .then_inc(y_done, 1)
                dve.tensor_copy(ytok[:, 0:NBLK, side],
                                bank[:, 0:SEQ].rearrange("p (b t) -> p b t", b=NBLK))\
                    .then_inc(bank_read, 1)
            dve.wait_ge(y_done, DC)
            dve.wait_ge(bank_read, ph["final"]["tile"] + DC)
            for b in range(NBLK + 1):
                n = P if b < NBLK else NSAMP
                dve.wait_ge(fstd_done, b + 1)
                dve.reciprocal(small[0:n, 8 + b:9 + b], small[0:n, 4 + b:5 + b]).then_inc(finv_done, 1)
            dve.wait_ge(fin_landed, 16)
            for b in range(NBLK + 1):
                n = P if b < NBLK else NSAMP
                dve.wait_ge(finv_done, b + 1)
                dve.wait_ge(fsq_done, b + 1)
                dve.scalar_tensor_tensor(out=yout[0:n, b, :], in0=ytok[0:n, b, :],
                                         scalar=small[0:n, 8 + b:9 + b], in1=gain_fin[0:n, :],
                                         op0=ALU.mult, op1=ALU.mult).then_inc(y_done, 1)

        def scalar_final(act):
            act.wait_ge(bank_read, ph["final"]["tile"] + DC)
            act.wait_ge(y_done, DC)
            for b in range(NBLK + 1):
                n = P if b < NBLK else NSAMP
                act.activation(yout[0:n, b, :], ytok[0:n, b, :], ACT.Square,
                               accum_out=small[0:n, b:b + 1]).then_inc(fsq_done, 1)
            for b in range(NBLK + 1):
                n = P if b < NBLK else NSAMP
                act.wait_ge(fsq_done, b + 1)
                act.activation(small[0:n, 4 + b:5 + b], small[0:n, b:b + 1], ACT.Sqrt,
                               scale=1.0 / D, bias=eps[0:n, :]).then_inc(fstd_done, 1)

        def pool_final(pool):
            for b in range(NBLK):
                pool.wait_ge(y_done, DC + b + 1)
                store(pool, A["y_prompt"][0, b * P:(b + 1) * P, :], yout[:, b, :])
            pool.wait_ge(y_done, DC + NBLK + 1)
            store(pool, A["y_sample"].rearrange("b s d -> (b s) d"), yout[0:NSAMP, NBLK, :])

        G0 = ph[("mix", 1)]
        LV = range(len(LEVELS))
        assert len(LEVELS) == NSAMP
        V_NAMES = (["rank", "gl"] + [f"z{h}" for h in range(GH)] + ["minz", "loga"]
                   + [f"cum{h}" for h in range(GH)] + ["att0", "dr0", "qz0", "qz", "cpd0", "cpd1"]
                   + [n for lv in LV for n in
                      ([f"dr{lv + 1}"] if lv < LV[-1] else []) + [f"qf{lv}"] + ([], ["cp0_0"])[lv == 1]
                      + ([f"cp{lv - 1}_{e}" for e in range(2)] if lv > 1 else [])
                      + [f"sn{lv}_{h}" for h in range(GH)]]
                   + [f"cp{LV[-1]}_{e}" for e in range(2)]
                   + ["ost0", "ost1", "o0", "o1", "o2", "os"] + [f"o{i}" for i in range(3, DC)]
                   + [n for h in range(GH) for n in (f"hinv{h}", f"og{2 * h}", f"og{2 * h + 1}")])
        S_NAMES = (["rank", "absz", "e", "ln", "qs", "kc", "qss", "ea", "edk", "kt0", "kt1", "ed0"]
                   + [n for lv in LV for n in ([f"ed{lv + 1}"] if lv < LV[-1] else [])
                      + [f"sm{lv}_{h}" for h in range(GH)]]
                   + ["sf0", "sf1", "silu"] + [f"sq{i}" for i in range(DC)] + [f"hstd{h}" for h in range(GH)])
        G_NAMES = (["qf0s", "kf0s", "dk", "dl0", "kd"]
                   + [n for lv in LV for n in ([f"dl{lv + 1}"] if lv < LV[-1] else [])
                      + [f"kf{lv}"]])
        T_NAMES = (["gl"] + [f"z{h}" for h in range(GH)] + ["dg", "kt0", "kt1"]
                   + [n for lv in LV for n in [f"lv{lv}"]
                      + ([f"so{lv - 1}"] if lv else []) + (["st0", "st1"] if lv == 4 else [])]
                   + [f"so{LV[-1]}", "o0", "o1", "o2", "ot"] + [f"o{i}" for i in range(3, DC)] + [f"hs{h}" for h in range(GH)])
        gla_v = Steps(sem("gla_vector"), V_NAMES)
        gla_s = Steps(sem("gla_scalar"), S_NAMES)
        gla_g = Steps(sem("gla_gpsimd"), G_NAMES)
        gla_t = Steps(sem("gla_tensor"), T_NAMES)

        LOGITS = [ps[7], ps[4], ps[5], ps[6]]
        SCORES = [ps[1], ps[2]]
        SAMPLE_O, OUTPUTS = [ps[3], ps[7]], [ps[1], ps[2], ps[0]]
        HEAD_SUMS = [ps[4], ps[5], ps[6], ps[4]]
        v_landed = [sem(f"v_landed{b}") for b in range(2)]
        v_stored = sem("v_stored")

        def halves_of(t, m):
            return t[:, :, :].rearrange("p h (n e m) -> p (h n) e m", e=2, m=m)

        def pe_gate(pe):
            w = gla_v.wait
            pe.wait_ge(gate_landed, 32)
            w(pe, "rank")
            for c in range(DC):
                for k, (weight, moving) in enumerate(((rank_hi, xh), (rank_hi, xl), (rank_lo, xh))):
                    mm = pe.matmul(ps[7][0:RANK, 0:TOK], weight[:, c, :], moving[:, c, :],
                                   start=(c == 0 and k == 0), stop=(c == DC - 1 and k == 2))
            gla_t.did(mm, "gl")
            w(pe, "gl")
            pe.wait_ge(rms_done, ph[("in", 1)]["norm"])
            for h in range(GH):
                gla_t.did(pe.matmul(LOGITS[h][:, 0:TOK], w_gate[:, h * DK:(h + 1) * DK], gl[:, :],
                                    start=True, stop=True), f"z{h}")
            w(pe, "z3")

        def pe_gla(pe):
            w = gla_v.wait
            pe.wait_ge(bank_read, G0["tile"])
            gla_s.wait(pe, "kc")
            scores(pe, SCORES, kc, qc, "dg")
            gla_g.wait(pe, "kd")
            pe.wait_ge(unturned, 2 * (ph[("in", 1)]["turn"] + DC))
            for b in range(NBLK):
                for h in range(GH):
                    mm = pe.transpose(TURN[b][:, h * P:(h + 1) * P], kd[:, h, b * P:(b + 1) * P],
                                      ident[:, :])
                gla_t.did(mm, f"kt{b}")
            gla_s.wait(pe, "qss")
            for lv in LV:
                w(pe, f"qf{lv}")
                gla_g.wait(pe, f"kf{lv}")
                if lv == 0:
                    for h in range(GH):
                        mm = pe.matmul(ps[0][:, h * P:(h + 1) * P], kf[:, h, 0:P], qf[:, h, P:SEQ],
                                       start=True, stop=True, skip_group_check=True)
                    gla_t.did(mm, "lv0")
                else:
                    w(pe, "cpd1" if lv == 1 else f"cp{lv - 1}_1")
                    scores(pe, SCORES, kf, qf, f"lv{lv}")
                if lv:
                    w(pe, f"sn{lv - 1}_{GH - 1}")
                    sample_output(pe, lv - 1)
                if lv == 4:
                    gla_s.wait(pe, "kt1")
                    for h in range(GH):
                        for b in range(NBLK):
                            mm = pe.matmul(TURN[h // 2][:, (h % 2) * DV:(h % 2 + 1) * DV],
                                           kd_tok[:, b, h * DK:(h + 1) * DK],
                                           v_tok[:, b, h * DV:(h + 1) * DV], start=(b == 0),
                                           stop=(b == NBLK - 1), skip_group_check=True)
                        if h % 2:
                            gla_t.did(mm, f"st{h // 2}")
            w(pe, f"sn{LV[-1]}_{GH - 1}")
            sample_output(pe, LV[-1])
            w(pe, f"cp{LV[-1]}_1")
            for i in range(DC):
                if i == 3:
                    w(pe, "ost1")
                    for c in range(DC):
                        mm = pe.transpose(SAMPLE_O[0][:, c * NSAMP:(c + 1) * NSAMP],
                                          o_tok[:, c * P:(c + 1) * P], ident[0:NSAMP, 0:NSAMP])
                    gla_t.did(mm, "ot")
                h, side = i // 2, slice(i * P, (i + 1) * P)
                bank = OUTPUTS[i % 3]
                if i >= 3:
                    w(pe, f"o{i - 3}")
                pe.matmul(bank[:, 0:P], v_tok[:, 0, side], att[:, h, 0, :], start=True, stop=True,
                          skip_group_check=True)
                pe.matmul(bank[:, P:SEQ], v_tok[:, 0, side], att01[:, h, :], start=True, stop=False,
                          skip_group_check=True)
                gla_t.did(pe.matmul(bank[:, P:SEQ], v_tok[:, 1, side], att[:, h, 1, :], start=False,
                                    stop=True, skip_group_check=True), f"o{i}")
            for h in range(GH):
                gla_s.wait(pe, f"sq{2 * h + 1}")
                if h == 3:
                    gla_s.wait(pe, "hstd0")
                for e in range(2):
                    mm = pe.matmul(HEAD_SUMS[h][:, 0:TOK], ones[:, 0:P], o_sq[:, 2 * h + e, :],
                                   start=(e == 0), stop=(e == 1))
                gla_t.did(mm, f"hs{h}")

        def sample_output(pe, b):
            for h in range(GH):
                mm = pe.matmul(SAMPLE_O[h // 2][0:NSAMP, (h % 2) * DV:(h % 2 + 1) * DV],
                               qz[:, h, b, :], states[:, b % 4, h, :],
                               start=(b == 0 and h % 2 == 0), stop=(b == NSAMP - 1),
                               skip_group_check=True)
            gla_t.did(mm, f"so{b}")

        def scores(pe, banks, k, q, name):
            for h in range(GH):
                for b in range(NBLK):
                    at = (h % 2) * SEQ + b * P
                    side = slice(b * P, (b + 1) * P)
                    mm = pe.matmul(banks[h // 2][:, at:at + P], k[:, h, side], q[:, h, side],
                                   start=True, stop=True, skip_group_check=True)
            gla_t.did(mm, name)

        def vector_gate(dve):
            did, wt = gla_v.did, gla_t.wait
            wt(dve, "gl")
            did(dve.tensor_tensor(gl[:, :], ps[7][0:RANK, 0:TOK], rinv[0:RANK, :], ALU.mult), "gl")
            for h in range(GH):
                wt(dve, f"z{h}")
                did(dve.tensor_scalar(zt[:, h, :], LOGITS[h][:, 0:TOK], cols[:, 64 + h:65 + h], None,
                                      ALU.add), f"z{h}")
            gla_v.wait(dve, "z3")
            gla_s.wait(dve, "absz")
            did(dve.tensor_scalar(zt[:, :, :], zt[:, :, :], 0.0, 1.0 / GATE_NORM, ALU.min, ALU.mult),
                "minz")
            gla_s.wait(dve, "ln")
            gla_v.wait(dve, "minz")
            did(dve.scalar_tensor_tensor(out=loga[:, :, :], in0=loga[:, :, :],
                                         scalar=-1.0 / GATE_NORM, in1=zt[:, :, :], op0=ALU.mult,
                                         op1=ALU.add), "loga")
            gla_v.wait(dve, "loga")
            dve.wait_ge(stored, 16)
            for h in range(GH):
                did(dve.tensor_tensor_scan(cum[:, h, :], ones[:, 0:SEQ], loga[:, h, 0:SEQ], 0.0,
                                           ALU.mult, ALU.add), f"cum{h}")
            did(dve.memset(att[:, :, :, :], 0.0), "att0")
            gla_v.wait(dve, "cum3")
            log_decay_right(dve, 0)

        def log_decay_right(dve, n):
            m = LEVELS[n]
            c, d = halves_of(cum, m), halves_of(decay[n % 2], m)
            gla_v.did(dve.tensor_tensor(d[:, :, 1, :], c[:, :, 1, :], c[:, :, 0, m - 1:m]
                                        .broadcast_to([P, GH * SEQ // (2 * m), m]), ALU.subtract),
                      f"dr{n}")

        def vector_gla(dve):
            did, wt = gla_v.did, gla_t.wait
            dve.wait_ge(mm_done, 2 * ph[("out", 1)]["piece"])
            did(dve.memset(qz[:, :, :, :], 0.0), "qz0")
            gla_v.wait(dve, "qz0")
            gla_s.wait(dve, "qss")
            did(dve.tensor_copy(qz[:, :, :, :].rearrange("p h b c -> p h (b c)")
                                [:, :, 0:NSAMP * NSAMP:NSAMP + 1], feat[:, 0:GH, SEQ:TOK]), "qz")
            wt(dve, "dg")
            gla_v.wait(dve, "att0")
            dve.wait_ge(mask_landed, 16)
            copy_level(dve, len(LEVELS) - 1, SCORES, "cpd")
            for lv, m in enumerate(LEVELS):
                if lv < LV[-1]:
                    gla_g.wait(dve, f"kf{lv - 1}" if lv else "kd")
                    if lv:
                        gla_v.wait(dve, f"qf{lv - 1}")
                    log_decay_right(dve, lv + 1)
                gla_s.wait(dve, f"ed{lv}")
                if lv:
                    wt(dve, f"lv{lv - 1}")
                else:
                    gla_g.wait(dve, "qf0s")
                    gla_s.wait(dve, "qs")
                did(dve.tensor_tensor(halves_of(qf, m)[:, :, 1, :], halves_of(qc, m)[:, :, 1, :],
                                      halves_of(decay[lv % 2], m)[:, :, 1, :], ALU.mult), f"qf{lv}")
                if lv == 1:
                    wt(dve, "lv0")
                    did(dve.tensor_copy(att01[:, :, :], ps[0][:, :].rearrange("p (h t) -> p h t", h=GH)),
                        "cp0_0")
                elif lv > 1:
                    copy_level(dve, lv - 2, SCORES, f"cp{lv - 1}_")
                dve.wait_ge(v_landed[lv % 2], 16 * (lv // 2 + 1))
                for h in range(GH):
                    gla_s.wait(dve, f"sm{lv}_{h}")
                    did(dve.scalar_tensor_tensor(
                        out=states[:, lv % 4, h, :], in0=v_row[:, lv % 2, h * DV:(h + 1) * DV],
                        scalar=feat[:, GH + h, SEQ + lv:SEQ + lv + 1], in1=states[:, lv % 4, h, :],
                        op0=ALU.mult, op1=ALU.add), f"sn{lv}_{h}")
            wt(dve, f"lv{LV[-1]}")
            copy_level(dve, LV[-1] - 1, SCORES, f"cp{LV[-1]}_")
            wt(dve, f"so{LV[-1]}")
            for e in range(2):
                did(dve.tensor_copy(o_tok[:, e * 512:(e + 1) * 512], SAMPLE_O[e][0:NSAMP, :]),
                    f"ost{e}")
            for i in range(DC):
                if i == 3:
                    wt(dve, "ot")
                    did(dve.tensor_copy(feat[:, DC:2 * DC, SEQ:TOK], SAMPLE_O[0][:, 0:DC * NSAMP]
                                        .rearrange("p (i b) -> p i b", i=DC)), "os")
                wt(dve, f"o{i}")
                did(dve.tensor_copy(feat[:, DC + i, 0:SEQ], OUTPUTS[i % 3][:, 0:SEQ]), f"o{i}")
            for i in range(DC):
                if i % 2 == 0:
                    h = i // 2
                    gla_s.wait(dve, f"hstd{h}")
                    did(dve.reciprocal(head_std[:, h, :], head_std[:, h, :]), f"hinv{h}")
                    gla_v.wait(dve, f"hinv{h}")
                    gla_s.wait(dve, "silu")
                need(dve, al_done, G0["act"] + i - 1)
                did(dve.scalar_tensor_tensor(out=feat[:, DC + i, :], in0=feat[:, DC + i, :],
                                             scalar=cols[:, 68 + i % 2:69 + i % 2],
                                             in1=head_std[:, i // 2, :], op0=ALU.mult, op1=ALU.mult),
                    f"og{i}")
                gla_v.wait(dve, f"og{i}")
                dve.tensor_tensor(abuf[:, i % 2, :], feat[:, DC + i, :], feat[:, 2 * DC + i, :],
                                  ALU.mult).then_inc(a_done, 1)
                if i:
                    mixer_lo(dve, G0["act"], i - 1)
            mixer_lo(dve, G0["act"], DC - 1)

        def copy_level(dve, mask, banks, name):
            for e in range(2):
                if e == 0 and name != "cpd":
                    gla_t.wait(dve, f"lv{name[2:-1]}")
                if name != "cpd":
                    former = "cpd" if name == "cp1_" else f"cp{mask}_"
                    gla_v.wait(dve, f"{former}{e}")
                gla_v.did(dve.copy_predicated(
                    att[:, 2 * e:2 * e + 2, :, :].rearrange("p h b t -> p (h b) t"),
                    level_mask[:, mask:mask + 1, :].broadcast_to([P, 2 * NBLK, P]),
                    banks[e][:, :].rearrange("p (n t) -> p n t", t=P)), f"{name}{e}")

        def mixer_lo(dve, act0, c):
            dve.wait_ge(ah_done, act0 + c + 1)
            dve.tensor_tensor(actl[:, c, :], abuf[:, c % 2, :], acth[:, c, :].bitcast(F32),
                              ALU.subtract).then_inc(al_done, 1)

        def mixer_hi(act, act0, c, number):
            act.wait_ge(a_done, number + 1)
            act.activation(acth[:, c, :], abuf[:, c % 2, :], ACT.Copy).then_inc(ah_done, 1)

        def scalar_rank(act):
            act.wait_ge(gate_landed, 32)
            act.wait_ge(mm_done, 2 * ph[("in", 1)]["piece"])
            gla_s.did(act.activation(rank_hi[:, :, :], w_rank[:, :, :], ACT.Copy), "rank")

        def vector_rank(dve):
            gla_s.wait(dve, "rank")
            gla_v.did(dve.tensor_tensor(rank_lo[:, :, :], w_rank[:, :, :],
                                        rank_hi[:, :, :].bitcast(F32), ALU.subtract), "rank")

        def scalar_gate(act):
            did = gla_s.did
            gla_v.wait(act, "z3")
            did(act.activation(loga[:, :, :], zt[:, :, :], ACT.Abs), "absz")
            gla_s.wait(act, "absz")
            did(act.activation(loga[:, :, :], loga[:, :, :], ACT.Exp, scale=-1.0), "e")
            gla_s.wait(act, "e")
            did(act.activation(loga[:, :, :], loga[:, :, :], ACT.Ln, bias=1.0), "ln")

        def scalar_decay(act):
            did = gla_s.did
            act.wait_ge(bank_read, ph[("in", 1)]["tile"] + DC)
            did(act.activation(qc[:, :, :], feat[:, 0:GH, 0:SEQ], ACT.Copy, scale=DK ** -0.5), "qs")
            did(act.activation(kc[:, :, :], feat[:, GH:2 * GH, 0:SEQ], ACT.Copy), "kc")
            did(act.activation(feat[:, 0:GH, SEQ:TOK], feat[:, 0:GH, SEQ:TOK], ACT.Copy,
                               scale=DK ** -0.5), "qss")
            gla_v.wait(act, "loga")
            did(act.activation(ea[:, :, :], loga[:, :, SEQ:TOK], ACT.Exp), "ea")
            gla_g.wait(act, "dk")
            did(act.activation(decay[1][:, :, :], decay[1][:, :, :], ACT.Exp), "edk")

        def scalar_gla(act):
            did, wv, wg, wt = gla_s.did, gla_v.wait, gla_g.wait, gla_t.wait
            for b in range(NBLK):
                wt(act, f"kt{b}")
                did(act.activation(kd_tok[:, b, :], TURN[b][:, :], ACT.Copy), f"kt{b}")
            gla_s.wait(act, "ea")
            for lv in range(-1, len(LEVELS)):
                if lv < LV[-1]:
                    wg(act, f"dl{lv + 1}")
                    wv(act, f"dr{lv + 1}")
                    decayed = decay[(lv + 1) % 2][:, :, :]
                    did(act.activation(decayed, decayed, ACT.Exp), f"ed{lv + 1}")
                if lv >= 0:
                    act.wait_ge(state_landed[lv % 4], 16 * (lv // 4 + 1))
                    for h in range(GH):
                        did(act.activation(states[:, lv % 4, h, :], states[:, lv % 4, h, :],
                                           ACT.Copy, scale=ea[:, h, lv:lv + 1]), f"sm{lv}_{h}")
            wv(act, f"qf{len(LEVELS) - 1}")
            wg(act, f"kf{len(LEVELS) - 1}")
            for e in range(2):
                wt(act, f"st{e}")
                did(act.activation(s_fin[:, 2 * e:2 * e + 2, :],
                                   TURN[e][:, :].rearrange("p (h v) -> p h v", h=2), ACT.Copy),
                    f"sf{e}")
            did(act.activation(feat[:, 2 * DC:3 * DC, :], feat[:, 2 * DC:3 * DC, :], ACT.Silu), "silu")
            for i in range(DC):
                wv(act, f"o{i}" if i >= 3 else "os")
                did(act.activation(o_sq[:, i, :], feat[:, DC + i, :], ACT.Square), f"sq{i}")
            for h in range(GH):
                bank = HEAD_SUMS[h]
                wt(act, f"hs{h}")
                did(act.activation(head_std[:, h, :], bank[:, 0:TOK], ACT.Sqrt, scale=1.0 / DV,
                                   bias=eps[:, :]), f"hstd{h}")
            for c in range(DC):
                mixer_hi(act, G0["act"], c, c)

        def pool_gla(pool):
            did, wv, ws, wt = gla_g.did, gla_v.wait, gla_s.wait, gla_t.wait
            pool.wait_ge(mm_done, 2 * ph[("in", 1)]["piece"])
            pool.dma_start(level_mask[:, :, :], A["c_masks"]).then_inc(mask_landed, 16)
            pool.wait_ge(stored, 16)
            did(pool.memset(qf[:, :, :], 0.0), "qf0s")
            did(pool.memset(kf[:, :, :], 0.0), "kf0s")
            wv(pool, "cum3")
            did(pool.tensor_tensor(decay[1][:, :, :], cum[:, :, SEQ - 1:SEQ].broadcast_to([P, GH, SEQ]),
                                   cum[:, :, :], ALU.subtract), "dk")
            for lv in range(-1, len(LEVELS)):
                if lv < LV[-1]:
                    n = lv + 1
                    m = LEVELS[n]
                    c, d = halves_of(cum, m), halves_of(decay[n % 2], m)
                    ref = c[:, :, 0, m - 1:m].broadcast_to([P, GH * SEQ // (2 * m), m])
                    if n == 1:
                        ws(pool, "edk")
                        ws(pool, "kc")
                        did(pool.tensor_tensor(kd[:, :, :], kc[:, :, :], decay[1][:, :, :],
                                               ALU.mult), "kd")
                        gla_g.wait(pool, "kd")
                    if n > 1:
                        wv(pool, f"qf{n - 2}")
                        gla_g.wait(pool, f"kf{n - 2}")
                    did(pool.tensor_tensor(d[:, :, 0, :], ref, c[:, :, 0, :], ALU.subtract), f"dl{n}")
                if lv >= 0:
                    m = LEVELS[lv]
                    ws(pool, f"ed{lv}")
                    if lv:
                        wt(pool, f"lv{lv - 1}")
                    else:
                        gla_g.wait(pool, "kf0s")
                    did(pool.tensor_tensor(halves_of(kf, m)[:, :, 0, :], halves_of(kc, m)[:, :, 0, :],
                                           halves_of(decay[lv % 2], m)[:, :, 0, :], ALU.mult),
                        f"kf{lv}")
            ws(pool, "sf1")
            store(pool, A["gla_state_prompt"][0, 0].rearrange("h k v -> k h v"), s_fin[:, :, :])
            pool.wait_ge(stored, 32)

        def sp_states(sp):
            state = A["state_gla"][0].rearrange("b h k v -> k b h v")
            out = A["gla_state_sample"][0].rearrange("b h k v -> k b h v")
            sp.wait_ge(mm_done, 2 * ph[("in", 1)]["piece"])
            for b in range(4):
                sp.dma_start(states[:, b], state[:, b]).then_inc(state_landed[b], 16)
            sp.wait_ge(unturned, 2 * (ph[("in", 1)]["turn"] + DC))
            sp.dma_start(v_scratch.ap(), vs_tok[:, :]).then_inc(v_stored, 16)
            sp.wait_ge(v_stored, 16)

            def load_v(b):
                sp.dma_start(v_row[:, b % 2, :], v_scratch.ap()[b:b + 1, :].broadcast_to([P, D]))\
                    .then_inc(v_landed[b % 2], 16)

            load_v(0)
            load_v(1)
            for b in range(NSAMP):
                gla_v.wait(sp, f"sn{b}_{GH - 1}")
                if b + 2 < NSAMP:
                    load_v(b + 2)
                sp.dma_start(out[:, b], states[:, b % 4]).then_inc(state_stored[b % 4], 16)
                if 2 <= b and b + 2 < NSAMP:
                    sp.wait_ge(state_stored[(b - 2) % 4], 16)
                    gla_t.wait(sp, f"so{b - 2}")
                    sp.dma_start(states[:, (b + 2) % 4], state[:, b + 2])\
                        .then_inc(state_landed[(b + 2) % 4], 16)
            for slot in range(4):
                sp.wait_ge(state_stored[slot], 32)

        M0, IN2 = ph[("mix", 2)], ph[("in", 2)]
        NPG = NSAMP * NPAGES
        MP = MH // 2
        SUMS_FROM, SUMS = 3, 4
        SUMS_LEFT = NPG - SUMS * (3 * DC // 4 - SUMS_FROM)
        extras = {0: ["bs"], 2: ["sl", "sln", "smx"], 3: ["sri", "spn", "own"], 4: ["np"]}
        moba_v = Steps(sem("moba_vector"),
                       ["rows", "rowneg", "spz", "nk", "z0", "z1"]
                       + [n for k in range(MP + 5) for n in (
                           ([f"ri{k - 1}", f"na{k - 1}", f"nb{k - 1}"] if 1 <= k <= MP else [])
                           + ([f"oc{k - 3}"] if 3 <= k < MP + 3 else [])
                           + ([f"la{k}", f"lb{k}", f"mxa{k}", f"mxb{k}"] if k < MP else [])
                           + extras.get(k, [])
                           + ([f"lo{k - 5}"] if k >= 5 else []))]
                       + ["ext", "os"])
        moba_s = Steps(sem("moba_scalar"),
                       [n for k in range(MP + 4) for n in (
                           ([f"{n}{k}_{e}" for n in ("ea", "eb") for e in range(2)] if k < MP else [])
                           + ([f"pt{k - 1}"] if 1 <= k <= MP else [])
                           + {2: ["sex"], 3: ["spt0", "spt1"]}.get(k, [])
                           + ([f"hi{k - 4}"] if k >= 4 else []))])
        moba_t = Steps(sem("moba_tensor"),
                       ["rows"] + [n for k in range(MP + 4) for n in (
                           ([f"s{k}"] if k < MP else []) + ([f"pv{k - 4}"] if k >= 4 else [])
                           + ([f"t{k - 1}"] if 1 <= k <= MP else [])
                           + ([f"o{k - 2}"] if 2 <= k < MP + 2 else [])
                           + {0: ["bs", "zn"], 2: ["sct"], 3: ["spt", "pnt"]}.get(k, []))]
                       + ["os"])
        keys_multiplied = sem("keys_multiplied")
        keys_summed = sem("keys_summed")
        SB, ACC, MISC, TB, OB = allps[:, 0:2, :], allps[:, 2:4, :], ps[4], allps[:, 5:7, :], ps[7]
        BLOCKS = ((0, SEQ), (SEQ, SEQ + P))

        def load_page(eng, n):
            page = n % NPG
            cache = A["cache_k"] if n < NPG else A["cache_v"]
            number = eng.value_load(table[0:1, page:page + 1], min_val=0, max_val=NPOOL - 1)
            eng.dma_start(pages[:, n % PAGE_SLOTS, :], cache[0][bass.ds(number, 1), :, :, :]
                          .rearrange("a p h d -> p (a h d)"))\
                .then_inc((keys_landed if n < NPG else values_landed)[n % PAGE_SLOTS], 16)

        def by_key(g, n):
            last = strip[:, 2 * g:2 * g + 2, n - 1:n]
            return bass.AP(tensor=last.tensor, offset=last.offset,
                           ap=[last.ap[0], last.ap[1], [-1, n]])

        def pool_moba(pool):
            pool.wait_ge(mm_done, 2 * IN2["piece"])
            pool.wait_ge(ss_done, IN2["norm"])
            for b in range(NSAMP):
                pool.dma_start(relb[:, b, :], A["rel_bias"]).then_inc(bias_landed, 16)
            pool.dma_start(of_strip[:, 0:STRIP], A["c_of_strip"]).then_inc(bias_landed, 16)
            pool.dma_start(of_past[:, :], A["c_of_past"]).then_inc(bias_landed, 16)
            pool.wait_ge(unturned, 2 * (IN2["turn"] + DC))
            pool.dma_start(q_scratch.ap(), vts[:, 0:D]).then_inc(scratch_landed, 16)
            pool.wait_ge(scratch_landed, 16)
            for b in range(2):
                pool.dma_start(q_row[:, b, :], q_scratch.ap()[b:b + 1, :].broadcast_to([P, D]))\
                    .then_inc(q_landed[b], 16)
            for n in range(NPG):
                b = n // NPAGES
                pool.wait_ge(q_landed[b % 2], 16 * (b // 2 + 1))
                pool.wait_ge(keys_landed[n % PAGE_SLOTS], 16 * (n // PAGE_SLOTS + 1))
                if n >= 2:
                    pool.wait_ge(keys_summed, n - 1)
                pool.tensor_tensor(prod[:, n % 2, :], pages[:, n % PAGE_SLOTS, :],
                                   q_row[:, b % 2, :], ALU.mult).then_inc(keys_multiplied, 1)
                if n == 0:
                    moba_v.wait(pool, "rowneg")
                    pool.dma_start(scratch.ap()[:, 0:STRIP], rows[:, 0:STRIP])\
                        .then_inc(scratch_landed, 16)
                if n == 3:
                    pool.wait_ge(scratch_landed, 32)
                    shifted = bass.AP(tensor=scratch.ap().tensor, offset=0,
                                      ap=[[1, P], [STRIP + 1, MH], [1, 2 * P]])
                    pool.dma_start(strip[:, :, :], shifted).then_inc(strip_landed, 16)
                if n % NPAGES == NPAGES - 1 and b + 2 < NSAMP:
                    pool.wait_ge(keys_multiplied, n + 1)
                    pool.dma_start(q_row[:, b % 2, :], q_scratch.ap()[b + 2:b + 3, :]
                                   .broadcast_to([P, D])).then_inc(q_landed[b % 2], 16)
            pool.wait_ge(unturned, 2 * (IN2["turn"] + 3 * DC))
            for name, at in (("k_new", D), ("v_new", 2 * D)):
                store(pool, A[name + "_prompt"][0, 0].rearrange("(b p) h d -> p b (h d)", p=P),
                      vt[:, :, at:at + D])
                store(pool, A[name + "_sample"][0].rearrange("b o h d -> (b o) (h d)"),
                      vts[:, at:at + D])

        def sp_keys(sp, piece):
            if piece == 3:
                sp.wait_ge(table_landed, 16)
                sp.wait_ge(mm_done, 2 * IN2["piece"])
                for n in range(PAGE_SLOTS):
                    load_page(sp, n)
            if piece >= 9:
                for n in (2 * piece - 14, 2 * piece - 13):
                    sp.wait_ge(keys_multiplied, n - PAGE_SLOTS + 1)
                    load_page(sp, n)

        def sp_pages(sp):
            sp.wait_ge(table_landed, 16)
            for n in range(NPG - 2, 2 * NPG):
                page = n - NPG
                if page < 0:
                    sp.wait_ge(keys_multiplied, n - PAGE_SLOTS + 1)
                elif page < PAGE_SLOTS:
                    sp.wait_ge(keys_multiplied, n - PAGE_SLOTS + 1)
                else:
                    moba_t.wait(sp, f"pv{(page - PAGE_SLOTS) // NPAGES}")
                load_page(sp, n)

        def pe_rows(pe):
            pe.wait_ge(bias_landed, 16 * (NSAMP + 2))
            moba_t.did(pe.matmul(ps[7][0:MH, 0:STRIP], relb[:, 0, :], of_strip[:, 0:STRIP],
                                 start=True, stop=True), "rows")

        def vector_rows(dve):
            moba_t.wait(dve, "rows")
            moba_v.did(dve.tensor_copy(rows[:, P - 1:STRIP], ps[7][0:MH, P - 1:STRIP]), "rows")
            moba_v.did(dve.memset(rows[:, 0:P - 1], NEG), "rowneg")

        def vector_sum_keys(dve, n, slot, column, page):
            dve.wait_ge(keys_multiplied, n + 1)
            dve.tensor_reduce(sc[:, page, column], prod[:, slot, :]
                              .rearrange("p (h d) -> p h d", h=MH), AX.X, ALU.add)\
                .then_inc(keys_summed, 1)

        def pe_moba(pe):
            did, wv, ws = moba_t.did, moba_v.wait, moba_s.wait
            pe.wait_ge(bank_read, M0["tile"])
            for k in range(MP + 4):
                if k < MP:
                    if k:
                        wv(pe, f"lb{k - 1}")
                    for e in range(2):
                        r = slice(DH * e, DH * e + DH)
                        pe.matmul(SB[:, e, 0:SEQ], feat[r, k, P:SEQ], feat[r, DC + k, 0:SEQ],
                                  start=True, stop=True, skip_group_check=True)
                        mm = pe.matmul(SB[:, e, SEQ:SEQ + P], feat[r, k, 0:P], feat[r, DC + k, 0:P],
                                       start=True, stop=True, skip_group_check=True)
                    did(mm, f"s{k}")
                if k >= 4:
                    b = k - 4
                    if b == 0:
                        wv(pe, "np")
                        ws(pe, "spt1")
                        for e in range(2):
                            pe.matmul(ACC[:, e, :], new_p[:, :],
                                      vts[:, 2 * D + e * 512:2 * D + (e + 1) * 512], start=True,
                                      stop=False, skip_group_check=True)
                    r = slice(32 * (b // 2), 32 * (b // 2) + 32)
                    for pg in range(NPAGES):
                        n = NPAGES * b + pg
                        pe.wait_ge(values_landed[n % PAGE_SLOTS], 16 * (n // PAGE_SLOTS + 1))
                        for e in range(2):
                            mm = pe.matmul(ACC[r, e, :], sp_tok[:, pg, b, :],
                                           pages[:, n % PAGE_SLOTS, e * 512:(e + 1) * 512],
                                           start=False, stop=(b % 2 == 1 and pg == NPAGES - 1),
                                           skip_group_check=True,
                                           tile_position=(0, 32 * (b // 2)))
                    did(mm, f"pv{b}")
                if 1 <= k <= MP:
                    g = k - 1
                    wv(pe, f"nb{g}")
                    if g:
                        ws(pe, f"pt{g - 1}")
                    for e in range(2):
                        for t in range(3):
                            mm = pe.transpose(TB[:, e, t * P:(t + 1) * P],
                                              logit[:, g % 2, e, t * P:(t + 1) * P], ident[:, :])
                    did(mm, f"t{g}")
                if 2 <= k < MP + 2:
                    g = k - 2
                    ws(pe, f"pt{g}")
                    if g == 0:
                        pe.wait_ge(unturned, 2 * (IN2["turn"] + 3 * DC))
                    if g:
                        wv(pe, f"oc{g - 1}")
                    for e in range(2):
                        h, r = 2 * g + e, slice(DH * e, DH * e + DH)
                        v = [vt[:, b, 2 * D + h * DH:2 * D + (h + 1) * DH] for b in range(NBLK)]
                        pr = prob_t[:, g % 2, e, :]
                        pe.matmul(OB[r, 0:P], v[0], pr[:, SEQ:SEQ + P], start=True,
                                  stop=True, skip_group_check=True)
                        pe.matmul(OB[r, P:SEQ], v[0], pr[:, 0:P], start=True, stop=False,
                                  skip_group_check=True)
                        mm = pe.matmul(OB[r, P:SEQ], v[1], pr[:, P:SEQ], start=False,
                                       stop=True, skip_group_check=True)
                    did(mm, f"o{g}")
                if k == 0:
                    did(pe.matmul(MISC[:, 0:SEQ + 1], relb[:, :, :].rearrange("p b h -> p (b h)"),
                                  of_past[:, :], start=True, stop=True, skip_group_check=True), "bs")
                    wv(pe, "z1")
                    did(pe.matmul(MISC[:, 384:385], new_z[:, :, :, :].rearrange("p b c e -> p (b c e)"),
                                  ones[:, 0:1], start=True, stop=True, skip_group_check=True), "zn")
                if k == 2:
                    wv(pe, "bs")
                    pe.wait_ge(keys_summed, NPG)
                    for pg in range(NPAGES):
                        mm = pe.transpose(MISC[:, pg * P:(pg + 1) * P], sc[:, pg, :], ident[:, :])
                    did(mm, "sct")
                if k == 3:
                    wv(pe, "spn")
                    for pg in range(NPAGES):
                        mm = pe.transpose(MISC[:, pg * P:(pg + 1) * P],
                                          slog[:, pg * P:(pg + 1) * P], ident[:, :])
                    did(mm, "spt")
                    wv(pe, "own")
                    did(pe.transpose(MISC[0:NSAMP, 384:512], new_own[:, :], ident[:, :]), "pnt")
            wv(pe, "ext")
            for c in range(DC):
                mm = pe.matmul(MISC[:, c * NSAMP:(c + 1) * NSAMP], ext[:, c * P:(c + 1) * P],
                               own[:, :], start=True, stop=True, skip_group_check=True)
            did(mm, "os")

        def vector_moba(dve):
            did, wt, ws = moba_v.did, moba_t.wait, moba_s.wait
            scale = DH ** -0.5
            dve.wait_ge(mm_done, 2 * ph[("out", 2)]["piece"])
            did(dve.memset(sp_tok[:, :, :, :], 0.0), "spz")
            did(dve.tensor_tensor(new_qk[:, :, :], feat[:, 0:DC, SEQ:TOK], feat[:, DC:2 * DC, SEQ:TOK],
                                  ALU.mult), "nk")
            moba_v.wait(dve, "nk")
            for e in range(2):
                did(dve.tensor_scalar(new_z[:, :, :, e], new_qk[:, :, :].rearrange("p c b -> p b c"),
                                      halves[:, e:e + 1], None, ALU.mult), f"z{e}")
            dve.wait_ge(strip_landed, 16)
            for k in range(MP + 5):
                if 1 <= k <= MP:
                    g, i = k - 1, (k - 1) % 2
                    ws(dve, f"eb{g}_1")
                    did(dve.reciprocal(softs[:, i, 2, :, :], softs[:, i, 1, :, :]), f"ri{g}")
                    moba_v.wait(dve, f"ri{g}")
                    for n, (lo, hi) in enumerate(BLOCKS):
                        inverse = softs[:, i, 2, n, :].unsqueeze(2).broadcast_to([P, 2, hi - lo])
                        did(dve.tensor_tensor(logit[:, i, :, lo:hi], logit[:, i, :, lo:hi], inverse,
                                              ALU.mult), f"n{'ab'[n]}{g}")
                if 3 <= k < MP + 3:
                    g = k - 3
                    wt(dve, f"o{g}")
                    did(dve.tensor_copy(feat[:, g, 0:SEQ], OB[:, 0:SEQ]), f"oc{g}")
                if k < MP:
                    wt(dve, f"s{k}")
                    if k >= 2:
                        wt(dve, f"t{k - 2}")
                    i = k % 2
                    for n, (lo, hi) in enumerate(BLOCKS):
                        did(dve.scalar_tensor_tensor(
                            out=logit[:, i, :, lo:hi], in0=SB[:, :, lo:hi], scalar=scale,
                            in1=by_key(k, hi - lo), op0=ALU.mult, op1=ALU.add), f"l{'ab'[n]}{k}")
                    for n, (lo, hi) in enumerate(BLOCKS):
                        moba_v.wait(dve, f"l{'ab'[n]}{k}")
                        did(dve.tensor_reduce(softs[:, i, 0, n, :], logit[:, i, :, lo:hi], AX.X,
                                              ALU.max, negate=True), f"mx{'ab'[n]}{k}")
                if k == 0:
                    wt(dve, "zn")
                    did(dve.tensor_copy(sbias[:, :], MISC[:, 0:SEQ + 1]), "bs")
                if k < 2:
                    left = -(-SUMS_LEFT // 2)
                    for n in range(NPG)[NPG - SUMS_LEFT:][k * left:(k + 1) * left]:
                        b = n // NPAGES
                        vector_sum_keys(dve, n, n % 2, slice(b * MH, (b + 1) * MH), n % NPAGES)
                if k == 2:
                    wt(dve, "sct")
                    did(dve.scalar_tensor_tensor(
                        out=slog[:, 0:SEQ], in0=MISC[:, 0:SEQ], scalar=scale, in1=sbias[:, 0:SEQ],
                        op0=ALU.mult, op1=ALU.add), "sl")
                    did(dve.scalar_tensor_tensor(
                        out=slog[:, SEQ:SEQ + 1], in0=MISC[:, 384:385], scalar=scale,
                        in1=sbias[:, SEQ:SEQ + 1], op0=ALU.mult, op1=ALU.add), "sln")
                    moba_v.wait(dve, "sln")
                    did(dve.tensor_reduce(small[:, 0:1], slog[:, :], AX.X, ALU.max, negate=True),
                        "smx")
                if k == 3:
                    ws(dve, "sex")
                    did(dve.reciprocal(small[:, 2:3], small[:, 1:2]), "sri")
                    moba_v.wait(dve, "sri")
                    did(dve.tensor_scalar(slog[:, :], slog[:, :], small[:, 2:3], None, ALU.mult),
                        "spn")
                    moba_v.wait(dve, "spn")
                    did(dve.tensor_scalar(new_own[:, :], own[:, :], slog[:, SEQ:SEQ + 1], None,
                                          ALU.mult), "own")
                if k == 4:
                    ws(dve, "spt1")
                    did(dve.tensor_copy(new_p[:, :], MISC[0:NSAMP, 384:512]), "np")
                if k >= 5:
                    c = k - 5
                    ws(dve, f"hi{c}")
                    did(dve.tensor_tensor(actl[:, c, 0:SEQ], feat[:, c, 0:SEQ],
                                          acth[:, c, 0:SEQ].bitcast(F32), ALU.subtract), f"lo{c}")
            wt(dve, f"pv{NSAMP - 1}")
            did(dve.tensor_tensor(ext[:, :].rearrange("p (h d) -> p h d", h=MH),
                                  ACC[:, :, :].rearrange("p e (h d) -> p (e h) d", d=DH),
                                  head_of[:, :].unsqueeze(2).broadcast_to([P, MH, DH]), ALU.mult),
                "ext")
            wt(dve, "os")
            did(dve.tensor_copy(feat[:, 0:DC, SEQ:TOK], MISC[:, 0:DC * NSAMP]
                                .rearrange("p (c b) -> p c b", c=DC)), "os")
            dve.wait_ge(ah_done, M0["act"] + DC)
            dve.tensor_tensor(actl[:, 0:DC, SEQ:TOK], feat[:, 0:DC, SEQ:TOK],
                              acth[:, 0:DC, SEQ:TOK].bitcast(F32), ALU.subtract).then_inc(al_done, DC)

        def scalar_moba(act):
            did, wt, wv = moba_s.did, moba_t.wait, moba_v.wait
            for k in range(MP + 4):
                if k < MP:
                    i = k % 2
                    for n, (lo, hi) in enumerate(BLOCKS):
                        wv(act, f"mx{'ab'[n]}{k}")
                        for e in range(2):
                            did(act.activation(logit[:, i, e, lo:hi], logit[:, i, e, lo:hi], ACT.Exp,
                                               bias=softs[:, i, 0, n, e:e + 1],
                                               accum_out=softs[:, i, 1, n, e:e + 1]),
                                f"e{'ab'[n]}{k}_{e}")
                if 1 <= k <= MP:
                    g = k - 1
                    wt(act, f"t{g}")
                    if g >= 2:
                        wt(act, f"o{g - 2}")
                    did(act.activation(prob_t[:, g % 2, :, :], TB[:, :, 0:3 * P], ACT.Copy), f"pt{g}")
                if k == 2:
                    wv(act, "smx")
                    did(act.activation(slog[:, :], slog[:, :], ACT.Exp, bias=small[:, 0:1],
                                       accum_out=small[:, 1:2]), "sex")
                if k == 3:
                    wt(act, "pnt")
                    for e in range(2):
                        did(act.activation(
                            sp_tok[:, :, e::2, MH * e:MH * e + MH],
                            MISC[:, 0:SEQ].rearrange("p (g b e h) -> p g b e h", g=NPAGES, e=2, h=MH)
                            [:, :, :, e, :], ACT.Copy), f"spt{e}")
                if k >= 4:
                    c = k - 4
                    wv(act, f"oc{c}")
                    did(act.activation(acth[:, c, 0:SEQ], feat[:, c, 0:SEQ], ACT.Copy), f"hi{c}")
            wv(act, "os")
            act.activation(acth[:, 0:DC, SEQ:TOK], feat[:, 0:DC, SEQ:TOK], ACT.Copy)\
                .then_inc(ah_done, DC)

        block = ctx.enter_context(nc.Block())

        @block.sync
        def _(sp):
            sp_input(sp)
            for layer in range(DEPTH):
                for kind in ("in", "out", "up", "down"):
                    stream(sp, (kind, layer))

        @block.gpsimd
        def _(pool):
            pool_setup(pool)
            for layer in range(DEPTH):
                if layer % 3 == 0:
                    pool_sgu(pool, layer)
                elif layer % 3 == 1:
                    pool_gla(pool)
                else:
                    pool_moba(pool)
                if layer == DEPTH - 1:
                    pool.wait_ge(al_done, ph[("mix", layer)]["act"] + HC)
                    pool.dma_start(gain_fin[:, :], A["norm_final"].rearrange("(o d) -> o d", o=1)
                                   .broadcast_to([P, D])).then_inc(fin_landed, 16)
                pool_squares(pool, ("out", layer))
                if layer < DEPTH - 1:
                    pool_squares(pool, ("down", layer))
            pool_final(pool)
            pool.wait_ge(stored, 16 * len(STORES))

        @block.scalar
        def _(act):
            scalar_setup(act)
            scalar_load(act)
            for layer in range(DEPTH):
                name = ("in", layer)
                if layer % 3 == 0:
                    scalar_in(act, name, 0, 6, ACT.Gelu, turns=True, first_of_phase=True)
                    scalar_lnstd(act, layer)
                    scalar_in(act, name, 6, 6 + NORM_STEPS, ACT.Gelu, into_feat=-HC, norm_v=True)
                    scalar_in(act, name, 6 + NORM_STEPS, 12, ACT.Gelu, into_feat=-HC)
                    scalar_sgu(act, layer)
                elif layer % 3 == 1:
                    scalar_rank(act)
                    scalar_in(act, name, 0, 2, None, first_of_phase=True)
                    scalar_gate(act)
                    scalar_in(act, name, 2, 4, ACT.Copy, turns=True, reads_feat=True)
                    scalar_decay(act)
                    scalar_in(act, name, 4, 6, None)
                    scalar_gla(act)
                else:
                    scalar_in(act, name, 0, 6, ACT.Copy, turns=True, reads_feat=True,
                              first_of_phase=True)
                    scalar_moba(act)
                scalar_out(act, ("out", layer))
                scalar_up(act, layer)
                scalar_out(act, ("down", layer))
            scalar_final(act)

        @block.tensor
        def _(pe):
            pe_load(pe)
            for layer in range(DEPTH):
                name = ("in", layer)
                new_norm = ph[name]["norm"] - 1
                if layer % 3 == 0:
                    pe_project(pe, name, 0, 6, turns_from=0, new_norm=new_norm)
                    pe_project(pe, name, 6, 12)
                    pe_sgu(pe, layer)
                elif layer % 3 == 1:
                    pe_project(pe, name, 0, 2, new_norm=new_norm)
                    pe_gate(pe)
                    pe_project(pe, name, 2, 4, turns_from=2)
                    pe_project(pe, name, 4, 6)
                    pe_gla(pe)
                else:
                    pe_project(pe, name, 0, SUMS_FROM, turns_from=0, new_norm=new_norm)
                    pe_rows(pe)
                    pe_project(pe, name, SUMS_FROM, 6, turns_from=0)
                    pe_moba(pe)
                pe_out(pe, ("out", layer))
                pe_project(pe, ("up", layer), 0, FC // 2, new_norm=ph[("up", layer)]["norm"] - 1)
                pe_out(pe, ("down", layer))
            pe_final(pe)

        @block.vector
        def _(dve):
            vector_load(dve)
            for layer in range(DEPTH):
                name = ("in", layer)
                if layer % 3 == 0:
                    vector_in(dve, name, 0, 6, stats_of=True, first_of_phase=True)
                    vector_moments(dve, layer)
                    vector_in(dve, name, 6, 6 + NORM_STEPS, norm_v=True)
                    vector_in(dve, name, 6 + NORM_STEPS, 12)
                    vector_sgu(dve, layer)
                elif layer % 3 == 1:
                    vector_rank(dve)
                    vector_in(dve, name, 0, 2, whole=True, first_of_phase=True)
                    vector_gate(dve)
                    vector_in(dve, name, 2, 6, whole=True)
                    vector_gla(dve)
                else:
                    vector_in(dve, name, 0, SUMS_FROM, whole=True, first_of_phase=True)
                    vector_rows(dve)
                    vector_in(dve, name, SUMS_FROM, 6, whole=True, sum_keys=True)
                    vector_moba(dve)
                vector_out(dve, ("out", layer))
                vector_up(dve, layer)
                vector_out(dve, ("down", layer))
            vector_final(dve)


def _constants():
    s, t = np.arange(P)[:, None], np.arange(P)[None, :]
    masks = [(s // (2 * m) == t // (2 * m)) & (s % (2 * m) < m) & (t % (2 * m) >= m)
             for m in LEVELS[1:]] + [s == t]

    def buckets(dist):
        exact = BUCKETS // 2
        far = np.maximum(dist, exact).astype(np.float32)
        large = exact + (np.log(far / exact) / np.float32(np.log(MAXDIST / exact))
                         * (BUCKETS - exact)).astype(np.int32)
        bucket = np.where(dist < exact, dist, np.minimum(large, BUCKETS - 1))
        return (np.arange(BUCKETS)[:, None] == bucket[None]) & (dist >= 0)[None]

    f = np.float32
    return {
        "c_ident": np.eye(P, dtype=f),
        "c_halves": (np.arange(P)[:, None] // DH == np.arange(2)[None]).astype(f),
        "c_own": (np.arange(P)[:, None] // MH == np.arange(NSAMP)[None]).astype(f),
        "c_head_of": (np.arange(P)[:, None] % MH == np.arange(MH)[None]).astype(f),
        "c_masks": np.stack(masks, 1).astype(np.int32),
        "c_of_strip": buckets(np.arange(STRIP) - (P - 1)).astype(f),
        "c_of_past": buckets(SEQ - np.arange(SEQ + 1)).astype(f),
    }


_INS = ["x_prompt", "x_sample", "cache_k", "cache_v", "page_table", "state_gla",
        "norm_mix", "norm_ffn", "norm_final", "w_in_a", "ln_a_g", "ln_a_b", "w_s_a", "b_s_a",
        "w_out_a", "w_in_b", "w_gate_b", "b_gate_b", "gn_b", "w_out_b", "w_in_c", "w_out_c",
        "rel_bias", "w_up", "w_down"]
_OUTS = [("y_prompt", (1, SEQ, D)), ("y_sample", (NSAMP, 1, D)),
         ("k_new_prompt", (1, 1, SEQ, MH, DH)), ("v_new_prompt", (1, 1, SEQ, MH, DH)),
         ("k_new_sample", (1, NSAMP, 1, MH, DH)), ("v_new_sample", (1, NSAMP, 1, MH, DH)),
         ("gla_state_prompt", (1, 1, GH, DK, DV)), ("gla_state_sample", (1, NSAMP, GH, DK, DV)),
         ("sgu_v_sample", (2, NSAMP, 1, HALF))]


def kernel(**inputs):
    import concourse.bacc as bacc
    from concourse.bass_utils import run_bass_kernel_spmd

    nc = bacc.Bacc("TRN2", target_bir_lowering=False, num_devices=1)
    arrays, A = {}, {}
    for name, a in [(n, inputs[n]) for n in _INS] + list(_constants().items()):
        a = np.ascontiguousarray(a)
        arrays[f"in_{name}"] = a
        A[name] = nc.dram_tensor(f"in_{name}", a.shape, mybir.dt.from_np(a.dtype),
                                 kind="ExternalInput").ap()
    for name, shape in _OUTS:
        A[name] = nc.dram_tensor(f"out_{name}", shape, F32, kind="ExternalOutput").ap()
    build(nc, A)
    got = run_bass_kernel_spmd(nc, [arrays], core_ids=[0]).results[0]
    return tuple(got[f"out_{name}"] for name, _ in _OUTS)
```
